# Optimizing a Trainium2 kernel written in Bass

```python
import math
import jax, jax.numpy as jnp
from jax import lax
import numpy as np

D_MODEL = 1024
BATCH = 1
SEQ = 1024
DEPTH = 1
DEC_BATCH = 8
DEC_SEQ = 4
PAST_LEN = 1024
PAGE_SIZE = 128

A_HEAD_DIM = 64
A_WIDTH = D_MODEL // 2
A_HEADS = A_WIDTH // A_HEAD_DIM
A_GROUPS = 2
A_HPG = A_HEADS // A_GROUPS
A_STATE = 64
A_CONV = 4
A_CONV_DIM = A_WIDTH + 2 * A_GROUPS * A_STATE
A_CHUNK = 128
B_CH = 16
B_WIDTH = D_MODEL // 2
B_GROUPS = B_WIDTH // B_CH
B_STATE = 64
C_HEAD_DIM = 64
C_WIDTH = D_MODEL // 2
C_HEADS = C_WIDTH // C_HEAD_DIM
C_KV_HEADS = 2
C_GQA = C_HEADS // C_KV_HEADS
C_KV_WIDTH = C_KV_HEADS * C_HEAD_DIM
WINDOW = 128
REL_BUCKETS = 32
REL_MAX_DIST = 128
D_FF = -(-8 * D_MODEL // (3 * 256)) * 256
N_BRANCH = 3
EPS = 1e-6
OFF_Z = 0
OFF_XBC = OFF_Z + A_WIDTH
OFF_DT = OFF_XBC + A_CONV_DIM
OFF_U = OFF_DT + A_HEADS
OFF_Q = OFF_U + B_WIDTH
OFF_K = OFF_Q + C_WIDTH
OFF_V = OFF_K + C_KV_WIDTH
OFF_GATE = OFF_V + C_KV_WIDTH
IN_COLS = OFF_GATE + N_BRANCH * D_MODEL

kernel_name = 'hybrid_ssd_s5_swa_step'

def rmsnorm(x, w):
    xf = x.astype(jnp.float32)
    y = xf * lax.rsqrt(jnp.mean(xf * xf, axis=-1, keepdims=True) + EPS)
    return (y * w.astype(jnp.float32)).astype(x.dtype)

def causal_conv(xbc, buf, w, b):
    full = jnp.concatenate([buf.astype(xbc.dtype), xbc], axis=1)
    out = lax.conv_general_dilated(full, w[:, None, :].astype(xbc.dtype), window_strides=(1,), padding='VALID', dimension_numbers=('NWC', 'WIO', 'NWC'), feature_group_count=xbc.shape[-1])
    return out + b.astype(xbc.dtype), full[:, full.shape[1] - (A_CONV - 1):]

def ssd_scan(x, dt, a, bm, cm, h0):
    bsz, l, g, k, p = x.shape
    n = bm.shape[-1]
    q = A_CHUNK if l % A_CHUNK == 0 else l
    c = l // q
    xs = (x * dt[..., None]).reshape(bsz, c, q, g, k, p)
    a_cum = jnp.cumsum((dt * a).reshape(bsz, c, q, g, k), axis=2)
    bc = bm.reshape(bsz, c, q, g, n)
    cc = cm.reshape(bsz, c, q, g, n)
    seg = a_cum[:, :, :, None] - a_cum[:, :, None, :]
    tri = jnp.tril(jnp.ones((q, q), dtype=bool))[:, :, None, None]
    decay_in = jnp.exp(jnp.where(tri, seg, -jnp.inf))
    cb = jnp.einsum('bcqgn,bcsgn->bcqsg', cc, bc)
    y_diag = jnp.einsum('bcqsgk,bcsgkp->bcqgkp', cb[..., None] * decay_in, xs)
    decay_end = jnp.exp(a_cum[:, :, -1:] - a_cum)
    chunk_states = jnp.einsum('bcsgn,bcsgkp->bcgkpn', bc, xs * decay_end[..., None])
    chunk_decay = jnp.exp(a_cum[:, :, -1])

    def step(h, inp):
        dec, st = inp
        return dec[..., None, None] * h + st, h

    h_last, h_prev = lax.scan(step, h0, (jnp.moveaxis(chunk_decay, 1, 0), jnp.moveaxis(chunk_states, 1, 0)))
    h_prev = jnp.moveaxis(h_prev, 0, 1)
    y_off = jnp.einsum('bcqgn,bcgkpn->bcqgkp', cc, h_prev) * jnp.exp(a_cum)[..., None]
    return (y_diag + y_off).reshape(bsz, l, g, k, p), h_last

def ssd_mixer(z, xbc, dt_raw, conv_buf, h0, conv_w, conv_b, a_log, dt_bias, d, norm_w):
    bsz, l = z.shape[:2]
    xbc_c, new_buf = causal_conv(xbc, conv_buf, conv_w, conv_b)
    xbc_c = jax.nn.silu(xbc_c.astype(jnp.float32))
    x = xbc_c[..., :A_WIDTH].reshape(bsz, l, A_GROUPS, A_HPG, A_HEAD_DIM)
    bm = xbc_c[..., A_WIDTH:A_WIDTH + A_GROUPS * A_STATE].reshape(bsz, l, A_GROUPS, A_STATE)
    cm = xbc_c[..., A_WIDTH + A_GROUPS * A_STATE:].reshape(bsz, l, A_GROUPS, A_STATE)
    dt = jax.nn.softplus(dt_raw.astype(jnp.float32) + dt_bias.astype(jnp.float32)).reshape(bsz, l, A_GROUPS, A_HPG)
    a = -jnp.exp(a_log.astype(jnp.float32)).reshape(A_GROUPS, A_HPG)
    h0 = h0.astype(jnp.float32).reshape(bsz, A_GROUPS, A_HPG, A_HEAD_DIM, A_STATE)
    y, h = ssd_scan(x, dt, a, bm, cm, h0)
    y = y + d.astype(jnp.float32).reshape(A_GROUPS, A_HPG)[..., None] * x
    y = y.reshape(bsz, l, A_WIDTH) * jax.nn.silu(z.astype(jnp.float32))
    return rmsnorm(y, norm_w), new_buf, h.reshape(bsz, A_HEADS, A_HEAD_DIM, A_STATE)

def lin_combine(e1, e2):
    a1, b1 = e1
    a2, b2 = e2
    return a1 * a2, a2 * b1 + b2

def s5_mixer(u, h_re, h_im, lam_re, lam_im, log_dt, b_re, b_im, c_re, c_im, d, w_glu):
    bsz, l = u.shape[:2]
    uf = u.astype(jnp.float32).reshape(bsz, l, B_GROUPS, B_CH)
    lam = lax.complex(lam_re.astype(jnp.float32), lam_im.astype(jnp.float32))
    step = jnp.exp(log_dt.astype(jnp.float32))[:, None]
    a_bar = jnp.exp(lam * step)
    b_bar = ((a_bar - 1.0) / lam)[:, :, None] * lax.complex(b_re.astype(jnp.float32), b_im.astype(jnp.float32))
    c_mat = lax.complex(c_re.astype(jnp.float32), c_im.astype(jnp.float32))
    h0 = lax.complex(h_re.astype(jnp.float32), h_im.astype(jnp.float32))
    bu = jnp.einsum('gph,blgh->blgp', b_bar, uf.astype(jnp.complex64))
    a_seq = jnp.broadcast_to(a_bar, bu.shape)
    a_cum, h = lax.associative_scan(lin_combine, (a_seq, bu), axis=1)
    h = h + a_cum * h0[:, None]
    y = jnp.real(jnp.einsum('ghp,blgp->blgh', c_mat, h)) + d.astype(jnp.float32) * uf
    g = jax.nn.gelu(y.reshape(bsz, l, B_WIDTH))
    gv = g @ w_glu.astype(jnp.float32)
    return gv[..., :B_WIDTH] * jax.nn.sigmoid(gv[..., B_WIDTH:]), h[:, -1]

def rel_bucket(n):
    n = jnp.maximum(n, 0)
    exact = REL_BUCKETS // 2
    nf = jnp.maximum(n, 1).astype(jnp.float32)
    large = exact + (jnp.log(nf / exact) / math.log(REL_MAX_DIST / exact) * (REL_BUCKETS - exact)).astype(jnp.int32)
    large = jnp.minimum(large, REL_BUCKETS - 1)
    return jnp.where(n < exact, n, large)

def rel_bias_for(n, table):
    bias = table[rel_bucket(n)].astype(jnp.float32)
    return jnp.moveaxis(bias, -1, 0).reshape(C_KV_HEADS, C_GQA, *n.shape)

def sink_softmax(s, sink):
    sk = sink[:, :, None, None]
    m = jnp.maximum(jnp.max(s, axis=-1, keepdims=True), sk)
    p = jnp.exp(s - m)
    return p / (jnp.sum(p, axis=-1, keepdims=True) + jnp.exp(sk - m))

def attn_prompt(q, k, v, table, sinks):
    bsz, l = q.shape[:2]
    nb = l // WINDOW
    qb = q.astype(jnp.float32).reshape(bsz, nb, WINDOW, C_KV_HEADS, C_GQA, C_HEAD_DIM)

    def band(t):
        tb = t.astype(jnp.float32).reshape(bsz, nb, WINDOW, C_KV_HEADS, C_HEAD_DIM)
        prev = jnp.pad(tb[:, :-1], ((0, 0), (1, 0), (0, 0), (0, 0), (0, 0)))
        return jnp.concatenate([prev, tb], axis=2)

    kb, vb = band(k), band(v)
    qi = jnp.arange(WINDOW)[:, None]
    kj = jnp.arange(2 * WINDOW)[None, :]
    dist = qi + WINDOW - kj
    valid = (dist >= 0) & (dist < WINDOW)
    first = (jnp.arange(nb)[:, None, None] == 0) & (kj[None] < WINDOW)
    mask = valid[None] & jnp.logical_not(first)
    s = jnp.einsum('bnqhgd,bnkhd->bnhgqk', qb, kb) * (C_HEAD_DIM ** -0.5) + rel_bias_for(dist, table)
    s = jnp.where(mask[None, :, None, None], s, -jnp.inf)
    p = sink_softmax(s, sinks.astype(jnp.float32).reshape(C_KV_HEADS, C_GQA))
    o = jnp.einsum('bnhgqk,bnkhd->bnqhgd', p, vb)
    return o.reshape(bsz, l, C_WIDTH)

def attn_sample(q, k, v, k_buf, v_buf, table, sinks):
    bsz, t = q.shape[:2]
    lb = k_buf.shape[1]
    kk = jnp.concatenate([k_buf.astype(jnp.float32), k.astype(jnp.float32)], axis=1)
    vv = jnp.concatenate([v_buf.astype(jnp.float32), v.astype(jnp.float32)], axis=1)
    dist = (lb + jnp.arange(t))[:, None] - jnp.arange(lb + t)[None, :]
    mask = (dist >= 0) & (dist < WINDOW)
    s = jnp.einsum('bqhgd,bkhd->bhgqk', q.astype(jnp.float32), kk) * (C_HEAD_DIM ** -0.5) + rel_bias_for(dist, table)
    s = jnp.where(mask, s, -jnp.inf)
    p = sink_softmax(s, sinks.astype(jnp.float32).reshape(C_KV_HEADS, C_GQA))
    o = jnp.einsum('bhgqk,bkhd->bqhgd', p, vv)
    return o.reshape(bsz, t, C_WIDTH), kk[:, kk.shape[1] - lb:], vv[:, vv.shape[1] - lb:]

def block(x, ssd_h, conv_buf, s5_re, s5_im, k_buf, v_buf,
          norm1_w, w_in, conv_w, conv_b, ssd_a_log, ssd_dt_bias, ssd_d, ssd_norm_w,
          s5_lam_re, s5_lam_im, s5_log_dt, s5_b_re, s5_b_im, s5_c_re, s5_c_im, s5_d, s5_w_glu,
          attn_sinks, w_br_a, w_br_b, w_br_c, w_out, norm2_w, w_ffn_up, w_ffn_down, rel_bias):
    bsz, l, _ = x.shape
    h = rmsnorm(x, norm1_w)
    proj = h @ w_in
    y_a, conv_new, ssd_new = ssd_mixer(proj[..., OFF_Z:OFF_XBC], proj[..., OFF_XBC:OFF_DT], proj[..., OFF_DT:OFF_U], conv_buf, ssd_h, conv_w, conv_b, ssd_a_log, ssd_dt_bias, ssd_d, ssd_norm_w)
    y_b, s5_new = s5_mixer(proj[..., OFF_U:OFF_Q], s5_re, s5_im, s5_lam_re, s5_lam_im, s5_log_dt, s5_b_re, s5_b_im, s5_c_re, s5_c_im, s5_d, s5_w_glu)
    q = proj[..., OFF_Q:OFF_K].reshape(bsz, l, C_KV_HEADS, C_GQA, C_HEAD_DIM)
    k = proj[..., OFF_K:OFF_V].reshape(bsz, l, C_KV_HEADS, C_HEAD_DIM)
    v = proj[..., OFF_V:OFF_GATE].reshape(bsz, l, C_KV_HEADS, C_HEAD_DIM)
    if k_buf is None:
        y_c = attn_prompt(q, k, v, rel_bias, attn_sinks)
        keep = min(WINDOW, l)
        k_new, v_new = k[:, l - keep:], v[:, l - keep:]
    else:
        y_c, k_new, v_new = attn_sample(q, k, v, k_buf, v_buf, rel_bias, attn_sinks)
    gates = jax.nn.sigmoid(proj[..., OFF_GATE:].astype(jnp.float32)).reshape(bsz, l, N_BRANCH, D_MODEL)
    mixed = gates[:, :, 0] * (y_a @ w_br_a) + gates[:, :, 1] * (y_b @ w_br_b) + gates[:, :, 2] * (y_c @ w_br_c)
    x = x + (mixed @ w_out).astype(x.dtype)
    h2 = rmsnorm(x, norm2_w)
    gu = h2 @ w_ffn_up
    x = x + ((jax.nn.silu(gu[..., :D_FF]) * gu[..., D_FF:]) @ w_ffn_down).astype(x.dtype)
    sd = x.dtype
    return x, (ssd_new.astype(sd), conv_new.astype(sd), jnp.real(s5_new).astype(sd), jnp.imag(s5_new).astype(sd), k_new.astype(sd), v_new.astype(sd))

def setup_inputs(seed: int = 0) -> dict:
    key = jax.random.key(seed)
    keys = iter(jax.random.split(key, 48))
    f32 = jnp.float32

    def nrm(shape, scale):
        return scale * jax.random.normal(next(keys), shape, f32)

    def unif(shape, lo, hi):
        return jax.random.uniform(next(keys), shape, f32, lo, hi)

    win_buf = min(WINDOW, PAST_LEN)
    x_prompt = nrm((BATCH, SEQ, D_MODEL), 1.0)
    x_sample = nrm((DEC_BATCH, DEC_SEQ, D_MODEL), 1.0)
    state_ssd = nrm((DEPTH, DEC_BATCH, A_HEADS, A_HEAD_DIM, A_STATE), 0.5)
    state_conv = nrm((DEPTH, DEC_BATCH, A_CONV - 1, A_CONV_DIM), 1.0)
    state_s5_re = nrm((DEPTH, DEC_BATCH, B_GROUPS, B_STATE), 0.3)
    state_s5_im = nrm((DEPTH, DEC_BATCH, B_GROUPS, B_STATE), 0.3)
    cache_k = nrm((DEPTH, DEC_BATCH, win_buf, C_KV_HEADS, C_HEAD_DIM), 1.0)
    cache_v = nrm((DEPTH, DEC_BATCH, win_buf, C_KV_HEADS, C_HEAD_DIM), 1.0)
    norm1_w = 1.0 + nrm((DEPTH, D_MODEL), 0.02)
    w_in = nrm((DEPTH, D_MODEL, IN_COLS), D_MODEL ** -0.5)
    conv_w = nrm((DEPTH, A_CONV, A_CONV_DIM), A_CONV ** -0.5)
    conv_b = nrm((DEPTH, A_CONV_DIM), 0.02)
    ssd_a_log = jnp.log(unif((DEPTH, A_HEADS), 1.0, 16.0))
    dt_init = jnp.exp(unif((DEPTH, A_HEADS), math.log(1e-3), math.log(1e-1)))
    ssd_dt_bias = dt_init + jnp.log(-jnp.expm1(-dt_init))
    ssd_d = 1.0 + nrm((DEPTH, A_HEADS), 0.02)
    ssd_norm_w = 1.0 + nrm((DEPTH, A_WIDTH), 0.02)
    s5_lam_re = -0.5 + nrm((DEPTH, B_GROUPS, B_STATE), 0.01)
    s5_lam_im = jnp.pi * jnp.arange(B_STATE, dtype=f32) + nrm((DEPTH, B_GROUPS, B_STATE), 0.01)
    s5_log_dt = unif((DEPTH, B_GROUPS), math.log(1e-3), math.log(1e-1))
    s5_b_re = nrm((DEPTH, B_GROUPS, B_STATE, B_CH), (2 * B_CH) ** -0.5)
    s5_b_im = nrm((DEPTH, B_GROUPS, B_STATE, B_CH), (2 * B_CH) ** -0.5)
    s5_c_re = nrm((DEPTH, B_GROUPS, B_CH, B_STATE), B_STATE ** -0.5)
    s5_c_im = nrm((DEPTH, B_GROUPS, B_CH, B_STATE), B_STATE ** -0.5)
    s5_d = nrm((DEPTH, B_GROUPS, B_CH), 1.0)
    s5_w_glu = nrm((DEPTH, B_WIDTH, 2 * B_WIDTH), B_WIDTH ** -0.5)
    attn_sinks = nrm((DEPTH, C_HEADS), 0.5)
    w_br_a = nrm((DEPTH, A_WIDTH, D_MODEL), A_WIDTH ** -0.5)
    w_br_b = nrm((DEPTH, B_WIDTH, D_MODEL), B_WIDTH ** -0.5)
    w_br_c = nrm((DEPTH, C_WIDTH, D_MODEL), C_WIDTH ** -0.5)
    w_out = nrm((DEPTH, D_MODEL, D_MODEL), D_MODEL ** -0.5)
    norm2_w = 1.0 + nrm((DEPTH, D_MODEL), 0.02)
    w_ffn_up = nrm((DEPTH, D_MODEL, 2 * D_FF), D_MODEL ** -0.5)
    w_ffn_down = nrm((DEPTH, D_FF, D_MODEL), D_FF ** -0.5)
    rel_bias = nrm((REL_BUCKETS, C_HEADS), 0.5)
    final_norm_w = 1.0 + nrm((D_MODEL,), 0.02)
    return {'x_prompt': x_prompt, 'x_sample': x_sample, 'state_ssd': state_ssd, 'state_conv': state_conv,
            'state_s5_re': state_s5_re, 'state_s5_im': state_s5_im, 'cache_k': cache_k, 'cache_v': cache_v,
            'norm1_w': norm1_w, 'w_in': w_in, 'conv_w': conv_w, 'conv_b': conv_b, 'ssd_a_log': ssd_a_log,
            'ssd_dt_bias': ssd_dt_bias, 'ssd_d': ssd_d, 'ssd_norm_w': ssd_norm_w, 's5_lam_re': s5_lam_re,
            's5_lam_im': s5_lam_im, 's5_log_dt': s5_log_dt, 's5_b_re': s5_b_re, 's5_b_im': s5_b_im,
            's5_c_re': s5_c_re, 's5_c_im': s5_c_im, 's5_d': s5_d, 's5_w_glu': s5_w_glu, 'attn_sinks': attn_sinks,
            'w_br_a': w_br_a, 'w_br_b': w_br_b, 'w_br_c': w_br_c, 'w_out': w_out, 'norm2_w': norm2_w,
            'w_ffn_up': w_ffn_up, 'w_ffn_down': w_ffn_down, 'rel_bias': rel_bias, 'final_norm_w': final_norm_w}

def reference(x_prompt, x_sample, state_ssd, state_conv, state_s5_re, state_s5_im, cache_k, cache_v,
              norm1_w, w_in, conv_w, conv_b, ssd_a_log, ssd_dt_bias, ssd_d, ssd_norm_w,
              s5_lam_re, s5_lam_im, s5_log_dt, s5_b_re, s5_b_im, s5_c_re, s5_c_im, s5_d, s5_w_glu,
              attn_sinks, w_br_a, w_br_b, w_br_c, w_out, norm2_w, w_ffn_up, w_ffn_down, rel_bias, final_norm_w):
    bp = x_prompt.shape[0]
    sd = x_prompt.dtype
    zero_ssd = jnp.zeros((bp, A_HEADS, A_HEAD_DIM, A_STATE), sd)
    zero_conv = jnp.zeros((bp, A_CONV - 1, A_CONV_DIM), sd)
    zero_s5 = jnp.zeros((bp, B_GROUPS, B_STATE), sd)
    xp, xs = x_prompt, x_sample
    new_p, new_s = [], []
    for i in range(DEPTH):
        lw = (norm1_w[i], w_in[i], conv_w[i], conv_b[i], ssd_a_log[i], ssd_dt_bias[i], ssd_d[i], ssd_norm_w[i],
              s5_lam_re[i], s5_lam_im[i], s5_log_dt[i], s5_b_re[i], s5_b_im[i], s5_c_re[i], s5_c_im[i], s5_d[i], s5_w_glu[i],
              attn_sinks[i], w_br_a[i], w_br_b[i], w_br_c[i], w_out[i], norm2_w[i], w_ffn_up[i], w_ffn_down[i])
        xp, st_p = block(xp, zero_ssd, zero_conv, zero_s5, zero_s5, None, None, *lw, rel_bias)
        xs, st_s = block(xs, state_ssd[i], state_conv[i], state_s5_re[i], state_s5_im[i], cache_k[i], cache_v[i], *lw, rel_bias)
        new_p.append(st_p)
        new_s.append(st_s)

    def stack(states, j):
        return jnp.stack([s[j] for s in states], axis=0)

    y_prompt = rmsnorm(xp, final_norm_w)
    y_sample = rmsnorm(xs, final_norm_w)
    return (y_prompt, y_sample,
            stack(new_p, 0), stack(new_p, 1), stack(new_p, 2), stack(new_p, 3), stack(new_p, 4), stack(new_p, 5),
            stack(new_s, 0), stack(new_s, 1), stack(new_s, 2), stack(new_s, 3), stack(new_s, 4), stack(new_s, 5))


_drawn_inputs = setup_inputs


def setup_inputs(seed=0):
    import zlib

    import numpy as np

    out = dict(_drawn_inputs(seed))
    spreads = {}
    factors = {'ssd_d': 5.286,
     'ssd_norm_w': 5.645,
     's5_lam_re': 64.956,
     'attn_sinks': 30.148,
     'norm2_w': 4.179,
     'final_norm_w': 22.956,
     'rel_bias': 3.379,
     's5_c_re': 3.192,
     's5_c_im': 3.189}
    for name, (base, spread) in spreads.items():
        noise = np.random.default_rng([zlib.crc32(name.encode()), seed]).standard_normal(out[name].shape)
        drawn = base * np.exp(spread * noise) if base else spread * noise
        out[name] = __import__('jax').numpy.asarray(drawn.astype(out[name].dtype))
    for name, factor in factors.items():
        out[name] = (out[name] * factor).astype(out[name].dtype)
    return out
```

```python
from contextlib import ExitStack
import math

import numpy as np

import concourse.bass as bass
from concourse import mybir

F32 = mybir.dt.float32
F32R = mybir.dt.float32r
BF16 = mybir.dt.bfloat16
ACT = mybir.ActivationFunctionType
ALU = mybir.AluOpType
AX = mybir.AxisListType

P = 128
D = 1024
SEQ = 1024
NSEQ, DSEQ = 8, 4
SMP = NSEQ * DSEQ
T = SEQ + SMP
KD = D // P
NBLK = SEQ // P
SUB = 8
CH = SEQ // SUB
CB = P // SUB
HD = 64
DFF = 2816
KF = DFF // P
EPS = 1e-6
CHUNKS = [(0, 384), (384, 384), (768, T - 768)]
NEG = -1e30
NBUCKET = 32

FFN_PASSES = [6, 6, 5, 5]
STAGES = [("u", 4, 1), ("gates1", 12, 1), ("glu", 4, 2), ("proj", 17, 1), ("gates2", 12, 1),
          ("branch", 12, 2), ("out", 8, 1)]
for _i, _n in enumerate(FFN_PASSES):
    STAGES += [(f"up{_i}", 2 * _n, 1), (f"down{_i}", 8, 1)]
UNIT0, TILE0, TILE_END = {}, {}, []
_u = _m = 0
for _name, _n, _per in STAGES:
    UNIT0[_name], TILE0[_name] = _u, _m
    for _ in range(_n):
        _m += _per
        _u += 1
        TILE_END.append(_m)
UNITS = _u

BW_P = CB * (2 * SUB - 1) * 2 * CB
BW_S = DSEQ * (P + DSEQ)
BW = BW_P + BW_S
BHALF = BW // 2
BSTEP = BHALF // 9


def buckets(dist):
    n = np.maximum(dist, 0)
    exact = NBUCKET // 2
    nf = np.maximum(n, 1).astype(np.float32)
    large = exact + (np.log(nf / np.float32(exact)) / np.float32(math.log(128 / exact))
                     * np.float32(NBUCKET - exact)).astype(np.int32)
    return np.where(n < exact, n, np.minimum(large, NBUCKET - 1))


PCOL = {}


def _fields():
    at = 0
    for name, n in [("ident", 128), ("tri", 128), ("negtri", 128), ("ones", 128), ("mask", 128),
                    ("tri_s", 32), ("negtri_s", 32), ("mask_s", 32), ("seqmask", 8), ("eps", 1),
                    ("norm1", 8), ("norm2", 8), ("normf", 8), ("conv_w", 24), ("conv_b", 6),
                    ("ssd_norm", 4), ("ssd_d", 4), ("a_log", 8), ("dt_bias", 8), ("sinks", 8),
                    ("sinks_s", 4), ("s5_d", 32), ("lam_re", 16), ("lam_im", 16), ("log_dt", 16)]:
        PCOL[name] = (at, n)
        at += n
    return at


NPAR = _fields()


def shape_constants():
    j = np.arange(P)
    real = SUB * (j % CB) + j // CB
    js = np.arange(SMP)
    ts, bs = js // NSEQ, js % NSEQ
    c = {}
    c["ident"] = np.eye(P)
    c["tri"] = (real[:, None] <= real[None, :]).astype(np.float64)
    c["negtri"] = -c["tri"]
    c["ones"] = np.ones((P, P))
    c["mask"] = np.where(c["tri"] > 0, 0.0, NEG)
    tri_s = ((bs[:, None] == bs[None, :]) & (ts[:, None] <= ts[None, :])).astype(np.float64)
    c["tri_s"], c["negtri_s"], c["mask_s"] = tri_s, -tri_s, np.where(tri_s > 0, 0.0, NEG)
    c["seqmask"] = (bs[:, None] == np.arange(NSEQ)[None, :]).astype(np.float64)
    c["eps"] = np.full((P, 1), EPS)
    cq = np.arange(CB)[:, None, None]
    dl = np.arange(2 * SUB - 1)[None, :, None]
    half, ck = np.arange(2)[None, :, None, None], np.arange(CB)[None, None, None, :]
    cq, dl = cq[..., None], dl[:, None, :, :].transpose(0, 1, 2, 3)
    dist_p = (SUB * (cq - ck) + P * (1 - half) + (SUB - 1) - dl).reshape(-1)
    t = np.arange(DSEQ)[:, None]
    k = np.arange(P + DSEQ)[None, :]
    dist_s = (P + t - k).reshape(-1)
    dist = np.concatenate([dist_p, dist_s])
    ok = (dist >= 0) & (dist < P)
    hot = np.zeros((NBUCKET + 1, BW), np.float32)
    hot[buckets(dist), np.arange(BW)] = ok
    hot[NBUCKET] = np.where(ok, 0.0, NEG)
    return c, hot


def build(nc, io):
    NG = 32
    NP = NG // 2
    UC = CH + 1 + 2 * NSEQ
    YC = CH + 1 + NSEQ

    top = ExitStack()
    ps_all = top.enter_context(nc.psum_tensor("ps", [P, 8, 512], F32))
    acc = [ps_all[:, n, :] for n in range(3)]
    bank = [ps_all[:, n, :] for n in range(8)]

    def sb(stack, name, shape, dt=F32):
        return stack.enter_context(nc.sbuf_tensor(name, shape, dt))

    def sem(name):
        return top.enter_context(nc.semaphore(name))

    HH = sb(top, "HH", [P, KD, T], F32R)
    HL = sb(top, "HL", [P, KD, T], F32R)
    WRAW = sb(top, "WRAW", [P, 2, 1024])
    WH = sb(top, "WH", [P, 2, 1024], F32R)
    WL = sb(top, "WL", [P, 2, 1024], F32R)
    GT = sb(top, "GT", [P, T])
    PRM = sb(top, "PRM", [P, NPAR])
    IDB = sb(top, "IDB", [P, P], BF16)
    MASKB = sb(top, "MASKB", [P, P], BF16)
    MASKSB = sb(top, "MASKSB", [SMP, SMP], BF16)
    ZERO = sb(top, "ZERO", [P, 1])

    def prm(name, a=0, n=None):
        at, width = PCOL[name]
        return PRM[:, at + a:at + (width if n is None else a + n)]

    IDENT = prm("ident")

    p0 = ExitStack()
    X0 = sb(p0, "X0", [P, KD, T])
    SQ = sb(p0, "SQ", [P, 2, T])
    ACC = sb(p0, "ACC", [P, T])
    RS = sb(p0, "RS", [P, T])
    HF = sb(p0, "HF", [P, 2, 384])
    HOT = sb(p0, "HOT", [P, BHALF])
    BTAB = sb(p0, "BTAB", [P, BHALF])
    RTAB = sb(p0, "RTAB", [P, 8])
    p0.close()
    p1 = ExitStack()
    UF = sb(p1, "UF", [P, 4, T])
    p1.close()
    p1 = ExitStack()
    W_re = sb(p1, "W_re", [P, NP, P])
    W_im = sb(p1, "W_im", [P, NP, P])
    sb(p1, "padUF", [P, 4 * T - 2 * NP * P])
    OFF_re = sb(p1, "OFF_re", [P, NP, P])
    OFF_im = sb(p1, "OFF_im", [P, NP, P])
    STT = sb(p1, "STT", [P, 2, NP, P])
    KT = sb(p1, "KT", [P, NG, SUB, 16])
    U = sb(p1, "U", [P, NG, UC])
    ROT = sb(p1, "ROT", [P, 2, 4, CH])
    BC = sb(p1, "BC", [P, 4, NP, 16])
    SP_ = sb(p1, "SP", [P, 40, NP])
    PWA = sb(p1, "PWA", [P, 2, NP, 9])
    PWD = sb(p1, "PWD", [P, 2, NP, 8])
    HST = sb(p1, "HST", [P, 2, 4, YC])
    S0 = sb(p1, "S0", [P, 2, NP, NSEQ])
    FIN = sb(p1, "FIN", [P, 2, NP])
    FINS = sb(p1, "FINS", [P, 2, NP, NSEQ])
    TS4 = sb(p1, "TS4", [P, 4, NP, NSEQ])
    s5_left = nc.sbuf_bytes_remaining
    p1.close()
    p1 = ExitStack()
    KTS = sb(p1, "KTS", [P, SUB, NG, 16])
    p1.close()
    p1 = ExitStack()
    RT = sb(p1, "RT", [P, 4, 4, CH])
    KI = sb(p1, "KI", [P, 2, 4, CH])
    KSC = sb(p1, "KSC", [P, 2, 4, CH])
    p1.close()
    p2 = ExitStack()
    PU = sb(p2, "PU", [P, 8, T])
    PX = sb(p2, "PX", [P, 12, T])
    pc = ExitStack()
    pdt = ExitStack()
    DTT = sb(pdt, "DTT", [P, 10, 9, 8])
    CV = sb(pc, "CV", [P, 2, T])
    TH = sb(pc, "TH", [P, 2, T])
    DTF = sb(pc, "DTF", [P, T])
    SCV = sb(pc, "SCV", [P, 6, 3, NSEQ])
    CST = sb(pc, "CST", [P, 6, 3])
    CSS = sb(pc, "CSS", [P, 6, 24])
    CW = sb(pc, "CW", [P, 30])
    conv_left = nc.sbuf_bytes_remaining
    pc.close()
    pd = ExitStack()
    XS = sb(pd, "XS", [P, 512])
    BT = sb(pd, "BT", [P, P])
    ET = sb(pd, "ET", [P, 4, P])
    L = sb(pd, "L", [P, 8, P])
    CD = sb(pd, "CD", [P, 4, P])
    XD = sb(pd, "XD", [P, 512])
    DE = sb(pd, "DE", [P, 8])
    HS = sb(pd, "HS", [P, 2, 4, HD])
    H0 = sb(pd, "H0", [P, NSEQ, 4, HD])
    ssd_left = nc.sbuf_bytes_remaining
    pd.close()
    pz = ExitStack()
    ZT = sb(pz, "ZT", [P, 2, T])
    ZQ = sb(pz, "ZQ", [P, T])
    ZA = sb(pz, "ZA", [P, T])
    ZR = sb(pz, "ZR", [P, T])
    pz.close()
    pdt.close()
    pt = ExitStack()
    BIAS = sb(pt, "BIAS", [P, 8, 2 * P])
    BIASS = sb(pt, "BIASS", [P, 2, P + DSEQ])
    SB = sb(pt, "SB", [P, 2, 4, 2 * P])
    PT = sb(pt, "PT", [P, 2, 512])
    KS = sb(pt, "KS", [P, NSEQ, P + DSEQ])
    QS = sb(pt, "QS", [P, NSEQ, 32])
    SM = sb(pt, "SM", [P, 2, 6, 4])
    attn_left = nc.sbuf_bytes_remaining
    pt.close()
    VN = BIAS[0:DSEQ, 0:4, :].rearrange("p a b -> p (a b)")
    VC = BIAS[:, 4:8, :].rearrange("p a b -> p (a b)").rearrange("p (s d) -> p s d", s=NSEQ)
    pm = ExitStack()
    GTB = sb(pm, "GTB", [P, 2, T])
    MT = sb(pm, "MT", [P, 2, 384])
    pm.close()
    p2.close()
    p2 = ExitStack()
    sb(p2, "padPU", [P, 8, T])
    GF = sb(p2, "GF", [P, 4, T])
    GGH = sb(p2, "GGH", [P, 4, T], F32R)
    GGL = sb(p2, "GGL", [P, 4, T], F32R)
    GLT = sb(p2, "GLT", [P, 3, 384])
    p2.close()
    p5 = ExitStack()
    X1 = sb(p5, "X1", [P, KD, T])
    FH = sb(p5, "FH", [P, 6, T], F32R)
    FL = sb(p5, "FL", [P, 6, T], F32R)
    FS = sb(p5, "FS", [P, 3, 384])
    FM = sb(p5, "FM", [P, 3, 384])
    SQ5 = sb(p5, "SQ5", [P, T])
    AC5 = sb(p5, "AC5", [P, T])
    RS5 = sb(p5, "RS5", [P, T])
    HF5 = sb(p5, "HF5", [P, 2, 384])
    p5.close()

    def dma_sem(name):
        return sem("dma_" + name)
    w_hi, et_half, pt_first, vn_half = sem("w_high"), sem("exp_acum_half"), sem("pt_first_half"), sem("v_new_half")
    kt_ok = sem("kt_ready")
    red_pre, conv_last, yn_ok = sem("s5_angle_clamped"), sem("conv_last_tap"), sem("y_a_normed")
    bsscr = nc.dram_tensor("bias_s_scratch", (8, BW_S), F32, kind="Internal").ap()
    N_OUT_TOTAL = 11 + KD
    LF = L[0:SMP, :, :].rearrange("p a b -> p (a b)")
    LS = LF[:, 0:512].rearrange("p (i h q) -> p i h q", i=2, h=8)
    BTM = LF[:, 512:1024].rearrange("p (b d) -> p b d", b=4)
    SFN = {}

    def SF(name):
        return SP_[:, SFN.setdefault(name, len(SFN)), :]

    def conv_finish(dve, stt, i):
        dve.wait_ge(th_ok, i + 1)
        stt(PX[:, i, :], TH[:, i % 2, :], 1.0, CV[:, i % 2, :], ALU.add, ALU.mult).then_inc(xbc_ok, 1)

    def softplus_and_cumsum(dve, do, sync, tt, ts, stt):
        f = lambda i: DTT[:, i, :, :]
        dve.wait_ge(dt_tr, 1)
        do(nc.vector.memset(f(0), 0.0))
        sync()
        do(tt(f(0)[:, 0:8, :], bank[3][:, 0:64].rearrange("p (a b) -> p a b", b=8),
              bc(prm("dt_bias").unsqueeze(1), [P, 8, 8]), ALU.add))
        do(tt(f(0)[0:SMP, 8, :], bank[3][0:SMP, 64:72], prm("dt_bias")[0:SMP, :], ALU.add))
        sync()
        do(ts(f(1), f(0), -1.0, ALU.mult))
        sync()
        do(tt(f(1), f(1), f(0), ALU.min))
        sync()
        dve.sem_inc(dt_m, 1)
        dve.wait_ge(dt_e, 1)
        do(ts(f(3), f(2), 2.0, ALU.add))
        sync()
        do(nc.vector.reciprocal(f(3), f(3)))
        sync()
        do(tt(f(3), f(2), f(3), ALU.mult))
        sync()
        do(tt(f(4), f(3), f(3), ALU.mult))
        sync()
        do(ts(f(5), f(4), 1.0 / 17, ALU.mult))
        sync()
        for k in range(15, 1, -2):
            do(stt(f(5), f(5), 1.0 / k, f(4), ALU.add, ALU.mult))
            sync()
        do(stt(f(5), f(5), 1.0, f(3), ALU.add, ALU.mult))
        do(ts(f(1), f(0), 0.0, ALU.max))
        sync()
        do(stt(f(5), f(5), 2.0, f(1), ALU.mult, ALU.add))
        sync()
        dve.wait_ge(ea_ok, 1)
        tt(f(6), f(5), bc(DTT[:, 9, 0, :].unsqueeze(1), [P, 9, 8]), ALU.mult).then_inc(ap_ok, 1)

    s_par, s_x = dma_sem("params"), [dma_sem(f"x{k}") for k in range(KD)]
    s_hot = dma_sem("bucket_selection")
    s_raw = [dma_sem(f"weights{i}") for i in range(2)]
    consts_ok, split_ok = sem("consts_ok"), sem("weights_split")
    acc_done = [sem(f"acc_done{n}") for n in range(3)]
    acc_free = [sem(f"acc_free{n}") for n in range(3)]
    sq_done, sq_used = sem("square_done"), sem("square_added")
    ns_done, rs_sq, rs_ok = sem("norm_sum_done"), sem("root_done"), sem("rstd_ready")
    hf_done, h_hi, h_lo = sem("h_full"), sem("h_high"), sem("h_low")
    bias_mm, bias_ev, s_bst = sem("bias_product"), sem("bias_evicted"), dma_sem("bias_stored")
    s_ust, s_uld, s_bc = dma_sem("u_stored"), dma_sem("u_loaded"), dma_sem("s5_params")
    u_zero, step_ok, ar_ok, mag_ok = sem("u_zeroed"), sem("s5_step"), sem("s5_ar"), sem("s5_mag")
    red_ok, sin_ok, w_ok, off_ok = sem("s5_angles"), sem("s5_sines"), sem("s5_W"), sem("s5_OFF")
    kt_zero, tap_mm, tap_ev, s_kt = sem("kt_zeroed"), sem("taps_done"), sem("taps_evicted"), dma_sem("kt_shifted")
    stt_mm, stt_ev = sem("stt_transposed"), sem("stt_evicted")
    sb_mm, st_mm, ki_ok, hst_ok = sem("s5_sample_sums"), sem("s5_step_sums"), sem("s5_rotated"), sem("s5_states")
    y_mm, y_ev, gelu_ok, s_gyst = sem("s5_y_done"), sem("s5_y_evicted"), sem("gelu_done"), dma_sem("gelu_stored")
    fin_ok = sem("s5_final")
    s_out = dma_sem("outputs")
    s_gst = dma_sem("gate_stored")
    s_gf, gg_hi, gg_lo = dma_sem("gelu_loaded"), sem("glu_high"), sem("glu_low")
    s_scv, cw_ok, cst_ok, conv_ok, th_ok, xbc_ok = (dma_sem("conv_state"), sem("conv_weights"), sem("conv_tails"),
                                                    sem("conv_done"), sem("conv_tanh"), sem("xbc_ready"))
    dt_tr, dt_m, dt_e, ap_ok, ea_ok = (sem("dt_transposed"), sem("dt_minus_abs"), sem("dt_exp"), sem("dtA_ready"),
                                       sem("exp_a_log"))
    nac_mm, nac_ok = sem("cumsum_done"), sem("cumsum_evicted")
    tr_mm, bt_ok, xs_ok = sem("ssd_transposed"), sem("b_rows_ready"), sem("xs_ready")
    cb_mm, e_mm, et_ok, m_mm, l_ok = (sem("cb_done"), sem("acum_spread"), sem("exp_acum"), sem("mask_added"),
                                      sem("decay_ready"))
    mm_ok, cd_ok, xd_ok, h_ok = sem("m_ready"), sem("cd_ready"), sem("xd_ready"), sem("state_ready")
    yd_mm, ss_mm, ye_ok = sem("ssd_y_done"), sem("ssd_state_sum"), sem("ssd_y_evicted")
    s_h0, btm_ok = dma_sem("ssd_state_in"), sem("b_by_sequence")
    zt_ok, ya_ok = sem("z_tanh"), sem("y_a_ready")
    s_bias, vt_mm, vt_ok = dma_sem("bias_loaded"), sem("v_transposed"), sem("v_rows_ready")
    at_s, sb_rd, sm_ok, ex_ok, p_ok = (sem("scores_done"), sem("scores_read"), sem("max_ready"), sem("exp_done"),
                                       sem("probs_ready"))
    tp_mm, pt_ok, pv_mm, yc_ok = sem("probs_transposed"), sem("pt_ready"), sem("pv_done"), sem("y_c_ready")
    s_ks, ks_ok, s_vc, vn_mm, vn_ok = (dma_sem("k_cache"), sem("k_all_ready"), dma_sem("v_cache"),
                                       sem("v_new_transposed"), sem("v_new_ready"))
    yh_hi, yh_lo = sem("y_high"), sem("y_low")
    s_gt = [dma_sem(f"gate_loaded{i}") for i in range(2)]
    mix_ok, mx_hi, mx_lo, s_x1 = sem("mix_added"), sem("mix_high"), sem("mix_low"), dma_sem("x_again")
    f_hi, f_lo = sem("ffn_high"), sem("ffn_low")
    y_ok = sem("y_final")
    chain, row_tile = sem("dve_chain"), sem("row_tile_done")

    uscr = nc.dram_tensor("u_scratch", (512, T), F32, kind="Internal").ap()
    gscr = nc.dram_tensor("gelu_scratch", (512, T), F32, kind="Internal").ap()
    bscr = nc.dram_tensor("bias_scratch", (8, BW), F32, kind="Internal").ap()
    tscr = nc.dram_tensor("gate_scratch", (24, P, T), F32, kind="Internal").ap()
    N_OUT = [0]

    def blk(a, n):
        return a[:, P * n:P * n + P]

    def as_steps(a, n0, nb):
        return a[:, 0:SEQ].rearrange("p (s n c) -> p n s c", s=SUB, c=CB)[:, n0:n0 + nb]

    def as_blocks(a, nb):
        return a[:, 0:nb * P].rearrange("p (n s c) -> p n s c", s=SUB, c=CB)

    def bc(a, shape):
        return a.broadcast_to(shape)

    def x_wait(eng, k):
        eng.wait_ge(s_x[k], 16)

    def ssd_wait(eng, k):
        eng.wait_ge(ya_ok, k + 1)

    def x1_wait(stage):
        def wait(eng, k):
            for n in range(3):
                eng.wait_ge(acc_free[n], TILE0[stage] + k + 1)
        return wait

    NORMS = [
        dict(tiles=KD, width=D, src=lambda k: X0[:, k, :], source_ready=x_wait, sq=[SQ[:, 0, :], SQ[:, 1, :]], acc=ACC, root=RS, hf=HF,
             weight="norm1"),
        dict(tiles=4, width=512, src=lambda k: PX[:, k, :], source_ready=ssd_wait, sq=[ZQ, ZR], acc=ZA, root=ZR,
             hf=None, weight="ssd_norm"),
        dict(tiles=KD, width=D, src=lambda k: X1[:, k, :], source_ready=x1_wait("out"), sq=[SQ5, GT], acc=AC5, root=RS5, hf=HF5,
             weight="norm2"),
        dict(tiles=KD, width=D, src=lambda k: X1[:, k, :], source_ready=x1_wait("down3"), sq=[SQ5, GT], acc=AC5, root=RS5, hf=None,
             weight="normf"),
    ]
    SQ_BASE = [0, 8, 12, 20]
    HF_BASE = {0: 0, 2: 24}

    def norm_sum_act(q):
        m = NORMS[q]
        for k in range(m["tiles"]):
            g = SQ_BASE[q] + k
            m["source_ready"](nc.scalar, k)
            if k >= 2:
                nc.scalar.wait_ge(sq_used, g - 1)
            nc.scalar.activation(m["sq"][k % 2][:], m["src"](k), ACT.Square).then_inc(sq_done, 1)
        for n, (c0, w) in enumerate(CHUNKS):
            nc.scalar.wait_ge(ns_done, 3 * q + n + 1)
            nc.scalar.activation(m["root"][:, c0:c0 + w], bank[3 + n][:, 0:w], ACT.Sqrt, bias=prm("eps"),
                                 scale=1.0 / m["width"]).then_inc(rs_sq, 1)

    def norm_sum_dve(q):
        m, dve = NORMS[q], nc.vector
        for k in range(m["tiles"]):
            g = SQ_BASE[q] + k
            dve.wait_ge(sq_done, g + 1)
            if k == 0:
                dve.tensor_copy(m["acc"][:], m["sq"][0][:]).then_inc(sq_used, 1)
            else:
                dve.wait_ge(sq_used, g)
                dve.tensor_tensor(m["acc"][:], m["acc"][:], m["sq"][k % 2][:], ALU.add).then_inc(sq_used, 1)
        for n, (c0, w) in enumerate(CHUNKS):
            dve.wait_ge(rs_sq, 3 * q + n + 1)
            dve.reciprocal(m["root"][:, c0:c0 + w], m["root"][:, c0:c0 + w]).then_inc(rs_ok, 1)

    def norm_sum_pe(q):
        m = NORMS[q]
        nc.tensor.wait_ge(sq_used, SQ_BASE[q] + m["tiles"])
        for n, (c0, w) in enumerate(CHUNKS):
            nc.tensor.matmul(bank[3 + n][:, 0:w], prm("ones"), m["acc"][:, c0:c0 + w], start=True,
                             stop=True).then_inc(ns_done, 1)

    def norm_split_dve(q):
        m, dve, b = NORMS[q], nc.vector, HF_BASE[q]
        steps = [(n, k) for n in range(3) for k in range(KD)]

        def low(i):
            n, k = steps[i]
            c0, w = CHUNKS[n]
            dve.wait_ge(h_hi, b + i + 1)
            dve.tensor_tensor(HL[:, k, c0:c0 + w], m["hf"][:, i % 2, 0:w], HH[:, k, c0:c0 + w].bitcast(F32),
                              ALU.subtract).then_inc(h_lo, 1)

        for i, (n, k) in enumerate(steps):
            c0, w = CHUNKS[n]
            dve.wait_ge(rs_ok, 3 * q + n + 1)
            if i >= 2:
                dve.wait_ge(h_lo, b + i - 1)
            dve.scalar_tensor_tensor(m["hf"][:, i % 2, 0:w], m["src"](k)[:, c0:c0 + w], prm(m["weight"], k, 1),
                                     m["root"][:, c0:c0 + w], ALU.mult, ALU.mult).then_inc(hf_done, 1)
            if i >= 1:
                low(i - 1)
        low(len(steps) - 1)

    def norm_split_act(q):
        m, b = NORMS[q], HF_BASE[q]
        for i, (n, k) in enumerate([(n, k) for n in range(3) for k in range(KD)]):
            c0, w = CHUNKS[n]
            nc.scalar.wait_ge(hf_done, b + i + 1)
            nc.scalar.copy(HH[:, k, c0:c0 + w], m["hf"][:, i % 2, 0:w]).then_inc(h_hi, 1)

    def y_dst(j):
        return PX[:, j, :] if j < 4 else PU[:, j - 4, :]

    block = top.enter_context(nc.Block())

    @block.sync
    def _(sp):
        sp.dma_start(PRM[:], io["params"]).then_inc(s_par, 16)
        for k in range(KD):
            sp.dma_start(X0[:, k, :], io["x"][k]).then_inc(s_x[k], 16)
        for u in range(2):
            sp.dma_start(WRAW[:, u, :], io["w"][u]).then_inc(s_raw[u], 16)
        sp.dma_start(HOT[:], io["hot"]).then_inc(s_hot, 16)
        sp.dma_start(RTAB[:], io["rtab"]).then_inc(s_hot, 16)

        def weights(i, u, slot):
            sp.wait_ge(split_ok, u - 1)
            sp.dma_start(WRAW[:, slot, :], io["w"][bass.ds(u, 1)].rearrange("a p n -> (a p) n")).then_inc(s_raw[slot], 16)

        with sp.Fori(1, UNITS // 2) as i:
            for slot in range(2):
                weights(i, i * 2 + slot, slot)
        sp.wait_ge(split_ok, UNITS - 2)
        sp.dma_start(WRAW[:, 0, :], io["w"][UNITS - 1]).then_inc(s_raw[0], 16)
        sp.wait_ge(s_out, 16 * N_OUT_TOTAL)

    @block.gpsimd
    def _(pool):
        nc.gpsimd.memset(ZERO[:], 0.0).then_inc(consts_ok, 1)
        pool.wait_ge(s_par, 16)
        nc.gpsimd.tensor_copy(IDB[:], IDENT).then_inc(consts_ok, 1)
        nc.gpsimd.tensor_copy(MASKB[:], prm("mask")).then_inc(consts_ok, 1)
        nc.gpsimd.tensor_copy(MASKSB[:], prm("mask_s")[0:SMP, :]).then_inc(consts_ok, 1)
        pool.wait_ge(consts_ok, 4)

        def split(slot, loaded, lows_before, tiles_done):
            pool.wait_ge(s_raw[slot], loaded)
            if tiles_done is not None:
                pool.wait_ge(acc_done[2], tiles_done)
            nc.gpsimd.tensor_tensor(WH[:, slot, :], WRAW[:, slot, :], bc(ZERO[:, 0:1], [P, 1024]),
                                    ALU.add).then_inc(w_hi, 1)
            pool.wait_ge(w_hi, lows_before + 1)
            nc.gpsimd.tensor_tensor(WL[:, slot, :], WRAW[:, slot, :], WH[:, slot, :].bitcast(F32),
                                    ALU.subtract).then_inc(split_ok, 1)

        u = 0
        while u < UNITS:
            need = [None if v < 2 else TILE_END[v - 2] for v in range(UNITS)]
            e = u + 1
            if u >= 2 and u + 1 < UNITS:
                d = need[u + 1] - need[u]
                while e < UNITS and need[e] - need[e - 1] == d:
                    e += 1
            pairs = (e - u) // 2
            if pairs >= 2:
                with pool.Fori(0, pairs) as i:
                    for s in range(2):
                        v = u + s
                        split(v % 2, i * 16 + 16 * (v // 2 + 1), i * 2 + v, i * (2 * d) + need[v])
                u += 2 * pairs
            else:
                split(u % 2, 16 * (u // 2 + 1), u, need[u])
                u += 1

    @block.tensor
    def _(pe):
        def mm3(out, k, slot, rh, rl, start, stop):
            wh, wl = WH[:, slot, k * P:(k + 1) * P], WL[:, slot, k * P:(k + 1) * P]
            nc.tensor.matmul(out, wh, rl, start=start, stop=False)
            nc.tensor.matmul(out, wl, rh, start=False, stop=False)
            return nc.tensor.matmul(out, wh, rh, start=False, stop=stop)

        fences = [0]

        def fence(inst):
            fence_set(inst)
            fence_wait()

        def fence_set(inst):
            inst.then_inc(row_tile, 1)
            fences[0] += 1

        def fence_wait():
            pe.wait_ge(row_tile, fences[0])

        def tile(no, slot, koff, nk, RH, RL, kbase=0, before=None):
            for n, (c0, w) in enumerate(CHUNKS):
                if before is not None:
                    before(n)
                if not (isinstance(no, int) and no == 0):
                    pe.wait_ge(acc_free[n], no)
                for k in range(nk):
                    last = mm3(acc[n][:, 0:w], koff + k, slot, RH[:, kbase + k, c0:c0 + w], RL[:, kbase + k, c0:c0 + w],
                               k == 0, k == nk - 1)
                last.then_inc(acc_done[n], 1)

        def unit(u, slot, tiles):
            pe.wait_ge(split_ok, u + 1)
            for args, kw in tiles:
                tile(args[0], slot, *args[1:], **kw)

        def gate(g):
            u = (UNIT0["gates1"] + g) if g < 12 else (UNIT0["gates2"] + g - 12)
            no = (TILE0["gates1"] + g) if g < 12 else (TILE0["gates2"] + g - 12)
            unit(u, u % 2, [((no, 0, KD, HH, HL), {})])

        def simple_loop(name, pairs, nk, RH, RL, skip=0, kbase=0, before=None):
            u0, t0 = UNIT0[name] + skip, TILE0[name] + skip
            with pe.Fori(0, pairs) as i:
                for s in range(2):
                    unit(i * 2 + (u0 + s), (u0 + s) % 2, [((i * 2 + (t0 + s), 0, nk, RH, RL, kbase), dict(before=before))])

        pe.wait_ge(s_par, 16)
        norm_sum_pe(0)
        for j in range(4):
            unit(j, j % 2, [((j, 0, KD, HH, HL),
                             dict(before=(lambda n: pe.wait_ge(h_lo, 8 * (n + 1))) if j == 0 else None))])

        pe.wait_ge(s_hot, 32)
        for i in range(18):
            half, q = divmod(i, 9)
            if i >= 2:
                pe.wait_ge(bias_ev, i - 1)
            r = 64 * half
            nc.tensor.matmul(bank[6 + i % 2][r:r + 8, 0:BSTEP], RTAB[r:r + NBUCKET + 1, :],
                             HOT[r:r + NBUCKET + 1, q * BSTEP:(q + 1) * BSTEP], start=True, stop=True).then_inc(bias_mm, 1)
        for g in range(3):
            gate(g)

        pe.wait_ge(w_ok, 1)
        pe.wait_ge(bias_ev, 18)
        for g in [*range(0, NG, 2), *range(1, NG, 2)]:
            r = 64 * (g % 2)
            if g == 1:
                fence(last)
            for part, wt in ((0, W_re), (1, W_im)):
                last = nc.tensor.matmul(bank[7][:, g * 16:(g + 1) * 16], wt[r:r + 64, g // 2, :],
                                        BC[r:r + 64, 2 + part, g // 2, :], start=(part == 0), stop=(part == 1))
        last.then_inc(tap_mm, 1)
        for i in range(8):
            if i >= 2:
                pe.wait_ge(stt_ev, i - 1)
            wt = (W_re, W_im)[i // 4]
            for j in range(4):
                last = nc.tensor.transpose(bank[5 + i % 2][:, j * P:(j + 1) * P], wt[:, 4 * (i % 4) + j, :], IDENT)
            last.then_inc(stt_mm, 1)
        gate(3)
        gate(4)

        pe.wait_ge(stt_ev, 8)
        pe.wait_ge(s_uld, 16 * 16)
        pe.wait_ge(tap_ev, 1)
        for g in range(NG):
            r = 64 * (g % 2)
            for part in range(2):
                c = part * 128 + (g // 2) * NSEQ
                last = nc.tensor.matmul(bank[7][r:r + 64, c:c + NSEQ], STT[:, part, g // 2, r:r + 64],
                                        U[:, g, YC:YC + NSEQ], start=True, stop=True)
        last.then_inc(sb_mm, 1)

        def step_sums(b):
            if b >= 1:
                pe.wait_ge(ki_ok, b)
            for j in range(4):
                pr = 4 * b + j
                for e in range(2):
                    for part in range(2):
                        last = nc.tensor.matmul(bank[3 + part][64 * e:64 * e + 64, j * CH:(j + 1) * CH],
                                                STT[:, part, pr, 64 * e:64 * e + 64], U[:, 2 * pr + e, 0:CH],
                                                start=True, stop=True)
            last.then_inc(st_mm, 1)

        def outputs(b):
            pe.wait_ge(hst_ok, b + 1)
            if b == 0:
                pe.wait_ge(kt_ok, 1)
                pe.wait_ge(off_ok, 1)
            for j in range(4):
                pr = 4 * b + j
                if pr >= 2:
                    pe.wait_ge(y_ev, pr - 1)
                for e in range(2):
                    g = 2 * pr + e
                    o = bank[5 + pr % 2][:, 256 * e:256 * e + YC]
                    nc.tensor.matmul(o, KT[:, g, :, :].rearrange("p t h -> p (t h)"), U[:, g, 0:YC], start=True, stop=False)
                    if e == 1:
                        fence_wait()
                    nc.tensor.matmul(o, OFF_re[64 * e:64 * e + 64, pr, :], HST[64 * e:64 * e + 64, 0, j, :],
                                     start=False, stop=False)
                    last = nc.tensor.matmul(o, OFF_im[64 * e:64 * e + 64, pr, :], HST[64 * e:64 * e + 64, 1, j, :],
                                            start=False, stop=True)
                    if e == 0:
                        fence_set(last)
                last.then_inc(y_mm, 1)

        step_sums(0)
        gate(5)
        step_sums(1)
        gate(6)
        outputs(0)
        step_sums(2)
        gate(7)
        outputs(1)
        step_sums(3)
        gate(8)
        outputs(2)
        gate(9)
        outputs(3)
        gate(10)
        gate(11)

        for i in range(4):
            u, no = UNIT0["glu"] + i, TILE0["glu"] + 2 * i
            if i == 0:
                pe.wait_ge(gg_lo, 4)
            unit(u, u % 2, [((no, 0, 4, GGH, GGL), {}), ((no + 1, 4, 4, GGH, GGL), {})])

        def dt_rows():
            for n in range(3):
                pe.wait_ge(acc_free[n], TILE0["proj"] + 7)
            for n in range(NBLK):
                nc.tensor.transpose(bank[3][:, n * 8:n * 8 + 8], blk(DTF[0:8, :], n), IDENT[0:8, 0:8])
            nc.tensor.transpose(bank[3][0:SMP, 64:72], DTF[0:8, SEQ:T], IDENT[0:8, 0:8]).then_inc(dt_tr, 1)

        simple_loop("proj", 4, KD, HH, HL)
        dt_rows()
        simple_loop("proj", 4, KD, HH, HL, skip=8)
        u = UNIT0["proj"] + 16
        unit(u, u % 2, [((TILE0["proj"] + 16, 0, KD, HH, HL), {})])

        def ssd_setup():
            pe.wait_ge(ap_ok, 1)
            pe.wait_ge(y_ev, 16)
            pe.wait_ge(fin_ok, 5)
            nc.tensor.matmul(bank[4][:, 0:64], prm("tri"), DTT[:, 6, 0:8, :], start=True, stop=True)
            nc.tensor.matmul(bank[4][0:SMP, 64:72], prm("tri_s")[0:SMP, :], DTT[0:SMP, 6, 8, :], start=True,
                             stop=True).then_inc(nac_mm, 1)
            pe.wait_ge(nac_ok, 1)
            pe.wait_ge(xbc_ok, 6)
            pe.wait_ge(consts_ok, 4)

        def ssd_chunk(n):
            smp = n == NBLK
            rows = SMP if smp else P
            cols = (lambda a: a[:, SEQ:T]) if smp else (lambda a: blk(a, n))
            tri = prm("negtri_s")[0:SMP, :] if smp else prm("negtri")
            pe.wait_ge(h_ok, n + 1)
            for i in range(4):
                nc.tensor.transpose(bank[3][0:rows, i * P:(i + 1) * P], cols(PX[:, i, :]), IDENT)
            if n >= 1:
                pe.wait_ge(mm_ok, n)
            nc.tensor.transpose(bank[4][0:rows, 0:P], cols(PX[:, 4, :]), IDENT).then_inc(tr_mm, 1)
            for g in range(2):
                r = 64 * g
                if g == 1:
                    fence(last)
                last = nc.tensor.matmul(bank[4][0:rows, P + r * 2:P + r * 2 + rows], cols(PX[r:r + 64, 4, :]),
                                        cols(PX[r:r + 64, 5, :]), start=True, stop=True)
            last.then_inc(cb_mm, 1)
            for g in range(2):
                if n >= 1:
                    pe.wait_ge(l_ok, n)
                for k in range(4):
                    last = nc.tensor.matmul(bank[5 + g][:, k * rows:(k + 1) * rows],
                                            bc(DTT[0:rows, 6, n, 4 * g + k:4 * g + k + 1], [rows, P]), tri,
                                            start=(k == 0), stop=(k == 3), skip_group_check=True)
                last.then_inc(e_mm, 1)
            pe.wait_ge(et_ok, n + 1)
            for g in range(2):
                mask = MASKSB[:] if smp else MASKB[:]
                last = nc.tensor.matmul(bank[5 + g][0:rows, 0:4 * rows], IDB[0:rows, 0:rows],
                                        bc(mask.unsqueeze(1), [rows, 4, rows]), start=False, stop=True,
                                        skip_group_check=True)
            last.then_inc(m_mm, 1)
            gate(12 + n)
            pe.wait_ge(mm_ok, n + 1)
            pe.wait_ge(cd_ok, n + 1)
            if n >= 1:
                pe.wait_ge(ye_ok, n)
            for h in range(8):
                g, k, i, r = h // 4, h % 4, h // 2, 64 * (h % 2)
                if h == 4:
                    fence(last)
                o = bank[7][r:r + 64, i * P:i * P + rows]
                m = L[0:rows, h, 0:rows] if not smp else LS[:, 1, h, :]
                nc.tensor.matmul(o, XS[0:rows, h * HD:(h + 1) * HD], m, start=True, stop=smp)
                if not smp:
                    last = nc.tensor.matmul(o, HS[64 * g:64 * g + 64, n % 2, k, :], CD[64 * g:64 * g + 64, k, :],
                                            start=False, stop=True)
                else:
                    for b in range(NSEQ):
                        last = nc.tensor.matmul(o[:, b:SMP:NSEQ], H0[64 * g:64 * g + 64, b, k, :],
                                                CD[64 * g:64 * g + 64, 0, k * SMP + b:(k + 1) * SMP:NSEQ],
                                                start=False, stop=True, skip_group_check=True)
            last.then_inc(yd_mm, 1)
            if not smp:
                pe.wait_ge(bt_ok, n + 1)
                pe.wait_ge(xd_ok, n + 1)
                for g in range(2):
                    last = nc.tensor.matmul(bank[3][64 * g:64 * g + 64, 0:256], BT[:, 64 * g:64 * g + 64],
                                            XD[:, 256 * g:256 * g + 256], start=True, stop=True)
                last.then_inc(ss_mm, 1)
            else:
                for b in range(NSEQ):
                    if b % 4 == 0:
                        pe.wait_ge(btm_ok, b // 4 + 1)
                    if b >= 2:
                        pe.wait_ge(h_ok, NBLK + b)
                    else:
                        pe.wait_ge(xd_ok, n + 1)
                    for g in range(2):
                        last = nc.tensor.matmul(bank[(3, 4)[b % 2]][64 * g:64 * g + 64, 0:256],
                                                BTM[:, b % 4, 64 * g:64 * g + 64],
                                                XD[0:SMP, 256 * g:256 * g + 256], start=True, stop=True)
                    last.then_inc(ss_mm, 1)

        ssd_setup()
        for n in range(NBLK + 1):
            ssd_chunk(n)
        gate(21)
        pe.wait_ge(h_ok, NBLK + 1 + NSEQ)
        norm_sum_pe(1)

        pe.wait_ge(rs_sq, 6)
        pe.wait_ge(h_ok, NBLK + 1 + NSEQ)
        for n in range(NBLK):
            last = nc.tensor.transpose(bank[5 + n // 4][:, (n % 4) * P:(n % 4 + 1) * P], blk(PX[:, 7, :], n), IDENT)
        last.then_inc(vt_mm, 1)

        def scores(a):
            n, kv = divmod(a, 2)
            if a >= 1:
                pe.wait_ge(sb_rd, a)
            lo = P if n == 0 else 0
            for i in range(4):
                at = (i % 2) * 256
                last = nc.tensor.matmul(bank[3 + i // 2][:, at + lo:at + 256], blk(PU[64 * kv:64 * kv + 64, 4 + i, :], n),
                                        PX[64 * kv:64 * kv + 64, 6, P * (n - 1) + lo:P * (n + 1)],
                                        start=True, stop=True)
            last.then_inc(at_s, 1)

        def pv(a):
            n, kv = divmod(a, 2)
            pe.wait_ge(p_ok, a + 1)
            if a >= 1:
                pe.wait_ge(pt_ok, a)
            else:
                pe.wait_ge(vt_ok, 2)
            for half in range(1 if n == 0 else 0, 2):
                for i in range(4):
                    last = nc.tensor.transpose(bank[5 + half][:, i * P:(i + 1) * P],
                                               SB[:, a % 2, i, half * P:half * P + P], IDENT)
            last.then_inc(tp_mm, 1)
            pe.wait_ge(pt_ok, a + 1)
            if a >= 1:
                pe.wait_ge(yc_ok, a)
            else:
                pe.wait_ge(ye_ok, NBLK + 1)
            vt = PX[:, 7, 0:SEQ].rearrange("p (n d) -> p n d", n=NBLK)
            o = bank[7][64 * kv:64 * kv + 64, :]
            if n >= 1:
                nc.tensor.matmul(o, vt[:, n - 1, 64 * kv:64 * kv + 64], PT[:, 0, :], start=True, stop=False)
            nc.tensor.matmul(o, vt[:, n, 64 * kv:64 * kv + 64], PT[:, 1, :], start=(n == 0), stop=True).then_inc(pv_mm, 1)

        scores(0)
        for a in range(2 * NBLK):
            if a in (4, 8):
                gate({4: 22, 8: 23}[a])
            if a + 1 < 2 * NBLK:
                scores(a + 1)
            pv(a)

        pe.wait_ge(ks_ok, 2)
        pe.wait_ge(sb_rd, 2 * NBLK)
        for kv in range(2):
            if kv == 1:
                fence(last)
            for b in range(NSEQ):
                r, y = 32 * (b % 4), 2 * (b // 4) + kv
                o = bank[3 + y // 2][r:r + 32, (y % 2) * 256:(y % 2) * 256 + P + DSEQ]
                last = nc.tensor.matmul(o, QS[64 * kv:64 * kv + 64, b, :], KS[64 * kv:64 * kv + 64, b, :],
                                        start=True, stop=True)
        last.then_inc(at_s, 1)
        pe.wait_ge(pt_ok, 2 * NBLK)
        for b in range(NSEQ):
            last = nc.tensor.transpose(bank[5 + b // 4][0:DSEQ, (b % 4) * P:(b % 4 + 1) * P],
                                       PX[:, 7, SEQ + b:T:NSEQ], IDENT)
        last.then_inc(vn_mm, 1)
        pe.wait_ge(vn_ok, 1)
        pe.wait_ge(p_ok, 2 * NBLK + 1)
        for y in range(4):
            nc.tensor.transpose(bank[5][:, y * P:(y + 1) * P], SB[:, 0, y, 0:P], IDENT)
            last = nc.tensor.transpose(bank[6][0:DSEQ, y * P:(y + 1) * P], SB[:, 0, y, P:P + DSEQ], IDENT)
        last.then_inc(tp_mm, 1)
        pe.wait_ge(pt_ok, 2 * NBLK + 1)
        pe.wait_ge(s_vc, 16)
        pe.wait_ge(yc_ok, 2 * NBLK)
        for b in range(NSEQ):
            for kv in range(2):
                y = 2 * (b // 4) + kv
                at = y * P + 32 * (b % 4)
                o = bank[7][64 * kv:64 * kv + 64, b * 16:(b + 1) * 16]
                nc.tensor.matmul(o, VC[:, b, 64 * kv:64 * kv + 64], PT[:, 0, at:at + 16], start=True, stop=False)
                last = nc.tensor.matmul(o, VN[:, b * P + 64 * kv:b * P + 64 * kv + 64], PT[0:DSEQ, 1, at:at + 16],
                                        start=False, stop=True)
        last.then_inc(pv_mm, 1)

        for q in range(3):
            for i in range(4):
                u, no = UNIT0["branch"] + 4 * q + i, TILE0["branch"] + 8 * q + 2 * i
                if i == 0:
                    pe.wait_ge(yh_lo, 4 * (q + 1))
                kb = (4, 0, 4)[q]
                unit(u, u % 2, [((no, 0, 4, HH, HL, kb), {}), ((no + 1, 4, 4, HH, HL, kb), {})])

        simple_loop("out", 4, KD, HH, HL, before=lambda n: pe.wait_ge(mx_lo, 8 * (n + 1)))
        norm_sum_pe(2)

        ff = 0
        for p, nf in enumerate(FFN_PASSES):
            simple_loop(f"up{p}", nf, KD, HH, HL,
                        before=(lambda n: pe.wait_ge(h_lo, 24 + 8 * (n + 1))) if p == 0 else None)
            ff += nf
            pe.wait_ge(f_lo, 3 * ff)
            simple_loop(f"down{p}", 4, nf, FH, FL)
        norm_sum_pe(3)

    @block.scalar
    def _(act):
        outs = [0]

        def out_dma(dst, src):
            act.dma_start(dst, src).then_inc(s_out, 16)
            outs[0] += 1

        def outs_landed():
            act.wait_ge(s_out, 16 * outs[0])

        def evict(no, dst):
            for n, (c0, w) in enumerate(CHUNKS):
                act.wait_ge(acc_done[n], no + 1)
                nc.scalar.copy(dst[:, c0:c0 + w], acc[n][:, 0:w]).then_inc(acc_free[n], 1)

        def evicted(no):
            for n in range(3):
                act.wait_ge(acc_free[n], no + 1)

        def gate(g):
            no = (TILE0["gates1"] + g) if g < 12 else (TILE0["gates2"] + g - 12)
            if g >= 1:
                act.wait_ge(s_gst, 16 * g)
            for n, (c0, w) in enumerate(CHUNKS):
                act.wait_ge(acc_done[n], no + 1)
                nc.scalar.activation(GT[:, c0:c0 + w], acc[n][:, 0:w], ACT.Tanh, scale=0.5).then_inc(acc_free[n], 1)
            evicted(no)
            act.dma_start(tscr[g], GT[:]).then_inc(s_gst, 16)

        act.wait_ge(s_par, 16)
        norm_sum_act(0)
        norm_split_act(0)

        for j in range(4):
            for n, (c0, w) in enumerate(CHUNKS):
                nb = min(w // P, NBLK - c0 // P)
                act.wait_ge(acc_done[n], j + 1)
                last = nc.scalar.copy(as_steps(UF[:, j, :], c0 // P, nb), as_blocks(acc[n], nb))
                if w > nb * P:
                    last = nc.scalar.copy(UF[:, j, SEQ:T], acc[n][:, nb * P:w])
                last.then_inc(acc_free[n], 1)
            evicted(TILE0["u"] + j)
            act.dma_start(uscr[j * P:(j + 1) * P, :], UF[:, j, :]).then_inc(s_ust, 16)
        for i in range(18):
            half, q = divmod(i, 9)
            r = 64 * half
            act.wait_ge(bias_mm, i + 1)
            nc.scalar.copy(BTAB[r:r + 8, q * BSTEP:(q + 1) * BSTEP], bank[6 + i % 2][r:r + 8, 0:BSTEP]).then_inc(bias_ev, 1)
        act.wait_ge(bias_ev, 18)
        act.dma_start(bscr[:, 0:BHALF], BTAB[0:8, :]).then_inc(s_bst, 16)
        act.dma_start(bscr[:, BHALF:BW_P], BTAB[64:72, 0:BW_P - BHALF]).then_inc(s_bst, 16)
        act.dma_start(bsscr, BTAB[64:72, BW_P - BHALF:BHALF]).then_inc(s_bst, 16)
        act.wait_ge(h_lo, 24)
        act.wait_ge(s_bst, 48)
        act.dma_start(BC[:], io["bc"]).then_inc(s_bc, 16)
        act.dma_start(S0[:], io["s0"]).then_inc(s_bc, 16)
        act.wait_ge(s_ust, 64)
        act.wait_ge(u_zero, 1)
        for s in range(SUB):
            act.dma_start(U[s * 16:(s + 1) * 16, :, 0:CH],
                          bass.AP(tensor=uscr.tensor, offset=s * CH, ap=[[T, 16], [16 * T, NG], [1, CH]])).then_inc(s_uld, 16)
        for t in range(DSEQ):
            src = bass.AP(tensor=uscr.tensor, offset=SEQ + t * NSEQ, ap=[[T, 16], [16 * T, NG], [1, NSEQ]])
            act.dma_start(U[t * 16:(t + 1) * 16, :, CH + 1:YC], src).then_inc(s_uld, 16)
            act.dma_start(U[(t + 4) * 16:(t + 5) * 16, :, YC:UC], src).then_inc(s_uld, 16)

        nc.scalar.activation(SF("step"), prm("log_dt"), ACT.Exp).then_inc(step_ok, 1)
        gate(0)
        act.wait_ge(ar_ok, 1)
        nc.scalar.activation(SF("mag"), SF("ar"), ACT.Exp).then_inc(mag_ok, 1)
        gate(1)
        act.wait_ge(red_ok, 1)
        nc.scalar.activation(SF("sin"), SF("r"), ACT.Sin)
        nc.scalar.activation(SF("cos"), SF("r2"), ACT.Sin).then_inc(sin_ok, 1)
        gate(2)
        for i in range(8):
            act.wait_ge(stt_mm, i + 1)
            nc.scalar.copy(STT[:, i // 4, 4 * (i % 4):4 * (i % 4) + 4, :].rearrange("p a b -> p (a b)"),
                           bank[5 + i % 2][:]).then_inc(stt_ev, 1)
        act.wait_ge(tap_mm, 1)
        act.wait_ge(kt_zero, 1)
        nc.scalar.copy(KTS[:, SUB - 1, :, :].rearrange("p g h -> p (g h)"), bank[7][:]).then_inc(tap_ev, 1)
        act.wait_ge(tap_ev, 1)
        for t in range(SUB - 1):
            act.dma_start(KTS[0:(t + 1) * 16, t, :, :], KTS[(SUB - 1 - t) * 16:P, SUB - 1, :, :]).then_inc(s_kt, 16)
        gate(3)
        gate(4)
        gate(5)
        gate(6)
        for b in range(4):
            for j in range(4):
                pr = 4 * b + j
                act.wait_ge(y_ev, pr + 1)
                nc.scalar.activation(U[:, 2 * pr:2 * pr + 2, 0:YC], U[:, 2 * pr:2 * pr + 2, 0:YC],
                                     ACT.Gelu_apprx_tanh).then_inc(gelu_ok, 1)
            if b < 3:
                gate(7 + b)
        act.wait_ge(gelu_ok, 16)
        for s in range(SUB):
            act.dma_start(bass.AP(tensor=gscr.tensor, offset=s * CH, ap=[[T, 16], [16 * T, NG], [1, CH]]),
                          U[s * 16:(s + 1) * 16, :, 0:CH]).then_inc(s_gyst, 16)
        for t in range(DSEQ):
            act.dma_start(bass.AP(tensor=gscr.tensor, offset=SEQ + t * NSEQ, ap=[[T, 16], [16 * T, NG], [1, NSEQ]]),
                          U[t * 16:(t + 1) * 16, :, CH + 1:YC]).then_inc(s_gyst, 16)
        act.wait_ge(fin_ok, 5)
        out_dma(io["s5p"], FIN[:])
        out_dma(io["s5s"], FINS[:])
        gate(10)
        gate(11)
        act.wait_ge(s_gyst, 12 * 16)
        act.wait_ge(y_mm, 16)
        outs_landed()
        for j in range(4):
            act.dma_start(GF[:, j, :], gscr[j * P:(j + 1) * P, :]).then_inc(s_gf, 16)
        act.wait_ge(s_gf, 64)
        for j in range(4):
            nc.scalar.copy(as_blocks(GGH[:, j, :], NBLK), as_steps(GF[:, j, :], 0, NBLK))
            nc.scalar.copy(GGH[:, j, SEQ:T], GF[:, j, SEQ:T]).then_inc(gg_hi, 1)
        for i in range(4):
            no = TILE0["glu"] + 2 * i
            for n, (c0, w) in enumerate(CHUNKS):
                act.wait_ge(acc_done[n], no + 1)
                nc.scalar.activation(GLT[:, n, 0:w], acc[n][:, 0:w], ACT.Sigmoid).then_inc(acc_free[n], 1)
        evicted(TILE0["proj"] - 1)
        act.dma_start(SCV[:], io["scv"]).then_inc(s_scv, 16)
        nc.scalar.activation(DTT[:, 9, 0, :], prm("a_log"), ACT.Exp).then_inc(ea_ok, 1)

        dests = [PX[:, i, :] for i in range(6)] + [DTF] + [PX[:, i, :] for i in (6, 7, 8, 9, 10, 11)] + \
                [PU[:, i, :] for i in (4, 5, 6, 7)]
        for i, dst in enumerate(dests):
            evict(TILE0["proj"] + i, dst)
            if i == 7:
                act.wait_ge(dt_m, 1)
                nc.scalar.activation(DTT[:, 2, :, :], DTT[:, 1, :, :], ACT.Exp).then_inc(dt_e, 1)
            if 8 <= i < 14:
                c = i - 8
                act.wait_ge(conv_ok, c + 1)
                if c >= 2:
                    act.wait_ge(xbc_ok, c - 1)
                nc.scalar.activation(TH[:, c % 2, :], CV[:, c % 2, :], ACT.Tanh).then_inc(th_ok, 1)
        act.wait_ge(cst_ok, 1)
        out_dma(io["conv_p"], CST[:])
        out_dma(io["conv_s"], CSS[:])
        evicted(TILE0["proj"] + 8)
        out_dma(io["kp"], blk(PX[:, 6, :], NBLK - 1))
        out_dma(io["vp"], blk(PX[:, 7, :], NBLK - 1))
        act.wait_ge(xbc_ok, 6)
        outs_landed()
        act.dma_start(H0[:], io["h0"]).then_inc(s_h0, 16)

        for n in range(NBLK + 1):
            smp = n == NBLK
            rows = SMP if smp else P
            act.wait_ge(cb_mm, n + 1)
            if n >= 1:
                act.wait_ge(ss_mm, n)
            nc.scalar.copy(BT[0:rows, :], bank[4][0:rows, 0:P]).then_inc(bt_ok, 1)
            act.wait_ge(e_mm, 2 * n + 2)
            if n >= 1:
                act.wait_ge(h_ok, n + 1)
                act.wait_ge(cd_ok, n)
            etf = ET[:].rearrange("p a b -> p (a b)")
            for g in range(2):
                nc.scalar.activation(etf[64 * g:64 * g + 64, 0:4 * rows], bank[5 + g][64 * g:64 * g + 64, 0:4 * rows],
                                     ACT.Exp).then_inc(et_half, 1)
            act.wait_ge(et_half, 2 * n + 2)
            act.sem_inc(et_ok, 1)
            act.wait_ge(m_mm, n + 1)
            if n >= 1:
                act.wait_ge(yd_mm, n)
                act.wait_ge(xd_ok, n)
            for h in range(8):
                dst = LS[:, 0, h, :] if smp else L[:, h, :]
                last = nc.scalar.activation(dst, bank[5 + h // 4][0:rows, (h % 4) * rows:(h % 4 + 1) * rows], ACT.Exp,
                                            bias=DTT[0:rows, 7, n, h:h + 1])
            last.then_inc(l_ok, 1)
            gate(12 + n)

        act.wait_ge(h_ok, NBLK + 1 + NSEQ)
        out_dma(io["ssd_p"], HS[:, 0, :, :])
        out_dma(io["ssd_s"], H0[:])
        outs_landed()
        act.wait_ge(ye_ok, NBLK + 1)
        for k in range(4):
            if k >= 2:
                act.wait_ge(ya_ok, k - 1)
            nc.scalar.activation(ZT[:, k % 2, :], PX[:, 8 + k, :], ACT.Tanh, scale=0.5).then_inc(zt_ok, 1)
        gate(21)
        norm_sum_act(1)

        act.wait_ge(yn_ok, 4)
        for s in range(SUB):
            for half in range(2):
                act.dma_start(BIAS[s * CB:(s + 1) * CB, :, half * P:half * P + P],
                              bass.AP(tensor=bscr.tensor, offset=(SUB - 1 - s + half * (2 * SUB - 1)) * CB,
                                      ap=[[(2 * SUB - 1) * 2 * CB, CB], [BW, 8], [1, P]])).then_inc(s_bias, 16)
        for r in range(0, P, 16):
            act.dma_start(BIASS[r:r + 16, :, :],
                          bass.AP(tensor=bsscr.tensor, offset=0,
                                  ap=[[P + DSEQ, 16], [4 * BW_S, 2], [1, P + DSEQ]])).then_inc(s_bias, 16)
        act.dma_start(KS[:, :, 0:P], io["ks"]).then_inc(s_ks, 16)
        act.wait_ge(vt_mm, 1)
        for i in range(2):
            nc.scalar.copy(PX[:, 7, 512 * i:512 * i + 512], bank[5 + i][:]).then_inc(vt_ok, 1)

        def exps(a):
            smp = a == 2 * NBLK
            act.wait_ge(sm_ok, a + 1)
            w = P + DSEQ if smp else 2 * P
            for i in range(4):
                v = SB[:, a % 2, i, 0:w]
                nc.scalar.activation(v, v, ACT.Exp, bias=SM[:, a % 2, 1, i:i + 1], accum_out=SM[:, a % 2, 3, i:i + 1])
            nc.scalar.activation(SM[:, a % 2, 4, :], SM[:, a % 2, 2, :], ACT.Exp).then_inc(ex_ok, 1)

        def p_rows(a):
            n = a // 2
            act.wait_ge(tp_mm, a + 1)
            if a >= 1:
                act.wait_ge(pv_mm, a)
            if n >= 1:
                nc.scalar.copy(PT[:, 0, :], bank[5][:]).then_inc(pt_first, 1)
            nc.scalar.copy(PT[:, 1, :], bank[6][:]).then_inc(pt_ok, 1)
            act.wait_ge(pv_mm, a + 1)
            kv = a % 2
            for i in range(4):
                last = nc.scalar.copy(blk(PU[64 * kv:64 * kv + 64, 4 + i, :], n),
                                      bank[7][64 * kv:64 * kv + 64, i * P:(i + 1) * P])
            last.then_inc(yc_ok, 1)

        exps(0)
        for a in range(2 * NBLK):
            if a in (4, 8):
                gate({4: 22, 8: 23}[a])
            if a + 1 < 2 * NBLK:
                exps(a + 1)
            p_rows(a)
        act.wait_ge(sb_rd, 2 * NBLK)
        act.dma_start(VC[:], io["vc"]).then_inc(s_vc, 16)
        act.wait_ge(vn_mm, 1)
        for i in range(2):
            nc.scalar.copy(VN[:, 512 * i:512 * i + 512], bank[5 + i][0:DSEQ, :]).then_inc(vn_half, 1)
        act.wait_ge(vn_half, 2)
        act.sem_inc(vn_ok, 1)
        act.wait_ge(ks_ok, 1)
        out_dma(io["kns"], KS[:, :, DSEQ:P + DSEQ])
        out_dma(io["vns"][P - DSEQ:P], VN.rearrange("p (s d) -> p s d", s=NSEQ))
        act.wait_ge(s_vc, 16)
        out_dma(io["vns"][0:P - DSEQ], VC[DSEQ:P, :, :])
        exps(2 * NBLK)
        act.wait_ge(tp_mm, 2 * NBLK + 1)
        nc.scalar.copy(PT[:, 0, :], bank[5][:]).then_inc(pt_first, 1)
        nc.scalar.copy(PT[0:DSEQ, 1, :], bank[6][0:DSEQ, :]).then_inc(pt_first, 1)
        act.wait_ge(pt_first, 2 * NBLK)
        act.sem_inc(pt_ok, 1)
        act.wait_ge(pv_mm, 2 * NBLK + 1)
        for i in range(4):
            last = nc.scalar.copy(PU[:, 4 + i, SEQ:T].rearrange("p (t b) -> p t b", b=NSEQ),
                                  bank[7][:, 0:P].rearrange("p (b i t) -> p i t b", i=4, t=DSEQ)[:, i])
        last.then_inc(yc_ok, 1)

        def y_high(q):
            for j in range(4):
                src = [PU[:, j, :], PX[:, j, :], PU[:, 4 + j, :]][q]
                nc.scalar.copy(HH[:, (4, 0, 4)[q] + j, :], src).then_inc(yh_hi, 1)

        def load_gate(t):
            q, j = divmod(t, 8)
            if t >= 2:
                act.wait_ge(acc_free[2], TILE0["branch"] + t - 1)
            act.dma_start(GTB[:, t % 2, :], tscr[(8, 0, 16)[q] + j]).then_inc(s_gt[t % 2], 16)

        act.wait_ge(acc_done[2], TILE_END[UNIT0["branch"] - 1])
        y_high(0)
        y_high(1)
        act.wait_ge(yc_ok, 2 * NBLK + 1)
        outs_landed()
        act.wait_ge(s_gst, 24 * 16)
        for t in range(24):
            load_gate(t)
            if t == 9:
                act.wait_ge(acc_done[2], TILE0["branch"] + 8)
                y_high(2)
        act.wait_ge(acc_done[2], TILE0["out"])
        act.wait_ge(mix_ok, 72)
        for n, (c0, w) in enumerate(CHUNKS):
            for k in range(KD):
                nc.scalar.copy(HH[:, k, c0:c0 + w], y_dst(k)[:, c0:c0 + w]).then_inc(mx_hi, 1)
        act.wait_ge(mx_lo, 24)
        for k in range(KD):
            act.dma_start(X1[:, k, :], io["x"][k]).then_inc(s_x[k], 16)
        norm_sum_act(2)
        norm_split_act(2)

        ff = 0
        for p, nf in enumerate(FFN_PASSES):
            t0 = TILE0[f"up{p}"]
            for f in range(nf):
                no = t0 + 2 * f
                for n, (c0, w) in enumerate(CHUNKS):
                    act.wait_ge(acc_done[n], no + 1)
                    nc.scalar.activation(FS[:, n, 0:w], acc[n][:, 0:w], ACT.Silu).then_inc(acc_free[n], 1)
                if f == 0 and p > 0:
                    act.wait_ge(acc_done[2], t0)
                for n, (c0, w) in enumerate(CHUNKS):
                    act.wait_ge(acc_free[n], no + 2)
                    nc.scalar.copy(FH[:, f, c0:c0 + w], FM[:, n, 0:w]).then_inc(f_hi, 1)
            ff += nf
        norm_sum_act(3)
        for k in range(KD):
            act.wait_ge(y_ok, 3 * (k + 1))
            out_dma(io["y"][k], X1[:, k, :])
        assert outs[0] == N_OUT_TOTAL

    @block.vector
    def _(dve):
        count = [0]

        def do(ins):
            ins.then_inc(chain, 1)
            count[0] += 1

        def sync():
            dve.wait_ge(chain, count[0])

        def tt(out, a, b, op=ALU.mult):
            return nc.vector.tensor_tensor(out, a, b, op)

        def ts(out, a, s1, op0, s2=None, op1=None):
            if op1 is None:
                return nc.vector.tensor_scalar(out, a, s1, None, op0)
            return nc.vector.tensor_scalar(out, a, s1, s2, op0, op1)

        def stt(out, a, s, b, op0=ALU.mult, op1=ALU.mult):
            return nc.vector.scalar_tensor_tensor(out=out, in0=a, scalar=s, in1=b, op0=op0, op1=op1)

        def cmul(o_re, o_im, a_re, a_im, b_re, b_im, t):
            do(tt(t[0], a_re, b_re))
            do(tt(t[1], a_im, b_im))
            do(tt(t[2], a_re, b_im))
            do(tt(t[3], a_im, b_re))
            sync()
            do(tt(o_re, t[0], t[1], ALU.subtract))
            do(tt(o_im, t[2], t[3], ALU.add))
            sync()

        norm_sum_dve(0)
        norm_split_dve(0)

        dve.wait_ge(s_bst, 48)
        dve.wait_ge(acc_free[0], 4)
        do(nc.vector.memset(HST[:], 0.0))
        nc.vector.memset(U[:, :, CH:UC], 0.0).then_inc(u_zero, 1)
        lre, lim = prm("lam_re"), prm("lam_im")
        dve.wait_ge(step_ok, 1)
        tt(SF("ar"), lre, SF("step")).then_inc(ar_ok, 1)
        do(tt(SF("th"), lim, SF("step")))
        sync()
        MAGIC, C1 = 12582912.0, 6.28125
        C2, PI = 2 * math.pi - C1, 3.1415925
        do(ts(SF("n"), SF("th"), 1 / (2 * math.pi), ALU.mult, MAGIC, ALU.add))
        sync()
        do(ts(SF("n"), SF("n"), MAGIC, ALU.subtract))
        sync()
        do(stt(SF("r"), SF("n"), -C1, SF("th"), ALU.mult, ALU.add))
        sync()
        do(stt(SF("r"), SF("n"), -C2, SF("r"), ALU.mult, ALU.add))
        sync()
        do(ts(SF("r2"), SF("r"), math.pi / 2, ALU.add))
        sync()
        do(ts(SF("n"), SF("r2"), math.pi, ALU.is_gt, -2 * math.pi, ALU.mult))
        sync()
        do(tt(SF("r2"), SF("r2"), SF("n"), ALU.add))
        sync()
        do(ts(SF("r2"), SF("r2"), PI, ALU.min, -PI, ALU.max))
        ts(SF("r"), SF("r"), PI, ALU.min, -PI, ALU.max).then_inc(red_pre, 1)
        dve.wait_ge(red_pre, 1)
        sync()
        dve.sem_inc(red_ok, 1)
        dve.wait_ge(mag_ok, 1)
        dve.wait_ge(sin_ok, 1)
        t4 = [TS4[:, i, :, 0] for i in range(4)]
        do(nc.vector.memset(PWA[:, 0, :, 0], 1.0))

        def unit(re, im):
            do(tt(t4[0], re, re))
            do(tt(t4[1], im, im))
            sync()
            do(tt(t4[0], t4[0], t4[1], ALU.add))
            sync()
            do(ts(t4[0], t4[0], -0.5, ALU.mult, 1.5, ALU.add))
            sync()
            do(tt(re, re, t4[0]))
            do(tt(im, im, t4[0]))
            sync()

        unit(SF("cos"), SF("sin"))
        do(nc.vector.memset(PWA[:, 1, :, 0], 0.0))
        do(tt(PWA[:, 0, :, 1], SF("mag"), SF("cos")))
        do(tt(PWA[:, 1, :, 1], SF("mag"), SF("sin")))
        sync()
        cmul(PWA[:, 0, :, 2], PWA[:, 1, :, 2], PWA[:, 0, :, 1], PWA[:, 1, :, 1], PWA[:, 0, :, 1], PWA[:, 1, :, 1], t4)
        for k in (2, 4):
            cmul(PWA[:, 0, :, k + 1:2 * k + 1], PWA[:, 1, :, k + 1:2 * k + 1],
                 PWA[:, 0, :, 1:k + 1], PWA[:, 1, :, 1:k + 1],
                 bc(PWA[:, 0, :, k:k + 1], [P, NP, k]), bc(PWA[:, 1, :, k:k + 1], [P, NP, k]),
                 [TS4[:, i, :, 0:k] for i in range(4)])
        for i in range(SUB):
            do(nc.vector.tensor_copy(PWD[:, :, :, i], PWA[:, :, :, SUB - 1 - i]))
        do(ts(SF("am"), PWA[:, 0, :, 1], 1.0, ALU.subtract))
        do(tt(SF("den"), lre, lre))
        do(tt(SF("n"), lim, lim))
        sync()
        do(tt(SF("den"), SF("den"), SF("n"), ALU.add))
        sync()
        do(nc.vector.reciprocal(SF("den"), SF("den")))
        do(tt(t4[0], SF("am"), lre))
        do(tt(t4[1], PWA[:, 1, :, 1], lim))
        do(tt(t4[2], PWA[:, 1, :, 1], lre))
        do(tt(t4[3], SF("am"), lim))
        sync()
        do(tt(t4[0], t4[0], t4[1], ALU.add))
        do(tt(t4[2], t4[2], t4[3], ALU.subtract))
        sync()
        do(tt(SF("f_re"), t4[0], SF("den")))
        do(tt(SF("f_im"), t4[2], SF("den")))
        sync()
        dve.wait_ge(s_bc, 32)
        dve.wait_ge(s_ust, 64)
        rt = [RT[:, i, 0:2, :].rearrange("p a b -> p (a b)").rearrange("p (a h) -> p a h", h=16) for i in range(4)]
        cmul(BC[:, 0, :, :], BC[:, 1, :, :], BC[:, 0, :, :], BC[:, 1, :, :],
             bc(SF("f_re").unsqueeze(2), [P, NP, 16]), bc(SF("f_im").unsqueeze(2), [P, NP, 16]), rt)
        do(ts(BC[:, 3, :, :], BC[:, 3, :, :], -1.0, ALU.mult))
        sync()
        s4 = [P, NP, SUB, 16]
        tmp = KT[:, 0:NP, :, :].rearrange("p a b c -> p (a b c)").rearrange("p (a b c) -> p a b c", a=NP, b=SUB)
        v4 = lambda a: a.rearrange("p a (b c) -> p a b c", b=SUB)
        pw = lambda a: bc(a.unsqueeze(3), s4)
        xw = lambda a: bc(a.unsqueeze(2), s4)
        pdr, pdi = pw(PWD[:, 0, :, :]), pw(PWD[:, 1, :, :])
        par, pai = pw(PWA[:, 0, :, 1:9]), pw(PWA[:, 1, :, 1:9])
        b_re, b_im, c_re, nc_im = (xw(BC[:, i, :, :]) for i in range(4))

        def combine(dst, a, x, b, y, op):
            do(tt(v4(dst[:]), a, x))
            do(tt(tmp, b, y))
            sync()
            do(tt(v4(dst[:]), v4(dst[:]), tmp, op))
            sync()

        combine(W_re, pdr, b_re, pdi, b_im, ALU.subtract)
        combine(W_im, pdr, b_im, pdi, b_re, ALU.add)
        dve.sem_inc(w_ok, 1)
        combine(OFF_re, c_re, par, nc_im, pai, ALU.add)
        combine(OFF_im, nc_im, par, c_re, pai, ALU.subtract)
        dve.sem_inc(off_ok, 1)

        def sq(o_re, o_im, re, im):
            cmul(o_re, o_im, re, im, re, im, t4)
            unit(o_re, o_im)

        sq(SF("q_re"), SF("q_im"), SF("cos"), SF("sin"))
        sq(SF("q2_re"), SF("q2_im"), SF("q_re"), SF("q_im"))
        sq(SF("up_re0"), SF("up_im0"), SF("q2_re"), SF("q2_im"))
        for lv in range(6):
            sq(SF(f"up_re{lv + 1}"), SF(f"up_im{lv + 1}"), SF(f"up_re{lv}"), SF(f"up_im{lv}"))
        for a, b in (("mag2", "mag"), ("mag4", "mag2"), ("mag8", "mag4")):
            do(tt(SF(a), SF(b), SF(b)))
            sync()

        s3 = [P, NP, NSEQ]
        t3 = [TS4[:, i, :, :] for i in range(4)]
        a4 = [bc(PWA[:, i, :, 4:5], s3) for i in range(2)]
        cmul(FINS[:, 0, :, :], FINS[:, 1, :, :], S0[:, 0, :, :], S0[:, 1, :, :], a4[0], a4[1], t3)
        dve.wait_ge(tap_mm, 1)
        dve.wait_ge(stt_mm, 8)
        nc.vector.memset(KTS[:], 0.0).then_inc(kt_zero, 1)
        dve.wait_ge(s_kt, 7 * 16)
        nc.vector.tensor_copy(KT[:].rearrange("p g t h -> p t g h"), KTS[:]).then_inc(kt_ok, 1)
        dve.wait_ge(kt_ok, 1)
        fins_done = [False]

        for b in range(4):
            pr0 = 4 * b
            rot = [ROT[:, i, :, :] for i in range(2)]
            if b == 0:
                do(nc.vector.memset(ROT[:, 0, :, 0:1], 1.0))
                do(nc.vector.memset(ROT[:, 1, :, 0:1], 0.0))
                sync()
            k = 1
            for lv in range(7):
                cmul(rot[0][:, :, k:2 * k], rot[1][:, :, k:2 * k], rot[0][:, :, 0:k], rot[1][:, :, 0:k],
                     bc(SF(f"up_re{lv}")[:, pr0:pr0 + 4].unsqueeze(2), [P, 4, k]),
                     bc(SF(f"up_im{lv}")[:, pr0:pr0 + 4].unsqueeze(2), [P, 4, k]),
                     [RT[:, i, :, 0:k] for i in range(4)])
                k *= 2
            if not fins_done[0]:
                dve.wait_ge(sb_mm, 1)
                tt(FINS[:].rearrange("p i a b -> p (i a b)"), FINS[:].rearrange("p i a b -> p (i a b)"),
                   bank[7][:, 0:2 * NP * NSEQ], ALU.add).then_inc(fin_ok, 1)
                fins_done[0] = True
            dve.wait_ge(st_mm, b + 1)
            s_re = bank[3].rearrange("p (a c) -> p a c", a=4)
            s_im = bank[4].rearrange("p (a c) -> p a c", a=4)
            do(tt(RT[:, 0], s_re, rot[0]))
            do(tt(RT[:, 1], s_im, rot[1]))
            do(tt(RT[:, 2], s_im, rot[0]))
            do(tt(RT[:, 3], s_re, rot[1]))
            sync()
            do(tt(KI[:, 0], RT[:, 0], RT[:, 1], ALU.add))
            tt(KI[:, 1], RT[:, 2], RT[:, 3], ALU.subtract).then_inc(ki_ok, 1)
            dve.wait_ge(ki_ok, b + 1)
            sync()
            for j in range(4):
                for i in range(2):
                    do(nc.vector.tensor_tensor_scan(KSC[:, i, j, :], bc(SF("mag8")[:, pr0 + j:pr0 + j + 1], [P, CH]),
                                                    KI[:, i, j, :], 0.0, ALU.mult, ALU.add))
            sync()
            do(tt(RT[:, 0], KSC[:, 0], rot[0]))
            do(tt(RT[:, 1], KSC[:, 1], rot[1]))
            do(tt(RT[:, 2], KSC[:, 0], rot[1]))
            do(tt(RT[:, 3], KSC[:, 1], rot[0]))
            if b >= 1:
                dve.wait_ge(y_mm, 4 * b)
            sync()
            do(tt(HST[:, 0, :, 1:CH], RT[:, 0, :, 0:CH - 1], RT[:, 1, :, 0:CH - 1], ALU.subtract))
            do(tt(HST[:, 1, :, 1:CH], RT[:, 2, :, 0:CH - 1], RT[:, 3, :, 0:CH - 1], ALU.add))
            do(nc.vector.tensor_copy(HST[:, :, :, CH + 1:YC], S0[:, :, pr0:pr0 + 4, :]))
            do(tt(FIN[:, 0, pr0:pr0 + 4], RT[:, 0, :, CH - 1], RT[:, 1, :, CH - 1], ALU.subtract))
            tt(FIN[:, 1, pr0:pr0 + 4], RT[:, 2, :, CH - 1], RT[:, 3, :, CH - 1], ALU.add).then_inc(fin_ok, 1)
            dve.wait_ge(fin_ok, b + 2)
            sync()
            dve.sem_inc(hst_ok, 1)
            for j in range(4):
                pr = pr0 + j
                dve.wait_ge(y_mm, pr + 1)
                for e in range(2):
                    g = 2 * pr + e
                    last = stt(U[:, g, 0:YC], U[:, g, 0:YC], prm("s5_d", g, 1), bank[5 + pr % 2][:, 256 * e:256 * e + YC],
                               ALU.mult, ALU.add)
                last.then_inc(y_ev, 1)

        for j in range(4):
            dve.wait_ge(gg_hi, j + 1)
            tt(as_blocks(GGL[:, j, :], NBLK), as_steps(GF[:, j, :], 0, NBLK),
               as_blocks(GGH[:, j, :].bitcast(F32), NBLK), ALU.subtract)
            tt(GGL[:, j, SEQ:T], GF[:, j, SEQ:T], GGH[:, j, SEQ:T].bitcast(F32), ALU.subtract).then_inc(gg_lo, 1)
        for i in range(4):
            no = TILE0["glu"] + 2 * i
            for n, (c0, w) in enumerate(CHUNKS):
                dve.wait_ge(acc_done[n], no + 2)
                dve.wait_ge(acc_free[n], no + 1)
                tt(PU[:, i, c0:c0 + w], GLT[:, n, 0:w], acc[n][:, 0:w]).then_inc(acc_free[n], 1)

        do(ts(CW[:], PRM[:, PCOL["conv_w"][0]:PCOL["conv_w"][0] + 30], 0.5, ALU.mult))
        sync()
        dve.wait_ge(s_scv, 16)
        for i in range(6):
            for n in range(3):
                dve.wait_ge(acc_free[n], TILE0["proj"] + i + 1)
            if i >= 2:
                dve.wait_ge(xbc_ok, i - 1)
            cv = CV[:, i % 2, :]
            x = PX[:, i, :]
            do(nc.vector.tensor_copy(CST[:, i, :], blk(x, NBLK - 1).rearrange("p (s c) -> p s c", s=SUB)[:, SUB - 3:SUB, CB - 1]))
            do(nc.vector.tensor_copy(CSS[:, i, :], x[:, SEQ + NSEQ:T]))
            do(ts(cv, x, CW[:, 4 * i + 3:4 * i + 4], ALU.mult, CW[:, 24 + i:25 + i], ALU.add))
            sync()
            cvp, xp = as_blocks(cv, NBLK), as_blocks(x, NBLK)
            scv = SCV[:, i, :, :].rearrange("p k b -> p (k b)")
            for d in range(1, 4):
                w = CW[:, 4 * i + 3 - d:4 * i + 4 - d]
                do(stt(cvp[:, :, d:, :], xp[:, :, 0:SUB - d, :], w, cvp[:, :, d:, :], ALU.mult, ALU.add))
                for s in range(d):
                    do(stt(cvp[:, :, s, 1:], xp[:, :, SUB - d + s, 0:CB - 1], w, cvp[:, :, s, 1:], ALU.mult, ALU.add))
                do(stt(cvp[:, 1:, 0:d, 0], xp[:, 0:NBLK - 1, SUB - d:, CB - 1], w, cvp[:, 1:, 0:d, 0], ALU.mult, ALU.add))
                o = SEQ + d * NSEQ
                do(stt(cv[:, o:T], x[:, SEQ:T - d * NSEQ], w, cv[:, o:T], ALU.mult, ALU.add))
                last = stt(cv[:, SEQ:o], scv[:, (3 - d) * NSEQ:3 * NSEQ], w, cv[:, SEQ:o], ALU.mult, ALU.add)
                if d < 3:
                    do(last)
                    sync()
                else:
                    last.then_inc(conv_last, 1)
            dve.wait_ge(conv_last, i + 1)
            sync()
            dve.sem_inc(conv_ok, 1)
            if i == 5:
                dve.sem_inc(cst_ok, 1)
            if i == 1:
                softplus_and_cumsum(dve, do, sync, tt, ts, stt)
            if i >= 1:
                conv_finish(dve, stt, i - 1)
        conv_finish(dve, stt, 5)
        dve.wait_ge(xbc_ok, 6)

        for n in range(1):
            dve.wait_ge(nac_mm, 1)
            do(nc.vector.tensor_copy(DTT[:, 7, 0:8, :], bank[4][:, 0:64].rearrange("p (a b) -> p a b", b=8)))
            nc.vector.tensor_copy(DTT[0:SMP, 7, 8, :], bank[4][0:SMP, 64:72]).then_inc(nac_ok, 1)
        dve.wait_ge(s_out, 16 * 6)
        nc.vector.memset(HS[:, 0, :, :], 0.0).then_inc(h_ok, 1)
        dve.wait_ge(s_h0, 16)
        for n in range(NBLK + 1):
            smp = n == NBLK
            rows = SMP if smp else P
            if n >= 1:
                dve.wait_ge(yd_mm, n)
                if n >= 2:
                    dve.wait_ge(ss_mm, n - 1)
            dve.wait_ge(tr_mm, n + 1)
            tt(XS[0:rows].rearrange("p (h d) -> p h d", d=HD), bank[3][0:rows].rearrange("p (h d) -> p h d", d=HD),
               bc(DTT[0:rows, 5, n, :].unsqueeze(2), [rows, 8, HD])).then_inc(xs_ok, 1)
            dve.wait_ge(et_ok, n + 1)
            c = PX[:, 5, SEQ:T] if smp else blk(PX[:, 5, :], n)
            etf, cdf = ET[:].rearrange("p a b -> p (a b)"), CD[:].rearrange("p a b -> p (a b)")
            if smp:
                tt(cdf[:, 0:4 * SMP].rearrange("p (k q) -> p k q", k=4), etf[:, 0:4 * SMP].rearrange("p (k q) -> p k q", k=4),
                   bc(c.unsqueeze(1), [P, 4, SMP])).then_inc(cd_ok, 1)
            else:
                tt(CD[:], ET[:], bc(c.unsqueeze(1), [P, 4, P])).then_inc(cd_ok, 1)
            dve.wait_ge(l_ok, n + 1)
            if smp:
                do(nc.vector.tensor_reduce(DE[0:SMP, :], LS[:, 0, :, SMP - NSEQ:SMP], AX.X, ALU.add))
            else:
                do(nc.vector.tensor_copy(DE[:], L[:, :, P - 1]))
            sync()
            dve.wait_ge(xs_ok, n + 1)
            dve.wait_ge(cb_mm, n + 1)
            if n >= 1:
                dve.wait_ge(ss_mm, n)
            tt(XD[0:rows].rearrange("p (h d) -> p h d", d=HD), XS[0:rows].rearrange("p (h d) -> p h d", d=HD),
               bc(DE[0:rows, :].unsqueeze(2), [rows, 8, HD])).then_inc(xd_ok, 1)
            for g in range(2):
                cbt = bank[4][0:rows, P + 128 * g:P + 128 * g + rows]
                if smp:
                    last = tt(LS[:, 1, 4 * g:4 * g + 4, :], LS[:, 0, 4 * g:4 * g + 4, :],
                              bc(cbt.unsqueeze(1), [rows, 4, rows]))
                else:
                    last = tt(L[:, 4 * g:4 * g + 4, :], L[:, 4 * g:4 * g + 4, :], bc(cbt.unsqueeze(1), [P, 4, P]))
                do(last)
            sync()
            dve.sem_inc(mm_ok, 1)
            if not smp:
                hp, hn = HS[:, n % 2, :, :], HS[:, (n + 1) % 2, :, :]
                do(tt(hn, hp, bc(ET[:, :, P - 1:P], [P, 4, HD])))
                sync()
                dve.wait_ge(ss_mm, n + 1)
                tt(hn, hn, bank[3][:, 0:256].rearrange("p (k d) -> p k d", d=HD), ALU.add).then_inc(h_ok, 1)
            dve.wait_ge(yd_mm, n + 1)
            for i in range(4):
                xi = PX[:, i, SEQ:T] if smp else blk(PX[:, i, :], n)
                yi = bank[7][:, i * P:i * P + rows]
                last = stt(xi, xi, prm("ssd_d", i, 1), yi, ALU.mult, ALU.add)
            last.then_inc(ye_ok, 1)
        for half in range(2):
            if half == 1:
                dve.wait_ge(ss_mm, NBLK + 4)
            else:
                dve.wait_ge(bt_ok, NBLK + 1)
            tt(BTM, bc(BT[0:SMP, :].unsqueeze(1), [SMP, 4, P]),
               bc(prm("seqmask", 4 * half, 4)[0:SMP, :].unsqueeze(2), [SMP, 4, P])).then_inc(btm_ok, 1)
            for b in range(4 * half, 4 * half + 4):
                etf = ET[:].rearrange("p a b -> p (a b)")[:, 0:4 * SMP].rearrange("p (k q) -> p k q", k=4)
                do(tt(H0[:, b, :, :], H0[:, b, :, :], bc(etf[:, :, SMP - NSEQ + b:SMP - NSEQ + b + 1], [P, 4, HD])))
                sync()
                dve.wait_ge(ss_mm, NBLK + b + 1)
                tt(H0[:, b, :, :], H0[:, b, :, :], bank[(3, 4)[b % 2]][:, 0:256].rearrange("p (k d) -> p k d", d=HD),
                   ALU.add).then_inc(h_ok, 1)
        for k in range(4):
            zt = ZT[:, k % 2, :]
            dve.wait_ge(zt_ok, k + 1)
            do(stt(zt, zt, 1.0, PX[:, 8 + k, :], ALU.add, ALU.mult))
            sync()
            stt(PX[:, k, :], PX[:, k, :], 0.5, zt, ALU.mult, ALU.mult).then_inc(ya_ok, 1)
        norm_sum_dve(1)
        dve.wait_ge(rs_ok, 6)
        for k in range(4):
            stt(PX[:, k, :], PX[:, k, :], prm("ssd_norm", k, 1), ZR[:], ALU.mult, ALU.mult).then_inc(yn_ok, 1)

        dve.wait_ge(s_ks, 16)
        nc.vector.tensor_copy(KS[:, :, P:P + DSEQ],
                              PX[:, 6, SEQ:T].rearrange("p (t b) -> p b t", b=NSEQ)).then_inc(ks_ok, 1)
        for d in range(2):
            for i in range(4):
                last = nc.vector.tensor_copy(QS[:, :, 16 * d + 4 * i:16 * d + 4 * i + 4],
                                             PU[:, 4 + i, SEQ:T].rearrange("p (t b) -> p b t", b=NSEQ))
        last.then_inc(ks_ok, 1)
        dve.wait_ge(s_bias, 24 * 16)

        def maxima(a):
            smp = a == 2 * NBLK
            n, kv = divmod(a, 2)
            z = SB[:, a % 2, :, :]
            w = P + DSEQ if smp else 2 * P
            if a >= 2:
                dve.wait_ge(tp_mm, a - 1)
            if n == 0:
                do(nc.vector.memset(z, NEG))
                sync()
            dve.wait_ge(at_s, a + 1)
            for j in range(2):
                ps = bank[3 + j].rearrange("p (i w) -> p i w", i=2)
                if smp:
                    last = stt(z[:, 2 * j:2 * j + 2, 0:w], ps[:, :, 0:w], HD ** -0.5, BIASS[:], ALU.mult, ALU.add)
                elif n == 0:
                    v = lambda x: x[:, :, P:]
                    last = stt(v(z[:, 2 * j:2 * j + 2, :]), v(ps), HD ** -0.5, v(BIAS[:, 4 * kv + 2 * j:4 * kv + 2 * j + 2, :]),
                               ALU.mult, ALU.add)
                else:
                    last = stt(z[:, 2 * j:2 * j + 2, :], ps, HD ** -0.5, BIAS[:, 4 * kv + 2 * j:4 * kv + 2 * j + 2, :],
                               ALU.mult, ALU.add)
                do(last)
            sync()
            dve.sem_inc(sb_rd, 1)
            sink = prm("sinks_s") if smp else prm("sinks", 4 * kv, 4)
            m = SM[:, a % 2, :, :]
            do(nc.vector.tensor_reduce(m[:, 0, :], z[:, :, 0:w], AX.X, ALU.max))
            sync()
            do(tt(m[:, 0, :], m[:, 0, :], sink, ALU.max))
            sync()
            do(ts(m[:, 1, :], m[:, 0, :], -1.0, ALU.mult))
            do(tt(m[:, 2, :], sink, m[:, 0, :], ALU.subtract))
            sync()
            dve.sem_inc(sm_ok, 1)

        def probs(a):
            m = SM[:, a % 2, :, :]
            w = P + DSEQ if a == 2 * NBLK else 2 * P
            dve.wait_ge(ex_ok, a + 1)
            do(tt(m[:, 5, :], m[:, 3, :], m[:, 4, :], ALU.add))
            sync()
            do(nc.vector.reciprocal(m[:, 5, :], m[:, 5, :]))
            sync()
            z = SB[:, a % 2, :, 0:w]
            tt(z, z, bc(m[:, 5, :].unsqueeze(2), [P, 4, w])).then_inc(p_ok, 1)

        maxima(0)
        for a in range(2 * NBLK):
            if a + 1 <= 2 * NBLK - 1:
                maxima(a + 1)
            probs(a)
        maxima(2 * NBLK)
        probs(2 * NBLK)

        def y_low(q):
            for j in range(4):
                src = [PU[:, j, :], PX[:, j, :], PU[:, 4 + j, :]][q]
                k = (4, 0, 4)[q] + j
                dve.wait_ge(yh_hi, 4 * q + j + 1)
                tt(HL[:, k, :], src, HH[:, k, :].bitcast(F32), ALU.subtract).then_inc(yh_lo, 1)

        y_low(0)
        y_low(1)
        mt = [0]
        for q in range(3):
            for j in range(8):
                t = 8 * q + j
                no = TILE0["branch"] + t
                if t == 10:
                    y_low(2)
                dve.wait_ge(s_gt[t % 2], 16 * (t // 2 + 1))
                for n, (c0, w) in enumerate(CHUNKS):
                    dve.wait_ge(acc_done[n], no + 1)
                    if mt[0] >= 2:
                        dve.wait_ge(mix_ok, mt[0] - 1)
                    tmp2 = MT[:, mt[0] % 2, 0:w]
                    stt(tmp2, GTB[:, t % 2, c0:c0 + w], 1.0, acc[n][:, 0:w], ALU.add, ALU.mult).then_inc(acc_free[n], 1)
                    dve.wait_ge(acc_free[n], no + 1)
                    dst = y_dst(j)[:, c0:c0 + w]
                    if q == 0:
                        ts(dst, tmp2, 0.5, ALU.mult).then_inc(mix_ok, 1)
                    else:
                        dve.wait_ge(mix_ok, mt[0])
                        stt(dst, tmp2, 0.5, dst, ALU.mult, ALU.add).then_inc(mix_ok, 1)
                    mt[0] += 1
        i = 0
        for n, (c0, w) in enumerate(CHUNKS):
            for k in range(KD):
                i += 1
                dve.wait_ge(mx_hi, i)
                tt(HL[:, k, c0:c0 + w], y_dst(k)[:, c0:c0 + w], HH[:, k, c0:c0 + w].bitcast(F32),
                   ALU.subtract).then_inc(mx_lo, 1)

        def add_to_x1(stage):
            for k in range(KD):
                no = TILE0[stage] + k
                if stage == "out":
                    dve.wait_ge(s_x[k], 32)
                for n, (c0, w) in enumerate(CHUNKS):
                    dve.wait_ge(acc_done[n], no + 1)
                    tt(X1[:, k, c0:c0 + w], X1[:, k, c0:c0 + w], acc[n][:, 0:w], ALU.add).then_inc(acc_free[n], 1)

        add_to_x1("out")
        norm_sum_dve(2)
        norm_split_dve(2)

        ff = 0
        for p, nf in enumerate(FFN_PASSES):
            t0 = TILE0[f"up{p}"]
            for f in range(nf):
                no = t0 + 2 * f
                for n, (c0, w) in enumerate(CHUNKS):
                    dve.wait_ge(acc_done[n], no + 2)
                    dve.wait_ge(acc_free[n], no + 1)
                    if ff > 0:
                        dve.wait_ge(f_lo, 3 * ff - 2 + n)
                    tt(FM[:, n, 0:w], FS[:, n, 0:w], acc[n][:, 0:w]).then_inc(acc_free[n], 1)
                for n, (c0, w) in enumerate(CHUNKS):
                    dve.wait_ge(f_hi, 3 * ff + n + 1)
                    tt(FL[:, f, c0:c0 + w], FM[:, n, 0:w], FH[:, f, c0:c0 + w].bitcast(F32), ALU.subtract).then_inc(f_lo, 1)
                ff += 1
            add_to_x1(f"down{p}")
        norm_sum_dve(3)
        dve.wait_ge(rs_ok, 12)
        for k in range(KD):
            for n, (c0, w) in enumerate(CHUNKS):
                stt(X1[:, k, c0:c0 + w], X1[:, k, c0:c0 + w], prm("normf", k, 1), RS5[:, c0:c0 + w], ALU.mult,
                    ALU.mult).then_inc(y_ok, 1)

    top.close()


def kernel(**inputs):
    import numpy as _np
    import concourse.bacc as _bacc
    from concourse.bass_utils import run_bass_kernel_spmd as _run

    a = {k: _np.asarray(v) for k, v in inputs.items()}
    f32 = _np.float32

    def cols(x):
        p = x["p"].reshape(NBLK, CB, SUB, -1).transpose(0, 2, 1, 3).reshape(SEQ, -1)
        s = x["s"].reshape(NSEQ, DSEQ, -1).transpose(1, 0, 2).reshape(SMP, -1)
        return _np.concatenate([p, s], 0).T

    x = cols({"p": a["x_prompt"][0], "s": a["x_sample"]}).reshape(KD, P, T)

    w_in = a["w_in"][0]
    z0, xbc0, dt0, u0, q0, k0, v0, g0 = 0, 512, 1280, 1288, 1800, 2312, 2440, 2568

    def tiles(w, c0, n):
        k = w.shape[0] // P
        return w[:, c0:c0 + n * P].reshape(k, P, n, P).transpose(2, 1, 0, 3)

    def flat(t):
        return t.reshape(t.shape[0], P, -1)

    wdt = _np.zeros((D, P), f32)
    wdt[:, 0:8] = w_in[:, dt0:dt0 + 8]
    wq = w_in[:, q0:q0 + 512].reshape(D, 2, 4, 64).transpose(0, 2, 1, 3).reshape(D, 512)
    gates = flat(tiles(w_in, g0, 24))
    glu = tiles(a["s5_w_glu"][0], 0, 8)
    glu = _np.stack([_np.concatenate([glu[j + 4], glu[j]], 1) for j in range(4)])
    wc = a["w_br_c"][0].reshape(2, 4, 64, D).transpose(1, 0, 2, 3).reshape(512, D)
    branch = []
    for w in (a["w_br_b"][0], a["w_br_a"][0], wc):
        t = tiles(w, 0, 8)
        branch += [_np.concatenate([t[2 * i], t[2 * i + 1]], 1) for i in range(4)]
    up = tiles(a["w_ffn_up"][0], 0, 2 * KF)
    down = tiles(a["w_ffn_down"][0], 0, KD)
    units = [flat(tiles(w_in, u0, 4)), gates[0:12], flat(glu),
             flat(tiles(w_in, xbc0, 6)), flat(tiles(wdt, 0, 1)), flat(tiles(w_in, k0, 1)), flat(tiles(w_in, v0, 1)),
             flat(tiles(w_in, z0, 4)), flat(tiles(wq, 0, 4)), gates[12:24], flat(_np.stack(branch)),
             flat(tiles(a["w_out"][0], 0, 8))]
    f = 0
    for n in FFN_PASSES:
        for j in range(f, f + n):
            units += [flat(up[j:j + 1]), flat(up[KF + j:KF + j + 1])]
        d = _np.zeros((KD, P, 1024), f32)
        d[:, :, 0:n * P] = flat(down[:, :, f:f + n])
        units.append(d)
        f += n
    w = _np.concatenate(units, 0)
    assert w.shape == (UNITS, P, 1024), w.shape

    consts, hot = shape_constants()
    par = _np.zeros((P, NPAR), f32)

    def put(name, v):
        at, n = PCOL[name]
        v = _np.asarray(v)
        par[0:v.shape[0], at:at + n] = v

    def rows(v):
        return _np.broadcast_to(v, (P, v.shape[-1]))

    for name, v in consts.items():
        put(name, v)
    for name, key in (("norm1", "norm1_w"), ("norm2", "norm2_w"), ("normf", "final_norm_w"), ("ssd_norm", "ssd_norm_w")):
        put(name, a[key].reshape(-1, P).T)
    put("conv_w", a["conv_w"][0].reshape(4, 6, P).transpose(2, 1, 0).reshape(P, 24))
    put("conv_b", a["conv_b"][0].reshape(6, P).T)
    put("ssd_d", _np.repeat(a["ssd_d"][0], HD).reshape(4, P).T)
    put("a_log", rows(a["ssd_a_log"][0]))
    put("dt_bias", rows(a["ssd_dt_bias"][0]))
    put("sinks", rows(a["attn_sinks"][0]))
    sk = a["attn_sinks"][0].reshape(2, 4)
    sk = _np.broadcast_to(sk.T[None, None, :, None, None, :], (4, 2, 4, DSEQ, 2, 2)).reshape(P, 4)
    put("sinks_s", sk)
    put("s5_d", _np.tile(a["s5_d"][0].T, (SUB, 1)))

    def pairs(v):
        return v.reshape(16, 2, 64, *v.shape[2:]).transpose(1, 2, 0, *range(3, v.ndim + 1)).reshape(P, 16, *v.shape[2:])

    put("lam_re", pairs(a["s5_lam_re"][0]))
    put("lam_im", pairs(a["s5_lam_im"][0]))
    put("log_dt", pairs(_np.broadcast_to(a["s5_log_dt"][0][:, None], (32, 64))))
    bcm = _np.stack([pairs(a["s5_b_re"][0]), pairs(a["s5_b_im"][0]),
                     pairs(a["s5_c_re"][0].transpose(0, 2, 1)), pairs(a["s5_c_im"][0].transpose(0, 2, 1))], 1)
    s0 = _np.stack([pairs(a[k][0].transpose(1, 2, 0)) for k in ("state_s5_re", "state_s5_im")], 1)
    hotp = _np.zeros((P, BHALF), f32)
    hotp[0:33] = hot[:, 0:BHALF]
    hotp[64:97] = hot[:, BHALF:]
    rtab = _np.zeros((P, 8), f32)
    for r in (0, 64):
        rtab[r:r + 32] = a["rel_bias"]
        rtab[r + 32] = 1.0
    h0 = a["state_ssd"][0].reshape(NSEQ, 2, 4, 64, 64).transpose(1, 4, 0, 2, 3).reshape(P, NSEQ, 4, 64)
    scv = a["state_conv"][0].reshape(NSEQ, 3, 6, P).transpose(3, 2, 1, 0)
    ks = a["cache_k"][0].reshape(NSEQ, P, P).transpose(2, 0, 1)
    vc = a["cache_v"][0].reshape(NSEQ, P, P).transpose(1, 0, 2)

    ins = {"params": par, "x": x, "w": w, "hot": hotp, "rtab": rtab, "bc": bcm, "s0": s0, "h0": h0, "scv": scv,
           "ks": ks, "vc": vc}
    outs = {"y": (KD, P, T), "ssd_p": (P, 4, HD), "conv_p": (P, 6, 3), "conv_s": (P, 6, 24), "s5p": (P, 2, 16),
            "s5s": (P, 2, 16, NSEQ), "kp": (P, P), "vp": (P, P), "ssd_s": (P, NSEQ, 4, HD),
            "kns": (P, NSEQ, P), "vns": (P, NSEQ, P)}
    nc = _bacc.Bacc("TRN2", target_bir_lowering=False, num_devices=1)
    io, arrays = {}, {}
    for name, v in ins.items():
        arrays["in_" + name] = _np.ascontiguousarray(v, dtype=f32)
        io[name] = nc.dram_tensor("in_" + name, v.shape, F32, kind="ExternalInput").ap()
    for name, shape in outs.items():
        io[name] = nc.dram_tensor("out_" + name, shape, F32, kind="ExternalOutput").ap()
    build(nc, io)
    res = _run(nc, [arrays], core_ids=[0]).results[0]
    o = {name: _np.asarray(res["out_" + name]) for name in outs}

    y = o["y"].reshape(D, T)
    y_p = y[:, 0:SEQ].reshape(D, NBLK, SUB, CB).transpose(1, 3, 2, 0).reshape(1, SEQ, D)
    y_s = y[:, SEQ:].reshape(D, DSEQ, NSEQ).transpose(2, 1, 0)
    ssd_p = o["ssd_p"].reshape(2, 64, 4, 64).transpose(0, 2, 3, 1).reshape(1, 1, 8, 64, 64)
    conv_p = o["conv_p"].transpose(2, 1, 0).reshape(1, 1, 3, 768)
    s5 = o["s5p"].reshape(2, 64, 2, 16).transpose(2, 3, 0, 1).reshape(2, 1, 1, 32, 64)

    def last_block(t):
        return t.reshape(2, 64, SUB, CB).transpose(3, 2, 0, 1).reshape(1, 1, P, 2, 64)

    ssd_s = o["ssd_s"].reshape(2, 64, NSEQ, 4, 64).transpose(2, 0, 3, 4, 1).reshape(1, NSEQ, 8, 64, 64)
    conv_s = o["conv_s"].reshape(P, 6, 3, NSEQ).transpose(3, 2, 1, 0).reshape(1, NSEQ, 3, 768)
    s5s = o["s5s"].reshape(2, 64, 2, 16, NSEQ).transpose(2, 4, 3, 0, 1).reshape(2, 1, NSEQ, 32, 64)
    k_s = o["kns"].reshape(2, 64, NSEQ, P).transpose(2, 3, 0, 1).reshape(1, NSEQ, P, 2, 64)
    v_s = o["vns"].reshape(P, NSEQ, 2, 64).transpose(1, 0, 2, 3).reshape(1, NSEQ, P, 2, 64)
    c = _np.ascontiguousarray
    return tuple(c(t) for t in (y_p, y_s, ssd_p, conv_p, s5[0], s5[1], last_block(o["kp"]), last_block(o["vp"]),
                                ssd_s, conv_s, s5s[0], s5s[1], k_s, v_s))
```

```python
from contextlib import ExitStack
import math

import numpy as np

import concourse.bass as bass
from concourse import mybir

F32 = mybir.dt.float32
F32R = mybir.dt.float32r
BF16 = mybir.dt.bfloat16
ACT = mybir.ActivationFunctionType
ALU = mybir.AluOpType
AX = mybir.AxisListType

P = 128
D = 1024
SEQ = 1024
NSEQ, DSEQ = 8, 4
SMP = NSEQ * DSEQ
T = SEQ + SMP
KD = D // P
NBLK = SEQ // P
SUB = 8
CH = SEQ // SUB
CB = P // SUB
HD = 64
DFF = 2816
KF = DFF // P
EPS = 1e-6
CHUNKS = [(0, 384), (384, 384), (768, T - 768)]
NEG = -1e30
NBUCKET = 32

FFN_PASSES = [6, 6, 5, 5]
STAGES = [("u", 4, 1), ("gates1", 12, 1), ("glu", 4, 2), ("proj", 17, 1), ("gates2", 12, 1),
          ("branch", 12, 2), ("out", 8, 1)]
for _i, _n in enumerate(FFN_PASSES):
    STAGES += [(f"up{_i}", 2 * _n, 1), (f"down{_i}", 8, 1)]
UNIT0, TILE0, TILE_END = {}, {}, []
_u = _m = 0
for _name, _n, _per in STAGES:
    UNIT0[_name], TILE0[_name] = _u, _m
    for _ in range(_n):
        _m += _per
        _u += 1
        TILE_END.append(_m)
UNITS = _u

BW_P = CB * (2 * SUB - 1) * 2 * CB
BW_S = DSEQ * (P + DSEQ)
BW = BW_P + BW_S
BHALF = BW // 2
BSTEP = BHALF // 9


def buckets(dist):
    n = np.maximum(dist, 0)
    exact = NBUCKET // 2
    nf = np.maximum(n, 1).astype(np.float32)
    large = exact + (np.log(nf / np.float32(exact)) / np.float32(math.log(128 / exact))
                     * np.float32(NBUCKET - exact)).astype(np.int32)
    return np.where(n < exact, n, np.minimum(large, NBUCKET - 1))


PCOL = {}


def _fields():
    at = 0
    for name, n in [("ident", 128), ("tri", 128), ("negtri", 128), ("ones", 128), ("mask", 128),
                    ("tri_s", 32), ("negtri_s", 32), ("mask_s", 32), ("seqmask", 8), ("eps", 1),
                    ("norm1", 8), ("norm2", 8), ("normf", 8), ("conv_w", 24), ("conv_b", 6),
                    ("ssd_norm", 4), ("ssd_d", 4), ("a_log", 8), ("dt_bias", 8), ("sinks", 8),
                    ("sinks_s", 4), ("s5_d", 32), ("lam_re", 16), ("lam_im", 16), ("log_dt", 16)]:
        PCOL[name] = (at, n)
        at += n
    return at


NPAR = _fields()


def shape_constants():
    j = np.arange(P)
    real = SUB * (j % CB) + j // CB
    js = np.arange(SMP)
    ts, bs = js // NSEQ, js % NSEQ
    c = {}
    c["ident"] = np.eye(P)
    c["tri"] = (real[:, None] <= real[None, :]).astype(np.float64)
    c["negtri"] = -c["tri"]
    c["ones"] = np.ones((P, P))
    c["mask"] = np.where(c["tri"] > 0, 0.0, NEG)
    tri_s = ((bs[:, None] == bs[None, :]) & (ts[:, None] <= ts[None, :])).astype(np.float64)
    c["tri_s"], c["negtri_s"], c["mask_s"] = tri_s, -tri_s, np.where(tri_s > 0, 0.0, NEG)
    c["seqmask"] = (bs[:, None] == np.arange(NSEQ)[None, :]).astype(np.float64)
    c["eps"] = np.full((P, 1), EPS)
    cq = np.arange(CB)[:, None, None]
    dl = np.arange(2 * SUB - 1)[None, :, None]
    half, ck = np.arange(2)[None, :, None, None], np.arange(CB)[None, None, None, :]
    cq, dl = cq[..., None], dl[:, None, :, :].transpose(0, 1, 2, 3)
    dist_p = (SUB * (cq - ck) + P * (1 - half) + (SUB - 1) - dl).reshape(-1)
    t = np.arange(DSEQ)[:, None]
    k = np.arange(P + DSEQ)[None, :]
    dist_s = (P + t - k).reshape(-1)
    dist = np.concatenate([dist_p, dist_s])
    ok = (dist >= 0) & (dist < P)
    hot = np.zeros((NBUCKET + 1, BW), np.float32)
    hot[buckets(dist), np.arange(BW)] = ok
    hot[NBUCKET] = np.where(ok, 0.0, NEG)
    return c, hot


def build(nc, io):
    NG = 32
    NP = NG // 2
    UC = CH + 1 + 2 * NSEQ
    YC = CH + 1 + NSEQ

    top = ExitStack()
    ps_all = top.enter_context(nc.psum_tensor("ps", [P, 8, 512], F32))
    acc = [ps_all[:, n, :] for n in range(3)]
    bank = [ps_all[:, n, :] for n in range(8)]

    def sb(stack, name, shape, dt=F32):
        return stack.enter_context(nc.sbuf_tensor(name, shape, dt))

    def sem(name):
        return top.enter_context(nc.semaphore(name))

    HH = sb(top, "HH", [P, KD, T], F32R)
    HL = sb(top, "HL", [P, KD, T], F32R)
    WRAW = sb(top, "WRAW", [P, 2, 1024])
    WH = sb(top, "WH", [P, 2, 1024], F32R)
    WL = sb(top, "WL", [P, 2, 1024], F32R)
    GT = sb(top, "GT", [P, T])
    PRM = sb(top, "PRM", [P, NPAR])
    IDB = sb(top, "IDB", [P, P], BF16)
    MASKB = sb(top, "MASKB", [P, P], BF16)
    MASKSB = sb(top, "MASKSB", [SMP, SMP], BF16)
    ZERO = sb(top, "ZERO", [P, 1])
    RC = sb(top, "RC", [P, NBLK + 1])

    def prm(name, a=0, n=None):
        at, width = PCOL[name]
        return PRM[:, at + a:at + (width if n is None else a + n)]

    IDENT = prm("ident")

    ps5 = ExitStack()
    SP_ = sb(ps5, "SP", [P, 40, NG // 2])
    p0 = ExitStack()
    X0 = sb(p0, "X0", [P, KD, T])
    SQ = sb(p0, "SQ", [P, 2, T])
    ACC = sb(p0, "ACC", [P, T])
    RS = sb(p0, "RS", [P, T])
    HF0 = sb(p0, "HF", [P, 2, 384])
    HF = [HF0[:, n, :] for n in range(2)]
    HOT = sb(p0, "HOT", [P, BHALF])
    BTAB = sb(p0, "BTAB", [P, BHALF])
    RTAB = sb(p0, "RTAB", [P, 8])
    p0.close()
    p1 = ExitStack()
    sb(p1, "padUF", [P, 4 * NP * P])
    UF = sb(p1, "UF", [P, 4, T])
    p1.close()
    p1 = ExitStack()
    W_re = sb(p1, "W_re", [P, NP, P])
    W_im = sb(p1, "W_im", [P, NP, P])
    OFF_re = sb(p1, "OFF_re", [P, NP, P])
    OFF_im = sb(p1, "OFF_im", [P, NP, P])
    STT = sb(p1, "STT", [P, 2, NP, P])
    KT = sb(p1, "KT", [P, NG, SUB, 16])
    U = sb(p1, "U", [P, NG, UC])
    ROT = sb(p1, "ROT", [P, 2, 4, CH])
    CDG = sb(p1, "CDG", [P, 2, NP, 2, 16])
    BC = sb(p1, "BC", [P, 4, NP, 16])
    PWA = sb(p1, "PWA", [P, 2, NP, 9])
    PWD = sb(p1, "PWD", [P, 2, NP, 8])
    HST = sb(p1, "HST", [P, 2, 4, YC])
    S0 = sb(p1, "S0", [P, 2, NP, NSEQ])
    FIN = sb(p1, "FIN", [P, 2, NP])
    FINS = sb(p1, "FINS", [P, 2, NP, NSEQ])
    TS4 = sb(p1, "TS4", [P, 4, NP, NSEQ])
    p1.close()
    p1 = ExitStack()
    KTS = sb(p1, "KTS", [P, SUB, NG, 16])
    p1.close()
    p1 = ExitStack()
    RT = sb(p1, "RT", [P, 4, 4, CH])
    KI = sb(p1, "KI", [P, 2, 4, CH])
    KSC = sb(p1, "KSC", [P, 2, 4, CH])
    p1.close()
    ps5.close()
    p2 = ExitStack()
    PU = sb(p2, "PU", [P, 8, T])
    PX = sb(p2, "PX", [P, 12, T])
    pc = ExitStack()
    pdt = ExitStack()
    DTT = sb(pdt, "DTT", [P, 10, 9, 8])
    ZB = [DTT[:, 0:4].rearrange("p a b c -> p (a b c)")[:, 0:2 * P].rearrange("p (a c) -> p a c", a=2)]
    CV = sb(pc, "CV", [P, 2, T])
    TH = sb(pc, "TH", [P, 2, T])
    DTF = sb(pc, "DTF", [P, T])
    SCV = sb(pc, "SCV", [P, 6, 3, NSEQ])
    CST = sb(pc, "CST", [P, 6, 3])
    CSS = sb(pc, "CSS", [P, 6, 24])
    CW = sb(pc, "CW", [P, 30])
    pc.close()
    pd = ExitStack()
    XS = sb(pd, "XS", [P, 512])
    BT = sb(pd, "BT", [P, P])
    ET = sb(pd, "ET", [P, 4, P])
    L = sb(pd, "L", [P, 8, P])
    CD = sb(pd, "CD", [P, 4, P])
    XD = sb(pd, "XD", [P, 512])
    DE = sb(pd, "DE", [P, 8])
    HS = sb(pd, "HS", [P, 2, 4, HD])
    H0 = sb(pd, "H0", [P, NSEQ, 4, HD])
    ZB.append(sb(pd, "ZB", [P, 2, P]))
    pd.close()
    pz = ExitStack()
    ZQ = sb(pz, "ZQ", [P, T])
    ZA = sb(pz, "ZA", [P, T])
    ZR = sb(pz, "ZR", [P, T])
    pz.close()
    pdt.close()
    pt = ExitStack()
    BIAS = sb(pt, "BIAS", [P, 8, 2 * P])
    BIASS = sb(pt, "BIASS", [P, 2, P + DSEQ])
    SB = sb(pt, "SB", [P, 2, 4, 2 * P])
    PT = sb(pt, "PT", [P, 2, 512])
    KS = sb(pt, "KS", [P, NSEQ, P + DSEQ])
    QS = sb(pt, "QS", [P, NSEQ, 32])
    SM = sb(pt, "SM", [P, 2, 6, 4])
    pt.close()
    GTB = PX[:, 8:10, :]
    MT = PX[:, 10, 0:2 * 384].rearrange("p (a c) -> p a c", a=2)
    VC = PX[:, 11, 0:NSEQ * P].rearrange("p (s d) -> p s d", s=NSEQ)
    VN = GT[0:DSEQ, 0:NSEQ * P]
    p2.close()
    p2 = ExitStack()
    sb(p2, "padPU", [P, 8, T])
    GF = sb(p2, "GF", [P, 4, T])
    GGH = sb(p2, "GGH", [P, 4, T], F32R)
    GGL = sb(p2, "GGL", [P, 4, T], F32R)
    GLT = sb(p2, "GLT", [P, 3, 384])
    p2.close()
    p5 = ExitStack()
    FH = sb(p5, "FH", [P, 6, T], F32R)
    FL = sb(p5, "FL", [P, 6, T], F32R)
    X1 = sb(p5, "X1", [P, KD, T])
    FS = sb(p5, "FS", [P, 3, 384])
    FM = sb(p5, "FM", [P, 3, 384])
    SQ5 = sb(p5, "SQ5", [P, T])
    AC5 = sb(p5, "AC5", [P, T])
    RS5 = sb(p5, "RS5", [P, T])
    HF5 = [FS[:, n, :] for n in range(3)] + [FM[:, n, :] for n in range(3)]
    p5.close()

    def dma_sem(name):
        return sem("dma_" + name)
    w_hi, et_half, vn_half = sem("w_high"), sem("exp_acum_half"), sem("v_new_half")
    kt_ok = sem("kt_ready")
    red_pre, conv_last, yn_ok = sem("s5_angle_clamped"), sem("conv_last_tap"), sem("y_a_normed")
    bsscr = nc.dram_tensor("bias_s_scratch", (8, BW_S), F32, kind="Internal").ap()
    N_OUT_TOTAL = 11 + KD
    LF = L[0:SMP, :, :].rearrange("p a b -> p (a b)")
    LS = LF[:, 0:512].rearrange("p (i h q) -> p i h q", i=2, h=8)
    BTM = LF[:, 512:1024].rearrange("p (b d) -> p b d", b=4)
    SFN = {}

    def SF(name):
        return SP_[:, SFN.setdefault(name, len(SFN)), :]

    def conv_finish(dve, stt, i):
        dve.wait_ge(th_ok, i + 1)
        stt(PX[:, i, :], TH[:, i % 2, :], 1.0, CV[:, i % 2, :], ALU.add, ALU.mult).then_inc(xbc_ok, 1)

    def softplus_and_cumsum(dve, do, sync, tt, ts, stt):
        f = lambda i: DTT[:, i, :, :]
        dve.wait_ge(dt_tr, 1)
        do(nc.vector.memset(f(0), 0.0))
        sync()
        do(tt(f(0)[:, 0:8, :], bank[3][:, 0:64].rearrange("p (a b) -> p a b", b=8),
              bc(prm("dt_bias").unsqueeze(1), [P, 8, 8]), ALU.add))
        do(tt(f(0)[0:SMP, 8, :], bank[3][0:SMP, 64:72], prm("dt_bias")[0:SMP, :], ALU.add))
        sync()
        do(ts(f(1), f(0), -1.0, ALU.mult))
        sync()
        do(tt(f(1), f(1), f(0), ALU.min))
        sync()
        dve.sem_inc(dt_m, 1)
        dve.wait_ge(dt_e, 1)
        do(ts(f(3), f(2), 2.0, ALU.add))
        sync()
        do(nc.vector.reciprocal(f(3), f(3)))
        sync()
        do(tt(f(3), f(2), f(3), ALU.mult))
        sync()
        do(tt(f(4), f(3), f(3), ALU.mult))
        sync()
        do(ts(f(5), f(4), 1.0 / 17, ALU.mult))
        sync()
        for k in range(15, 1, -2):
            do(stt(f(5), f(5), 1.0 / k, f(4), ALU.add, ALU.mult))
            sync()
        do(stt(f(5), f(5), 1.0, f(3), ALU.add, ALU.mult))
        do(ts(f(1), f(0), 0.0, ALU.max))
        sync()
        do(stt(f(5), f(5), 2.0, f(1), ALU.mult, ALU.add))
        sync()
        dve.wait_ge(ea_ok, 1)
        tt(f(6), f(5), bc(DTT[:, 9, 0, :].unsqueeze(1), [P, 9, 8]), ALU.mult).then_inc(ap_ok, 1)

    s_par, s_x = dma_sem("params"), [dma_sem(f"x{k}") for k in range(KD)]
    s_hot = dma_sem("bucket_selection")
    s_raw = [dma_sem(f"weights{i}") for i in range(2)]
    consts_ok, split_ok = sem("consts_ok"), sem("weights_split")
    acc_done = [sem(f"acc_done{n}") for n in range(3)]
    acc_free = [sem(f"acc_free{n}") for n in range(3)]
    sq_done, sq_used = sem("square_done"), sem("square_added")
    ns_done, rs_sq, rs_ok = sem("norm_sum_done"), sem("root_done"), sem("rstd_ready")
    hf_done, h_hi, h_lo = sem("h_full"), sem("h_high"), sem("h_low")
    bias_mm, bias_ev, s_bst = sem("bias_product"), sem("bias_evicted"), dma_sem("bias_stored")
    s_ust, s_uld, s_bc = dma_sem("u_stored"), dma_sem("u_loaded"), dma_sem("s5_params")
    u_zero, step_ok, ar_ok, mag_ok = sem("u_zeroed"), sem("s5_step"), sem("s5_ar"), sem("s5_mag")
    red_ok, sin_ok, w_ok, off_ok = sem("s5_angles"), sem("s5_sines"), sem("s5_W"), sem("s5_OFF")
    kt_zero, tap_mm, tap_ev, s_kt = sem("kt_zeroed"), sem("taps_done"), sem("taps_evicted"), dma_sem("kt_shifted")
    stt_mm, stt_ev = sem("stt_transposed"), sem("stt_evicted")
    sb_mm, st_mm, ki_ok, hst_ok = sem("s5_sample_sums"), sem("s5_step_sums"), sem("s5_rotated"), sem("s5_states")
    y_mm, y_ev, gelu_ok, s_gyst = sem("s5_y_done"), sem("s5_y_evicted"), sem("gelu_done"), dma_sem("gelu_stored")
    fin_ok = sem("s5_final")
    s_out = dma_sem("outputs")
    s_gst = dma_sem("gate_stored")
    s_gf, gg_hi, gg_lo = dma_sem("gelu_loaded"), sem("glu_high"), sem("glu_low")
    s_scv, cw_ok, cst_ok, conv_ok, th_ok, xbc_ok = (dma_sem("conv_state"), sem("conv_weights"), sem("conv_tails"),
                                                    sem("conv_done"), sem("conv_tanh"), sem("xbc_ready"))
    dt_tr, dt_m, dt_e, ap_ok, ea_ok = (sem("dt_transposed"), sem("dt_minus_abs"), sem("dt_exp"), sem("dtA_ready"),
                                       sem("exp_a_log"))
    nac_mm, nac_ok = sem("cumsum_done"), sem("cumsum_evicted")
    tr_mm, bt_ok, xs_ok = sem("ssd_transposed"), sem("b_rows_ready"), sem("xs_ready")
    cb_mm, e_mm, et_ok, m_mm, l_ok = (sem("cb_done"), sem("acum_spread"), sem("exp_acum"), sem("mask_added"),
                                      sem("decay_ready"))
    mm_ok, cd_ok, xd_ok, h_ok = sem("m_ready"), sem("cd_ready"), sem("xd_ready"), sem("state_ready")
    yd_mm, ss_mm, ye_ok = sem("ssd_y_done"), sem("ssd_state_sum"), sem("ssd_y_evicted")
    s_h0, btm_ok = dma_sem("ssd_state_in"), sem("b_by_sequence")
    zt_ok, ya_ok = sem("z_tanh"), sem("y_a_ready")
    s_biass = dma_sem("bias_s_loaded")
    s_bias = [dma_sem(f"bias_loaded{i}") for i in range(2)]
    vt_mm, vt_ok = sem("v_transposed"), sem("v_rows_ready")
    at_s, sb_rd, sm_ok, ex_ok, p_ok = (sem("scores_done"), sem("scores_read"), sem("max_ready"), sem("exp_done"),
                                       sem("probs_ready"))
    tp_mm, pt_ok, pv_mm, yc_ok = sem("probs_transposed"), sem("pt_ready"), sem("pv_done"), sem("y_c_ready")
    s_ks, ks_ok, s_vc, vn_mm, vn_ok = (dma_sem("k_cache"), sem("k_all_ready"), dma_sem("v_cache"),
                                       sem("v_new_transposed"), sem("v_new_ready"))
    yh_hi, yh_lo = sem("y_high"), sem("y_low")
    s_gt = [dma_sem(f"gate_loaded{i}") for i in range(2)]
    mix_ok, mx_hi, mx_lo, s_x1 = sem("mix_added"), sem("mix_high"), sem("mix_low"), dma_sem("x_again")
    f_hi, f_lo = sem("ffn_high"), sem("ffn_low")
    y_ok = sem("y_final")
    y_pool, y_act = sem("y_by_pool"), sem("y_by_scalar")
    h_lo_pool = sem("h_low_by_pool")
    rc_ok, rs_all = sem("rstd_by_token"), sem("rstd_spread")
    chain, row_tile = sem("dve_chain"), sem("row_tile_done")

    uscr = nc.dram_tensor("u_scratch", (512, T), F32, kind="Internal").ap()
    gscr = nc.dram_tensor("gelu_scratch", (512, T), F32, kind="Internal").ap()
    bscr = nc.dram_tensor("bias_scratch", (8, BW), F32, kind="Internal").ap()
    tscr = nc.dram_tensor("gate_scratch", (24, P, T), F32, kind="Internal").ap()

    def blk(a, n):
        return a[:, P * n:P * n + P]

    def as_steps(a, n0, nb):
        return a[:, 0:SEQ].rearrange("p (s n c) -> p n s c", s=SUB, c=CB)[:, n0:n0 + nb]

    def as_blocks(a, nb):
        return a[:, 0:nb * P].rearrange("p (n s c) -> p n s c", s=SUB, c=CB)

    def bc(a, shape):
        return a.broadcast_to(shape)

    def x_wait(eng, k):
        eng.wait_ge(s_x[k], 16)

    def ssd_wait(eng, k):
        eng.wait_ge(ya_ok, NBLK + 1)

    def x1_wait(stage):
        def wait(eng, k):
            for n in range(3):
                eng.wait_ge(acc_free[n], TILE0[stage] + k + 1)
        return wait

    NORMS = [
        dict(tiles=KD, width=D, src=lambda k: X0[:, k, :], source_ready=x_wait, sq=[SQ[:, 0, :], SQ[:, 1, :]], acc=ACC, root=RS, hf=HF,
             weight="norm1"),
        dict(tiles=4, width=512, src=lambda k: PX[:, k, :], source_ready=ssd_wait, sq=[ZQ, ZR], acc=ZA, root=ZR,
             hf=None, weight="ssd_norm"),
        dict(tiles=KD, width=D, src=lambda k: X1[:, k, :], source_ready=x1_wait("out"), sq=[SQ5, GT], acc=AC5, root=RS5, hf=HF5,
             weight="norm2"),
        dict(tiles=KD, width=D, src=lambda k: X1[:, k, :], source_ready=x1_wait("down3"), sq=[SQ5, GT], acc=AC5, root=RS5, hf=None,
             weight="normf"),
    ]
    SQ_BASE = [0, 8, 12, 20]
    HF_BASE = {0: 0, 2: 24}

    def norm_squares_act(q, beside=None):
        m = NORMS[q]
        for k in range(m["tiles"]):
            g = SQ_BASE[q] + k
            m["source_ready"](nc.scalar, k)
            if k >= 2:
                nc.scalar.wait_ge(sq_used, g - 1)
            nc.scalar.activation(m["sq"][k % 2][:], m["src"](k), ACT.Square).then_inc(sq_done, 1)
            if beside is not None:
                beside(k)

    def norm_roots_act(q):
        m = NORMS[q]
        nc.scalar.wait_ge(ns_done, q + 1)
        for rows, c0, c1 in ((P, 0, NBLK), (SMP, NBLK, NBLK + 1)):
            nc.scalar.activation(RC[0:rows, c0:c1], bank[3][0:rows, c0:c1], ACT.Sqrt, bias=prm("eps")[0:rows],
                                 scale=1.0 / m["width"]).then_inc(rs_sq, 1)
        for n, (c0, w) in enumerate(CHUNKS):
            nc.scalar.wait_ge(rs_all, 3 * q + n + 1)
            nc.scalar.copy(m["root"][:, c0:c0 + w], bank[3 + n][:, 0:w]).then_inc(rs_ok, 1)

    def norm_add_dve(q, k):
        m, dve = NORMS[q], nc.vector
        g = SQ_BASE[q] + k
        dve.wait_ge(sq_done, g + 1)
        if k == 0:
            dve.tensor_copy(m["acc"][:], m["sq"][0][:]).then_inc(sq_used, 1)
        else:
            dve.wait_ge(sq_used, g)
            dve.tensor_tensor(m["acc"][:], m["acc"][:], m["sq"][k % 2][:], ALU.add).then_inc(sq_used, 1)

    def norm_sum_dve(q, first=0):
        m, dve = NORMS[q], nc.vector
        for k in range(first, m["tiles"]):
            norm_add_dve(q, k)
        dve.wait_ge(rs_sq, 2 * q + 2)
        for rows, c0, c1 in ((P, 0, NBLK), (SMP, NBLK, NBLK + 1)):
            dve.reciprocal(RC[0:rows, c0:c1], RC[0:rows, c0:c1]).then_inc(rc_ok, 1)

    def norm_sum_pe(q):
        m = NORMS[q]
        nc.tensor.wait_ge(sq_used, SQ_BASE[q] + m["tiles"])
        for j in range(NBLK + 1):
            w = P if j < NBLK else SMP
            last = nc.tensor.matmul(bank[3][0:w, j:j + 1], m["acc"][:, P * j:P * j + w], prm("ones", 0, 1), start=True,
                                    stop=True)
        last.then_inc(ns_done, 1)
        nc.tensor.wait_ge(rc_ok, 2 * q + 2)
        for j in range(NBLK + 1):
            w = P if j < NBLK else SMP
            last = nc.tensor.matmul(bank[3 + j // 3][:, P * (j % 3):P * (j % 3) + w], bc(RC[0:w, j:j + 1], [w, P]),
                                    IDENT[0:w, 0:w], start=True, stop=True)
            if j % 3 == 2:
                last.then_inc(rs_all, 1)

    def pool_low(q, i):
        return q == 2 and i % 3 == 1

    def low_wait(eng, q, i):
        by_pool = sum(pool_low(q, x) for x in range(i + 1))
        eng.wait_ge(h_lo, HF_BASE[q] + i + 1 - by_pool)
        if by_pool:
            eng.wait_ge(h_lo_pool, by_pool)

    def norm_split_dve(q):
        m, dve, b = NORMS[q], nc.vector, HF_BASE[q]
        steps = [(n, k) for n in range(3) for k in range(KD)]
        slots = len(m["hf"])

        def low(i):
            if pool_low(q, i):
                return
            n, k = steps[i]
            c0, w = CHUNKS[n]
            dve.wait_ge(h_hi, b + i + 1)
            dve.tensor_tensor(HL[:, k, c0:c0 + w], m["hf"][i % slots][:, 0:w], HH[:, k, c0:c0 + w].bitcast(F32),
                              ALU.subtract).then_inc(h_lo, 1)

        for i, (n, k) in enumerate(steps):
            c0, w = CHUNKS[n]
            dve.wait_ge(rs_ok, 3 * q + n + 1)
            if i >= slots:
                low_wait(dve, q, i - slots)
            dve.scalar_tensor_tensor(m["hf"][i % slots][:, 0:w], m["src"](k)[:, c0:c0 + w], prm(m["weight"], k, 1),
                                     m["root"][:, c0:c0 + w], ALU.mult, ALU.mult).then_inc(hf_done, 1)
            if i >= 1:
                low(i - 1)
        low(len(steps) - 1)

    def norm_split_act(q, beside=None):
        m, b = NORMS[q], HF_BASE[q]
        for i, (n, k) in enumerate([(n, k) for n in range(3) for k in range(KD)]):
            c0, w = CHUNKS[n]
            nc.scalar.wait_ge(hf_done, b + i + 1)
            nc.scalar.copy(HH[:, k, c0:c0 + w], m["hf"][i % len(m["hf"])][:, 0:w]).then_inc(h_hi, 1)
            if beside is not None:
                beside(i)

    def y_dst(j):
        return PX[:, j, :] if j < 4 else PU[:, j - 4, :]

    ATTN_STEPS = [*range(NBLK), None, *range(NBLK, 2 * NBLK)]
    NSTEP = len(ATTN_STEPS)

    def branch_at(p):
        return p - 1 if p >= 1 else None

    def acc_of(no, n):
        return bank[3 + n] if no == TILE0["up0"] + 1 else acc[n]

    block = top.enter_context(nc.Block())

    @block.sync
    def _(sp):
        sp.dma_start(PRM[:], io["params"]).then_inc(s_par, 16)
        for k in range(KD):
            sp.dma_start(X0[:, k, :], io["x"][k]).then_inc(s_x[k], 16)
        for u in range(2):
            sp.dma_start(WRAW[:, u, :], io["w"][u]).then_inc(s_raw[u], 16)
        sp.dma_start(HOT[:], io["hot"]).then_inc(s_hot, 16)
        sp.dma_start(RTAB[:], io["rtab"]).then_inc(s_hot, 16)
        sp.dma_start(BC[:], io["bc"]).then_inc(s_bc, 16)
        sp.dma_start(S0[:], io["s0"]).then_inc(s_bc, 16)

        def weights(i, u, slot):
            sp.wait_ge(split_ok, u - 1)
            sp.dma_start(WRAW[:, slot, :], io["w"][bass.ds(u, 1)].rearrange("a p n -> (a p) n")).then_inc(s_raw[slot], 16)

        with sp.Fori(1, UNITS // 2) as i:
            for slot in range(2):
                weights(i, i * 2 + slot, slot)
        sp.wait_ge(split_ok, UNITS - 2)
        sp.dma_start(WRAW[:, 0, :], io["w"][UNITS - 1]).then_inc(s_raw[0], 16)
        sp.wait_ge(s_out, 16 * N_OUT_TOTAL)

    @block.gpsimd
    def _(pool):
        nc.gpsimd.memset(ZERO[:], 0.0).then_inc(consts_ok, 1)
        pool.wait_ge(s_par, 16)
        nc.gpsimd.tensor_copy(IDB[:], IDENT).then_inc(consts_ok, 1)
        nc.gpsimd.tensor_copy(MASKB[:], prm("mask")).then_inc(consts_ok, 1)
        nc.gpsimd.tensor_copy(MASKSB[:], prm("mask_s")[0:SMP, :]).then_inc(consts_ok, 1)
        pool.wait_ge(consts_ok, 4)

        def split(slot, loaded, lows_before, tiles_done):
            pool.wait_ge(s_raw[slot], loaded)
            if tiles_done is not None:
                pool.wait_ge(acc_done[2], tiles_done)
            nc.gpsimd.tensor_tensor(WH[:, slot, :], WRAW[:, slot, :], bc(ZERO[:, 0:1], [P, 1024]),
                                    ALU.add).then_inc(w_hi, 1)
            pool.wait_ge(w_hi, lows_before + 1)
            nc.gpsimd.tensor_tensor(WL[:, slot, :], WRAW[:, slot, :], WH[:, slot, :].bitcast(F32),
                                    ALU.subtract).then_inc(split_ok, 1)

        def norm_lows():
            for i in range(3 * KD):
                if pool_low(2, i):
                    n, k = divmod(i, KD)
                    c0, w = CHUNKS[n]
                    pool.wait_ge(h_hi, HF_BASE[2] + i + 1)
                    nc.gpsimd.tensor_tensor(HL[:, k, c0:c0 + w], HF5[i % 6][:, 0:w], HH[:, k, c0:c0 + w].bitcast(F32),
                                            ALU.subtract).then_inc(h_lo_pool, 1)

        u = 0
        while u < UNITS:
            need = [None if v < 2 else TILE_END[v - 2] for v in range(UNITS)]
            e = u + 1
            if u >= 2 and u + 1 < UNITS:
                d = need[u + 1] - need[u]
                while e < UNITS and e != UNIT0["up0"] + 2 and need[e] - need[e - 1] == d:
                    e += 1
            pairs = (e - u) // 2
            if pairs >= 2:
                with pool.Fori(0, pairs) as i:
                    for s in range(2):
                        v = u + s
                        split(v % 2, i * 16 + 16 * (v // 2 + 1), i * 2 + v, i * (2 * d) + need[v])
                u += 2 * pairs
            else:
                split(u % 2, 16 * (u // 2 + 1), u, need[u])
                u += 1
            if u == UNIT0["up0"] + 2:
                norm_lows()

        pool.wait_ge(rs_ok, 12)
        for k in (KD - 2, KD - 1):
            nc.gpsimd.tensor_tensor(X1[:, k, :], X1[:, k, :], RS5[:], ALU.mult).then_inc(y_pool, 1)

    @block.tensor
    def _(pe):
        def mm3(out, k, slot, rh, rl, start, stop):
            wh, wl = WH[:, slot, k * P:(k + 1) * P], WL[:, slot, k * P:(k + 1) * P]
            nc.tensor.matmul(out, wh, rl, start=start, stop=False)
            nc.tensor.matmul(out, wl, rh, start=False, stop=False)
            return nc.tensor.matmul(out, wh, rh, start=False, stop=stop)

        fences = [0]

        def fence(inst):
            fence_set(inst)
            fence_wait()

        def fence_set(inst):
            inst.then_inc(row_tile, 1)
            fences[0] += 1

        def fence_wait():
            pe.wait_ge(row_tile, fences[0])

        def tile(no, slot, koff, nk, RH, RL, kbase=0, before=None, chunks=range(3)):
            for n in chunks:
                c0, w = CHUNKS[n]
                if not (isinstance(no, int) and no == 0):
                    pe.wait_ge(acc_free[n], no)
                for k in range(nk):
                    if before is not None:
                        before(n, k)
                    last = mm3(acc[n][:, 0:w], koff + k, slot, RH[:, kbase + k, c0:c0 + w], RL[:, kbase + k, c0:c0 + w],
                               k == 0, k == nk - 1)
                last.then_inc(acc_done[n], 1)

        def unit(u, slot, tiles):
            pe.wait_ge(split_ok, u + 1)
            for args, kw in tiles:
                tile(args[0], slot, *args[1:], **kw)

        def gate(g, chunks=range(3)):
            u = (UNIT0["gates1"] + g) if g < 12 else (UNIT0["gates2"] + g - 12)
            no = (TILE0["gates1"] + g) if g < 12 else (TILE0["gates2"] + g - 12)
            unit(u, u % 2, [((no, 0, KD, HH, HL), dict(chunks=chunks))])

        def simple_loop(name, pairs, nk, RH, RL, skip=0, kbase=0, before=None):
            u0, t0 = UNIT0[name] + skip, TILE0[name] + skip
            with pe.Fori(0, pairs) as i:
                for s in range(2):
                    unit(i * 2 + (u0 + s), (u0 + s) % 2, [((i * 2 + (t0 + s), 0, nk, RH, RL, kbase), dict(before=before))])

        def first_unit(name, before, pairs=4, nk=KD, RH=HH, RL=HL):
            for s in range(2):
                u, no = UNIT0[name] + s, TILE0[name] + s
                unit(u, u % 2, [((no, 0, nk, RH, RL), dict(before=before if s == 0 else None))])
            simple_loop(name, pairs - 1, nk, RH, RL, skip=2)

        def first_pair(name, before):
            u, no = UNIT0[name], TILE0[name]
            pe.wait_ge(split_ok, u + 2)
            for n, (c0, w) in enumerate(CHUNKS):
                if no > 0:
                    pe.wait_ge(acc_free[n], no)
                for k in range(KD):
                    before(n, k)
                    for s in range(2):
                        last = mm3(acc_of(no + s, n)[:, 0:w], k, (u + s) % 2, HH[:, k, c0:c0 + w], HL[:, k, c0:c0 + w],
                                   k == 0, k == KD - 1)
                        if k == KD - 1:
                            last.then_inc(acc_done[n], 1)

        pe.wait_ge(s_par, 16)
        norm_sum_pe(0)

        pe.wait_ge(s_hot, 32)
        for i in range(18):
            half, q = divmod(i, 9)
            if i >= 2:
                pe.wait_ge(bias_ev, i - 1)
            r = 64 * half
            nc.tensor.matmul(bank[6 + i % 2][r:r + 8, 0:BSTEP], RTAB[r:r + NBUCKET + 1, :],
                             HOT[r:r + NBUCKET + 1, q * BSTEP:(q + 1) * BSTEP], start=True, stop=True).then_inc(bias_mm, 1)
        for j in range(4):
            unit(j, j % 2, [((j, 0, KD, HH, HL),
                             dict(before=(lambda n, k: pe.wait_ge(h_lo, 8 * n + k + 1)) if j == 0 else None))])


        pe.wait_ge(w_ok, 1)
        pe.wait_ge(bias_ev, 18)
        for pr in range(NP):
            for part, wt in ((0, W_re), (1, W_im)):
                last = nc.tensor.matmul(bank[7][:, pr * 32:(pr + 1) * 32], wt[:, pr, :],
                                        CDG[:, part, pr, :, :].rearrange("p e h -> p (e h)"),
                                        start=(part == 0), stop=(part == 1))
        last.then_inc(tap_mm, 1)
        for i in range(8):
            if i >= 2:
                pe.wait_ge(stt_ev, i - 1)
            wt = (W_re, W_im)[i // 4]
            for j in range(4):
                last = nc.tensor.transpose(bank[5 + i % 2][:, j * P:(j + 1) * P], wt[:, 4 * (i % 4) + j, :], IDENT)
            last.then_inc(stt_mm, 1)
        gate(0)
        gate(1)

        pe.wait_ge(stt_ev, 8)
        pe.wait_ge(s_uld, 16 * 16)
        pe.wait_ge(tap_ev, 1)
        for pr in range(NP):
            for part in range(2):
                c = (part * NP + pr) * 2 * NSEQ
                last = nc.tensor.matmul(bank[7][:, c:c + 2 * NSEQ], STT[:, part, pr, :], U[:, 2 * pr:2 * pr + 2, YC:YC + NSEQ],
                                        start=True, stop=True)
        last.then_inc(sb_mm, 1)

        def step_sums(b):
            if b >= 1:
                pe.wait_ge(ki_ok, b)
            for j in range(4):
                pr = 4 * b + j
                for e in range(2):
                    for part in range(2):
                        last = nc.tensor.matmul(bank[3 + part][64 * e:64 * e + 64, j * CH:(j + 1) * CH],
                                                STT[:, part, pr, 64 * e:64 * e + 64], U[:, 2 * pr + e, 0:CH],
                                                start=True, stop=True)
            last.then_inc(st_mm, 1)

        def outputs(b):
            pe.wait_ge(hst_ok, b + 1)
            if b == 0:
                pe.wait_ge(kt_ok, 1)
                pe.wait_ge(off_ok, 1)
            for j in range(4):
                pr = 4 * b + j
                if pr >= 2:
                    pe.wait_ge(y_ev, pr - 1)
                for e in range(2):
                    g = 2 * pr + e
                    o = bank[5 + pr % 2][:, 256 * e:256 * e + YC]
                    nc.tensor.matmul(o, KT[:, g, :, :].rearrange("p t h -> p (t h)"), U[:, g, 0:YC], start=True, stop=False)
                    if e == 1:
                        fence_wait()
                    nc.tensor.matmul(o, OFF_re[64 * e:64 * e + 64, pr, :], HST[64 * e:64 * e + 64, 0, j, :],
                                     start=False, stop=False)
                    last = nc.tensor.matmul(o, OFF_im[64 * e:64 * e + 64, pr, :], HST[64 * e:64 * e + 64, 1, j, :],
                                            start=False, stop=True)
                    if e == 0:
                        fence_set(last)
                last.then_inc(y_mm, 1)

        step_sums(0)
        gate(2)
        step_sums(1)
        gate(3)
        outputs(0)
        gate(4)
        step_sums(2)
        outputs(1)
        gate(5)
        step_sums(3)
        gate(6)
        outputs(2)
        gate(7)
        outputs(3)
        for g in range(8, 12):
            gate(g)

        for i in range(4):
            u, no = UNIT0["glu"] + i, TILE0["glu"] + 2 * i
            if i == 0:
                pe.wait_ge(gg_lo, 4)
            unit(u, u % 2, [((no, 0, 4, GGH, GGL), {}), ((no + 1, 4, 4, GGH, GGL), {})])

        def dt_rows():
            for n in range(3):
                pe.wait_ge(acc_free[n], TILE0["proj"] + 7)
            for n in range(NBLK):
                nc.tensor.transpose(bank[3][:, n * 8:n * 8 + 8], blk(DTF[0:8, :], n), IDENT[0:8, 0:8])
            nc.tensor.transpose(bank[3][0:SMP, 64:72], DTF[0:8, SEQ:T], IDENT[0:8, 0:8]).then_inc(dt_tr, 1)

        simple_loop("proj", 4, KD, HH, HL)
        dt_rows()
        simple_loop("proj", 4, KD, HH, HL, skip=8)
        u = UNIT0["proj"] + 16
        unit(u, u % 2, [((TILE0["proj"] + 16, 0, KD, HH, HL), {})])

        def ssd_setup():
            pe.wait_ge(ap_ok, 1)
            pe.wait_ge(y_ev, 16)
            pe.wait_ge(fin_ok, 5)
            nc.tensor.matmul(bank[4][:, 0:64], prm("tri"), DTT[:, 6, 0:8, :], start=True, stop=True)
            nc.tensor.matmul(bank[4][0:SMP, 64:72], prm("tri_s")[0:SMP, :], DTT[0:SMP, 6, 8, :], start=True,
                             stop=True).then_inc(nac_mm, 1)
            gate(12, [0])
            pe.wait_ge(nac_ok, 1)
            pe.wait_ge(xbc_ok, 6)
            pe.wait_ge(consts_ok, 4)

        def ssd_chunk(n):
            smp = n == NBLK
            rows = SMP if smp else P
            cols = (lambda a: a[:, SEQ:T]) if smp else (lambda a: blk(a, n))
            tri = prm("negtri_s")[0:SMP, :] if smp else prm("negtri")
            pe.wait_ge(h_ok, n + 1)
            for i in range(4):
                nc.tensor.transpose(bank[3][0:rows, i * P:(i + 1) * P], cols(PX[:, i, :]), IDENT)
            if n >= 1:
                pe.wait_ge(mm_ok, n)
            nc.tensor.transpose(bank[4][0:rows, 0:P], cols(PX[:, 4, :]), IDENT).then_inc(tr_mm, 1)
            for g in range(2):
                r = 64 * g
                if g == 1:
                    fence(last)
                last = nc.tensor.matmul(bank[4][0:rows, P + r * 2:P + r * 2 + rows], cols(PX[r:r + 64, 4, :]),
                                        cols(PX[r:r + 64, 5, :]), start=True, stop=True)
            last.then_inc(cb_mm, 1)
            for g in range(2):
                if n >= 1:
                    pe.wait_ge(l_ok, n)
                for k in range(4):
                    last = nc.tensor.matmul(bank[5 + g][:, k * rows:(k + 1) * rows],
                                            bc(DTT[0:rows, 6, n, 4 * g + k:4 * g + k + 1], [rows, P]), tri,
                                            start=(k == 0), stop=(k == 3), skip_group_check=True)
                last.then_inc(e_mm, 1)
            gate(12 + n, [1] if n == 0 else [0])
            pe.wait_ge(et_ok, n + 1)
            for g in range(2):
                mask = MASKSB[:] if smp else MASKB[:]
                last = nc.tensor.matmul(bank[5 + g][0:rows, 0:4 * rows], IDB[0:rows, 0:rows],
                                        bc(mask.unsqueeze(1), [rows, 4, rows]), start=False, stop=True,
                                        skip_group_check=True)
            last.then_inc(m_mm, 1)
            gate(12 + n, [2] if n == 0 else [1, 2])
            pe.wait_ge(mm_ok, n + 1)
            pe.wait_ge(cd_ok, n + 1)
            if n >= 1:
                pe.wait_ge(ye_ok, n)
            for h in range(8):
                g, k, i, r = h // 4, h % 4, h // 2, 64 * (h % 2)
                if h == 4:
                    fence(last)
                o = bank[7][r:r + 64, i * P:i * P + rows]
                m = L[0:rows, h, 0:rows] if not smp else LS[:, 1, h, :]
                nc.tensor.matmul(o, XS[0:rows, h * HD:(h + 1) * HD], m, start=True, stop=smp)
                if not smp:
                    last = nc.tensor.matmul(o, HS[64 * g:64 * g + 64, n % 2, k, :], CD[64 * g:64 * g + 64, k, :],
                                            start=False, stop=True)
                else:
                    for b in range(NSEQ):
                        last = nc.tensor.matmul(o[:, b:SMP:NSEQ], H0[64 * g:64 * g + 64, b, k, :],
                                                CD[64 * g:64 * g + 64, 0, k * SMP + b:(k + 1) * SMP:NSEQ],
                                                start=False, stop=True, skip_group_check=True)
            last.then_inc(yd_mm, 1)
            if not smp:
                pe.wait_ge(bt_ok, n + 1)
                pe.wait_ge(xd_ok, n + 1)
                for g in range(2):
                    last = nc.tensor.matmul(bank[3][64 * g:64 * g + 64, 0:256], BT[:, 64 * g:64 * g + 64],
                                            XD[:, 256 * g:256 * g + 256], start=True, stop=True)
                last.then_inc(ss_mm, 1)
            else:
                gate(21, [0])
                for b in range(NSEQ):
                    if b % 4 == 0:
                        pe.wait_ge(btm_ok, b // 4 + 1)
                    if b >= 2:
                        pe.wait_ge(h_ok, NBLK + b)
                    else:
                        pe.wait_ge(xd_ok, n + 1)
                    for g in range(2):
                        last = nc.tensor.matmul(bank[(3, 4)[b % 2]][64 * g:64 * g + 64, 0:256],
                                                BTM[:, b % 4, 64 * g:64 * g + 64],
                                                XD[0:SMP, 256 * g:256 * g + 256], start=True, stop=True)
                    last.then_inc(ss_mm, 1)

        def scores(p):
            a = ATTN_STEPS[p]
            if p >= 1:
                pe.wait_ge(sb_rd, p)
            if a is None:
                pe.wait_ge(ks_ok, 2)
                for kv in range(2):
                    if kv == 1:
                        fence(last)
                    for b in range(NSEQ):
                        r, y = 32 * (b % 4), 2 * (b // 4) + kv
                        o = bank[3 + y // 2][r:r + 32, (y % 2) * 256:(y % 2) * 256 + P + DSEQ]
                        last = nc.tensor.matmul(o, QS[64 * kv:64 * kv + 64, b, :], KS[64 * kv:64 * kv + 64, b, :],
                                                start=True, stop=True)
                last.then_inc(at_s, 1)
                return
            n, kv = divmod(a, 2)
            lo = P if n == 0 else 0
            for i in range(4):
                at = (i % 2) * 256
                last = nc.tensor.matmul(bank[3 + i // 2][:, at + lo:at + 256], blk(PU[64 * kv:64 * kv + 64, 4 + i, :], n),
                                        PX[64 * kv:64 * kv + 64, 6, P * (n - 1) + lo:P * (n + 1)],
                                        start=True, stop=True)
            last.then_inc(at_s, 1)

        ssd_setup()
        for n in range(NBLK + 1):
            ssd_chunk(n)
        gate(21, [1, 2])
        pe.wait_ge(h_ok, NBLK + 1 + NSEQ)
        norm_sum_pe(1)
        gate(22)
        pe.wait_ge(rs_ok, 6)
        scores(0)
        gate(23)

        pe.wait_ge(ye_ok, NBLK + 1)
        for n in range(NBLK):
            nc.tensor.transpose(bank[6 + n // 4][:, (n % 4) * P:(n % 4 + 1) * P], blk(PX[:, 7, :], n), IDENT)
        for b in range(NSEQ):
            r = 32 * (b // 4)
            last = nc.tensor.matmul(bank[5][r:r + DSEQ, (b % 4) * P:(b % 4 + 1) * P], PX[:, 7, SEQ + b:T:NSEQ], IDENT,
                                    start=True, stop=True)
        last.then_inc(vt_mm, 1)

        def branch(t, chunks):
            q, no = t // 8, TILE0["branch"] + t
            u = UNIT0["branch"] + t // 2
            if t % 8 == 0 and chunks[0] == 0:
                pe.wait_ge(yh_lo, 4 * (q + 1))
            if t % 2 == 0 and chunks[0] == 0:
                pe.wait_ge(split_ok, u + 1)
            tile(no, u % 2, 4 * (t % 2), 4, HH, HL, (4, 0, 4)[q], chunks=chunks)

        def transposed_probs(p):
            a = ATTN_STEPS[p]
            pe.wait_ge(p_ok, p + 1)
            if p >= 1:
                pe.wait_ge(pt_ok, p)
            else:
                pe.wait_ge(vt_ok, 2)
            if p == 2:
                pe.wait_ge(vn_ok, 1)
            if a is None:
                for y in range(4):
                    nc.tensor.transpose(bank[5][:, y * P:(y + 1) * P], SB[:, p % 2, y, 0:P], IDENT)
                    last = nc.tensor.transpose(bank[6][0:DSEQ, y * P:(y + 1) * P], SB[:, p % 2, y, P:P + DSEQ], IDENT)
            else:
                for half in range(1 if a < 2 else 0, 2):
                    for i in range(4):
                        last = nc.tensor.transpose(bank[5 + half][:, i * P:(i + 1) * P],
                                                   SB[:, p % 2, i, half * P:half * P + P], IDENT)
            last.then_inc(tp_mm, 1)

        def pv(p):
            a = ATTN_STEPS[p]
            pe.wait_ge(pt_ok, p + 1)
            if p >= 1:
                pe.wait_ge(yc_ok, p)
            if a is None:
                pe.wait_ge(s_vc, 16)
                for b in range(NSEQ):
                    for kv in range(2):
                        at = (2 * (b // 4) + kv) * P + 32 * (b % 4)
                        o = bank[7][64 * kv:64 * kv + 64, b * 16:(b + 1) * 16]
                        nc.tensor.matmul(o, VC[:, b, 64 * kv:64 * kv + 64], PT[:, 0, at:at + 16], start=True, stop=False)
                        last = nc.tensor.matmul(o, VN[:, b * P + 64 * kv:b * P + 64 * kv + 64], PT[0:DSEQ, 1, at:at + 16],
                                                start=False, stop=True)
                last.then_inc(pv_mm, 1)
                return
            n, kv = divmod(a, 2)
            vt = PX[:, 7, 0:SEQ].rearrange("p (n d) -> p n d", n=NBLK)
            o = bank[7][64 * kv:64 * kv + 64, :]
            if n >= 1:
                nc.tensor.matmul(o, vt[:, n - 1, 64 * kv:64 * kv + 64], PT[:, 0, :], start=True, stop=False)
            nc.tensor.matmul(o, vt[:, n, 64 * kv:64 * kv + 64], PT[:, 1, :], start=(n == 0), stop=True).then_inc(pv_mm, 1)

        for p in range(NSTEP):
            if p + 1 < NSTEP:
                scores(p + 1)
            t = branch_at(p)
            if t is not None and p < NSTEP - 1:
                branch(t, [0, 1])
            transposed_probs(p)
            if t is not None and p < NSTEP - 1:
                branch(t, [2])
            pv(p)
        branch(NSTEP - 2, [0, 1, 2])
        for t in range(16, 24):
            branch(t, [0, 1, 2])

        first_unit("out", lambda n, k: pe.wait_ge(mx_lo, 8 * n + k + 1))
        norm_sum_pe(2)

        ff = 0
        for p, nf in enumerate(FFN_PASSES):
            if p == 0:
                first_pair("up0", lambda n, k: low_wait(pe, 2, 8 * n + k))
                simple_loop("up0", nf - 1, KD, HH, HL, skip=2)
            else:
                simple_loop(f"up{p}", nf, KD, HH, HL)
            first_unit(f"down{p}", lambda n, k: pe.wait_ge(f_lo, 3 * (ff + k) + n + 1), nk=nf, RH=FH, RL=FL)
            ff += nf
        norm_sum_pe(3)

    @block.scalar
    def _(act):
        outs = [0]

        def out_dma(dst, src):
            act.dma_start(dst, src).then_inc(s_out, 16)
            outs[0] += 1

        def outs_landed():
            act.wait_ge(s_out, 16 * outs[0])

        def evict(no, dst):
            for n, (c0, w) in enumerate(CHUNKS):
                act.wait_ge(acc_done[n], no + 1)
                nc.scalar.copy(dst[:, c0:c0 + w], acc[n][:, 0:w]).then_inc(acc_free[n], 1)

        def evicted(no):
            for n in range(3):
                act.wait_ge(acc_free[n], no + 1)

        def gate(g):
            no = (TILE0["gates1"] + g) if g < 12 else (TILE0["gates2"] + g - 12)
            if g >= 1:
                act.wait_ge(s_gst, 16 * g)
            for n, (c0, w) in enumerate(CHUNKS):
                act.wait_ge(acc_done[n], no + 1)
                nc.scalar.activation(GT[:, c0:c0 + w], acc[n][:, 0:w], ACT.Tanh, scale=0.5).then_inc(acc_free[n], 1)
            evicted(no)
            act.dma_start(tscr[g], GT[:]).then_inc(s_gst, 16)

        act.wait_ge(s_par, 16)
        nc.scalar.activation(SF("step"), prm("log_dt"), ACT.Exp).then_inc(step_ok, 1)
        act.wait_ge(ar_ok, 1)
        nc.scalar.activation(SF("mag"), SF("ar"), ACT.Exp).then_inc(mag_ok, 1)
        act.wait_ge(red_ok, 1)
        nc.scalar.activation(SF("sin"), SF("r"), ACT.Sin)
        nc.scalar.activation(SF("cos"), SF("r2"), ACT.Sin).then_inc(sin_ok, 1)
        norm_squares_act(0)
        norm_roots_act(0)


        def bias_row(i):
            if i < 18:
                half, q = divmod(i, 9)
                r = 64 * half
                act.wait_ge(bias_mm, i + 1)
                nc.scalar.copy(BTAB[r:r + 8, q * BSTEP:(q + 1) * BSTEP], bank[6 + i % 2][r:r + 8, 0:BSTEP]).then_inc(bias_ev, 1)

        norm_split_act(0, beside=bias_row)
        act.wait_ge(h_lo, 24)
        act.wait_ge(bias_ev, 18)
        act.dma_start(bscr[:, 0:BHALF], BTAB[0:8, :]).then_inc(s_bst, 16)
        act.dma_start(bscr[:, BHALF:BW_P], BTAB[64:72, 0:BW_P - BHALF]).then_inc(s_bst, 16)
        act.dma_start(bsscr, BTAB[64:72, BW_P - BHALF:BHALF]).then_inc(s_bst, 16)

        for j in range(4):
            for n, (c0, w) in enumerate(CHUNKS):
                nb = min(w // P, NBLK - c0 // P)
                act.wait_ge(acc_done[n], j + 1)
                last = nc.scalar.copy(as_steps(UF[:, j, :], c0 // P, nb), as_blocks(acc[n], nb))
                if w > nb * P:
                    last = nc.scalar.copy(UF[:, j, SEQ:T], acc[n][:, nb * P:w])
                last.then_inc(acc_free[n], 1)
            evicted(TILE0["u"] + j)
            act.dma_start(uscr[j * P:(j + 1) * P, :], UF[:, j, :]).then_inc(s_ust, 16)
        act.wait_ge(s_ust, 64)
        act.wait_ge(u_zero, 1)
        for s in range(SUB):
            act.dma_start(U[s * 16:(s + 1) * 16, :, 0:CH],
                          bass.AP(tensor=uscr.tensor, offset=s * CH, ap=[[T, 16], [16 * T, NG], [1, CH]])).then_inc(s_uld, 16)
        for t in range(DSEQ):
            src = bass.AP(tensor=uscr.tensor, offset=SEQ + t * NSEQ, ap=[[T, 16], [16 * T, NG], [1, NSEQ]])
            act.dma_start(U[t * 16:(t + 1) * 16, :, CH + 1:YC], src).then_inc(s_uld, 16)
            act.dma_start(U[(t + 4) * 16:(t + 5) * 16, :, YC:UC], src).then_inc(s_uld, 16)

        for i in range(8):
            act.wait_ge(stt_mm, i + 1)
            nc.scalar.copy(STT[:, i // 4, 4 * (i % 4):4 * (i % 4) + 4, :].rearrange("p a b -> p (a b)"),
                           bank[5 + i % 2][:]).then_inc(stt_ev, 1)
        act.wait_ge(tap_mm, 1)
        act.wait_ge(kt_zero, 1)
        nc.scalar.copy(KTS[:, SUB - 1, :, :].rearrange("p g h -> p (g h)"), bank[7][:]).then_inc(tap_ev, 1)
        act.wait_ge(tap_ev, 1)
        for t in range(SUB - 1):
            act.dma_start(KTS[0:(t + 1) * 16, t, :, :], KTS[(SUB - 1 - t) * 16:P, SUB - 1, :, :]).then_inc(s_kt, 16)
        for g in range(4):
            gate(g)
        for b in range(4):
            for j in range(4):
                pr = 4 * b + j
                act.wait_ge(y_ev, pr + 1)
                nc.scalar.activation(U[:, 2 * pr:2 * pr + 2, 0:YC], U[:, 2 * pr:2 * pr + 2, 0:YC],
                                     ACT.Gelu_apprx_tanh).then_inc(gelu_ok, 1)
            for g in ([4], [5, 6], [7], [])[b]:
                gate(g)
        act.wait_ge(gelu_ok, 16)
        for s in range(SUB):
            act.dma_start(bass.AP(tensor=gscr.tensor, offset=s * CH, ap=[[T, 16], [16 * T, NG], [1, CH]]),
                          U[s * 16:(s + 1) * 16, :, 0:CH]).then_inc(s_gyst, 16)
        for t in range(DSEQ):
            act.dma_start(bass.AP(tensor=gscr.tensor, offset=SEQ + t * NSEQ, ap=[[T, 16], [16 * T, NG], [1, NSEQ]]),
                          U[t * 16:(t + 1) * 16, :, CH + 1:YC]).then_inc(s_gyst, 16)
        act.wait_ge(fin_ok, 5)
        out_dma(io["s5p"], FIN[:])
        out_dma(io["s5s"], FINS[:])
        gate(8)
        act.wait_ge(s_gyst, 12 * 16)
        act.wait_ge(y_mm, 16)
        outs_landed()
        for j in range(4):
            act.dma_start(GF[:, j, :], gscr[j * P:(j + 1) * P, :]).then_inc(s_gf, 16)
        gate(9)
        act.wait_ge(s_gf, 64)
        for j in range(4):
            nc.scalar.copy(as_blocks(GGH[:, j, :], NBLK), as_steps(GF[:, j, :], 0, NBLK))
            nc.scalar.copy(GGH[:, j, SEQ:T], GF[:, j, SEQ:T]).then_inc(gg_hi, 1)
        gate(10)
        gate(11)
        for i in range(4):
            no = TILE0["glu"] + 2 * i
            for n, (c0, w) in enumerate(CHUNKS):
                act.wait_ge(acc_done[n], no + 1)
                nc.scalar.activation(GLT[:, n, 0:w], acc[n][:, 0:w], ACT.Sigmoid).then_inc(acc_free[n], 1)
        evicted(TILE0["proj"] - 1)
        act.dma_start(SCV[:], io["scv"]).then_inc(s_scv, 16)
        nc.scalar.activation(DTT[:, 9, 0, :], prm("a_log"), ACT.Exp).then_inc(ea_ok, 1)

        dests = [PX[:, i, :] for i in range(6)] + [DTF] + [PX[:, i, :] for i in (6, 7, 8, 9, 10, 11)] + \
                [PU[:, i, :] for i in (4, 5, 6, 7)]
        for i, dst in enumerate(dests):
            evict(TILE0["proj"] + i, dst)
            if i == 7:
                act.wait_ge(dt_m, 1)
                nc.scalar.activation(DTT[:, 2, :, :], DTT[:, 1, :, :], ACT.Exp).then_inc(dt_e, 1)
            if 8 <= i < 14:
                c = i - 8
                act.wait_ge(conv_ok, c + 1)
                if c >= 2:
                    act.wait_ge(xbc_ok, c - 1)
                nc.scalar.activation(TH[:, c % 2, :], CV[:, c % 2, :], ACT.Tanh).then_inc(th_ok, 1)
        act.wait_ge(cst_ok, 1)
        out_dma(io["conv_p"], CST[:])
        out_dma(io["conv_s"], CSS[:])
        evicted(TILE0["proj"] + 8)
        out_dma(io["kp"], blk(PX[:, 6, :], NBLK - 1))
        out_dma(io["vp"], blk(PX[:, 7, :], NBLK - 1))
        act.wait_ge(xbc_ok, 6)
        outs_landed()
        act.dma_start(H0[:], io["h0"]).then_inc(s_h0, 16)

        for n in range(NBLK + 1):
            smp = n == NBLK
            rows = SMP if smp else P
            act.wait_ge(cb_mm, n + 1)
            if n >= 1:
                act.wait_ge(ss_mm, n)
            nc.scalar.copy(BT[0:rows, :], bank[4][0:rows, 0:P]).then_inc(bt_ok, 1)
            act.wait_ge(e_mm, 2 * n + 2)
            if n >= 1:
                act.wait_ge(h_ok, n + 1)
                act.wait_ge(cd_ok, n)
            etf = ET[:].rearrange("p a b -> p (a b)")
            for g in range(2):
                nc.scalar.activation(etf[64 * g:64 * g + 64, 0:4 * rows], bank[5 + g][64 * g:64 * g + 64, 0:4 * rows],
                                     ACT.Exp).then_inc(et_half, 1)
            act.wait_ge(et_half, 2 * n + 2)
            act.sem_inc(et_ok, 1)
            act.wait_ge(m_mm, n + 1)
            if n >= 1:
                act.wait_ge(yd_mm, n)
                act.wait_ge(xd_ok, n)
            for h in range(8):
                dst = LS[:, 0, h, :] if smp else L[:, h, :]
                last = nc.scalar.activation(dst, bank[5 + h // 4][0:rows, (h % 4) * rows:(h % 4 + 1) * rows], ACT.Exp,
                                            bias=DTT[0:rows, 7, n, h:h + 1])
            last.then_inc(l_ok, 1)
            if n >= 1:
                act.wait_ge(ya_ok, n)
            z = PX[:, 8:12, SEQ:T] if smp else PX[:, 8:12, P * n:P * n + P]
            for half in range(2):
                last = nc.scalar.activation(ZB[half][:, :, 0:rows], z[:, 2 * half:2 * half + 2, :], ACT.Tanh, scale=0.5)
            last.then_inc(zt_ok, 1)
            gate(12 + n)

        act.wait_ge(h_ok, NBLK + 1 + NSEQ)
        out_dma(io["ssd_p"], HS[:, 0, :, :])
        out_dma(io["ssd_s"], H0[:])
        norm_squares_act(1)
        gate(21)
        norm_roots_act(1)
        outs_landed()

        act.wait_ge(yn_ok, 4)
        def load_bias(half):
            for s in range(SUB):
                act.dma_start(BIAS[s * CB:(s + 1) * CB, :, half * P:half * P + P],
                              bass.AP(tensor=bscr.tensor, offset=(SUB - 1 - s + half * (2 * SUB - 1)) * CB,
                                      ap=[[(2 * SUB - 1) * 2 * CB, CB], [BW, 8], [1, P]])).then_inc(s_bias[half], 16)

        load_bias(1)
        gate(22)
        load_bias(0)
        def exps(p):
            act.wait_ge(sm_ok, p + 1)
            w = P + DSEQ if ATTN_STEPS[p] is None else 2 * P
            for i in range(4):
                v = SB[:, p % 2, i, 0:w]
                nc.scalar.activation(v, v, ACT.Exp, bias=SM[:, p % 2, 1, i:i + 1], accum_out=SM[:, p % 2, 3, i:i + 1])
            nc.scalar.activation(SM[:, p % 2, 4, :], SM[:, p % 2, 2, :], ACT.Exp).then_inc(ex_ok, 1)

        exps(0)
        gate(23)
        for r in range(0, P, 16):
            act.dma_start(BIASS[r:r + 16, :, :],
                          bass.AP(tensor=bsscr.tensor, offset=0,
                                  ap=[[P + DSEQ, 16], [4 * BW_S, 2], [1, P + DSEQ]])).then_inc(s_biass, 16)
        act.wait_ge(vt_mm, 1)
        for i in range(2):
            nc.scalar.copy(PX[:, 7, 512 * i:512 * i + 512], bank[6 + i][:]).then_inc(vt_ok, 1)

        def y_high(q):
            for j in range(4):
                src = [PU[:, j, :], PX[:, j, :], PU[:, 4 + j, :]][q]
                nc.scalar.copy(HH[:, (4, 0, 4)[q] + j, :], src).then_inc(yh_hi, 1)

        def load_gate(t):
            q, j = divmod(t, 8)
            if t >= 2:
                act.wait_ge(acc_free[2], TILE0["branch"] + t - 1)
            act.dma_start(GTB[:, t % 2, :], tscr[(8, 0, 16)[q] + j]).then_inc(s_gt[t % 2], 16)

        def pt_rows(p):
            a = ATTN_STEPS[p]
            act.wait_ge(tp_mm, p + 1)
            if p >= 1:
                act.wait_ge(pv_mm, p)
            k = DSEQ if a is None else P
            if a is None or a >= 2:
                nc.scalar.copy(PT[:, 0, :], bank[5][:])
            nc.scalar.copy(PT[0:k, 1, :], bank[6][0:k, :]).then_inc(pt_ok, 1)

        def yc_rows(p):
            a = ATTN_STEPS[p]
            act.wait_ge(pv_mm, p + 1)
            if a is None:
                for i in range(4):
                    last = nc.scalar.copy(PU[:, 4 + i, SEQ:T].rearrange("p (t b) -> p t b", b=NSEQ),
                                          bank[7][:, 0:P].rearrange("p (b i t) -> p i t b", i=4, t=DSEQ)[:, i])
            else:
                n, kv = divmod(a, 2)
                for i in range(4):
                    last = nc.scalar.copy(blk(PU[64 * kv:64 * kv + 64, 4 + i, :], n),
                                          bank[7][64 * kv:64 * kv + 64, i * P:(i + 1) * P])
            last.then_inc(yc_ok, 1)

        act.wait_ge(acc_done[2], TILE_END[UNIT0["branch"] - 1])
        pt_rows(0)
        y_high(0)
        yc_rows(0)
        act.wait_ge(s_gst, 24 * 16)
        for i in range(2):
            nc.scalar.copy(VN[:, 512 * i:512 * i + 512], bank[5][32 * i:32 * i + DSEQ, :]).then_inc(vn_half, 1)
        act.wait_ge(vn_half, 2)
        act.sem_inc(vn_ok, 1)
        load_gate(0)
        load_gate(1)
        exps(1)
        y_high(1)
        act.dma_start(KS[:, :, 0:P], io["ks"]).then_inc(s_ks, 16)
        act.dma_start(VC[:], io["vc"]).then_inc(s_vc, 16)
        for p in range(NSTEP):
            if 1 <= p < NSTEP - 1:
                exps(p + 1)
            t = branch_at(p)
            if t is not None and 1 <= t < 15:
                load_gate(t + 1)
            if p >= 1:
                pt_rows(p)
                yc_rows(p)
            if ATTN_STEPS[p] is None:
                out_dma(io["kns"], KS[:, :, DSEQ:P + DSEQ])
                out_dma(io["vns"][P - DSEQ:P], VN.rearrange("p (s d) -> p s d", s=NSEQ))
                out_dma(io["vns"][0:P - DSEQ], VC[DSEQ:P, :, :])
        act.wait_ge(yc_ok, NSTEP)
        y_high(2)
        load_gate(16)
        outs_landed()
        def x_again(k):
            act.dma_start(X1[:, k, :], io["x"][k]).then_inc(s_x[k], 16)

        for t in range(17, 24):
            load_gate(t)
            if t in (17, 19, 21):
                x_again((t - 17) // 2)
        act.wait_ge(acc_done[2], TILE0["out"])
        act.wait_ge(mix_ok, 72)
        for n, (c0, w) in enumerate(CHUNKS):
            for k in range(KD):
                nc.scalar.copy(HH[:, k, c0:c0 + w], y_dst(k)[:, c0:c0 + w]).then_inc(mx_hi, 1)
            x_again(3 + n)
        norm_squares_act(2, beside=lambda k: x_again(6 + k) if k < 2 else None)
        norm_roots_act(2)
        norm_split_act(2)

        low_wait(act, 2, 3 * KD - 1)
        ff = 0
        for p, nf in enumerate(FFN_PASSES):
            t0 = TILE0[f"up{p}"]
            for f in range(nf):
                no = t0 + 2 * f
                for n, (c0, w) in enumerate(CHUNKS):
                    act.wait_ge(acc_done[n], no + 1)
                    nc.scalar.activation(FS[:, n, 0:w], acc[n][:, 0:w], ACT.Silu).then_inc(acc_free[n], 1)
                if f == 0 and p > 0:
                    act.wait_ge(acc_done[2], t0)
                for n, (c0, w) in enumerate(CHUNKS):
                    act.wait_ge(acc_free[n], no + 2)
                    nc.scalar.copy(FH[:, f, c0:c0 + w], FM[:, n, 0:w]).then_inc(f_hi, 1)
            ff += nf
        norm_squares_act(3)
        norm_roots_act(3)
        for i, k in enumerate([0, 1, KD - 2, 2, 3, KD - 1, 4, 5]):
            if k < KD - 2:
                act.wait_ge(y_ok, k + 1)
            else:
                act.wait_ge(y_pool, k - KD + 3)
                nc.scalar.activation(X1[:, k, :], X1[:, k, :], ACT.Copy, scale=prm("normf", k, 1)).then_inc(y_act, 1)
                act.wait_ge(y_act, k - KD + 3)
            out_dma(io["y"][k], X1[:, k, :])
        assert outs[0] == N_OUT_TOTAL

    @block.vector
    def _(dve):
        count = [0]

        def do(ins):
            ins.then_inc(chain, 1)
            count[0] += 1

        def sync():
            dve.wait_ge(chain, count[0])

        def tt(out, a, b, op=ALU.mult):
            return nc.vector.tensor_tensor(out, a, b, op)

        def ts(out, a, s1, op0, s2=None, op1=None):
            if op1 is None:
                return nc.vector.tensor_scalar(out, a, s1, None, op0)
            return nc.vector.tensor_scalar(out, a, s1, s2, op0, op1)

        def stt(out, a, s, b, op0=ALU.mult, op1=ALU.mult):
            return nc.vector.scalar_tensor_tensor(out=out, in0=a, scalar=s, in1=b, op0=op0, op1=op1)

        def cmul(o_re, o_im, a_re, a_im, b_re, b_im, t):
            do(tt(t[0], a_re, b_re))
            do(tt(t[1], a_im, b_im))
            do(tt(t[2], a_re, b_im))
            do(tt(t[3], a_im, b_re))
            sync()
            do(tt(o_re, t[0], t[1], ALU.subtract))
            do(tt(o_im, t[2], t[3], ALU.add))
            sync()

        lre, lim = prm("lam_re"), prm("lam_im")
        dve.wait_ge(step_ok, 1)
        tt(SF("ar"), lre, SF("step")).then_inc(ar_ok, 1)
        do(tt(SF("th"), lim, SF("step")))
        sync()
        MAGIC, C1 = 12582912.0, 6.28125
        C2, PI = 2 * math.pi - C1, 3.1415925
        do(ts(SF("n"), SF("th"), 1 / (2 * math.pi), ALU.mult, MAGIC, ALU.add))
        sync()
        do(ts(SF("n"), SF("n"), MAGIC, ALU.subtract))
        sync()
        do(stt(SF("r"), SF("n"), -C1, SF("th"), ALU.mult, ALU.add))
        sync()
        do(stt(SF("r"), SF("n"), -C2, SF("r"), ALU.mult, ALU.add))
        sync()
        do(ts(SF("r2"), SF("r"), math.pi / 2, ALU.add))
        sync()
        do(ts(SF("n"), SF("r2"), math.pi, ALU.is_gt, -2 * math.pi, ALU.mult))
        sync()
        do(tt(SF("r2"), SF("r2"), SF("n"), ALU.add))
        sync()
        do(ts(SF("r2"), SF("r2"), PI, ALU.min, -PI, ALU.max))
        ts(SF("r"), SF("r"), PI, ALU.min, -PI, ALU.max).then_inc(red_pre, 1)
        dve.wait_ge(red_pre, 1)
        sync()
        dve.sem_inc(red_ok, 1)
        norm_sum_dve(0)
        norm_split_dve(0)

        dve.wait_ge(mag_ok, 1)
        dve.wait_ge(sin_ok, 1)
        t4 = [TS4[:, i, :, 0] for i in range(4)]
        do(nc.vector.memset(PWA[:, 0, :, 0], 1.0))

        def unit(re, im):
            do(tt(t4[0], re, re))
            do(tt(t4[1], im, im))
            sync()
            do(tt(t4[0], t4[0], t4[1], ALU.add))
            sync()
            do(ts(t4[0], t4[0], -0.5, ALU.mult, 1.5, ALU.add))
            sync()
            do(tt(re, re, t4[0]))
            do(tt(im, im, t4[0]))
            sync()

        unit(SF("cos"), SF("sin"))
        do(nc.vector.memset(PWA[:, 1, :, 0], 0.0))
        do(tt(PWA[:, 0, :, 1], SF("mag"), SF("cos")))
        do(tt(PWA[:, 1, :, 1], SF("mag"), SF("sin")))
        sync()
        cmul(PWA[:, 0, :, 2], PWA[:, 1, :, 2], PWA[:, 0, :, 1], PWA[:, 1, :, 1], PWA[:, 0, :, 1], PWA[:, 1, :, 1], t4)
        for k in (2, 4):
            cmul(PWA[:, 0, :, k + 1:2 * k + 1], PWA[:, 1, :, k + 1:2 * k + 1],
                 PWA[:, 0, :, 1:k + 1], PWA[:, 1, :, 1:k + 1],
                 bc(PWA[:, 0, :, k:k + 1], [P, NP, k]), bc(PWA[:, 1, :, k:k + 1], [P, NP, k]),
                 [TS4[:, i, :, 0:k] for i in range(4)])
        for i in range(SUB):
            do(nc.vector.tensor_copy(PWD[:, :, :, i], PWA[:, :, :, SUB - 1 - i]))
        do(ts(SF("am"), PWA[:, 0, :, 1], 1.0, ALU.subtract))
        do(tt(SF("den"), lre, lre))
        do(tt(SF("n"), lim, lim))
        sync()
        do(tt(SF("den"), SF("den"), SF("n"), ALU.add))
        sync()
        do(nc.vector.reciprocal(SF("den"), SF("den")))
        do(tt(t4[0], SF("am"), lre))
        do(tt(t4[1], PWA[:, 1, :, 1], lim))
        do(tt(t4[2], PWA[:, 1, :, 1], lre))
        do(tt(t4[3], SF("am"), lim))
        sync()
        do(tt(t4[0], t4[0], t4[1], ALU.add))
        do(tt(t4[2], t4[2], t4[3], ALU.subtract))
        sync()
        do(tt(SF("f_re"), t4[0], SF("den")))
        do(tt(SF("f_im"), t4[2], SF("den")))
        sync()
        dve.wait_ge(s_bc, 32)
        dve.wait_ge(bias_mm, 18)
        rt = [OFF_re[:, 2 * i:2 * i + 2, :].rearrange("p a b -> p (a b)").rearrange("p (a h) -> p a h", h=16) for i in range(4)]
        cmul(BC[:, 0, :, :], BC[:, 1, :, :], BC[:, 0, :, :], BC[:, 1, :, :],
             bc(SF("f_re").unsqueeze(2), [P, NP, 16]), bc(SF("f_im").unsqueeze(2), [P, NP, 16]), rt)
        do(ts(BC[:, 3, :, :], BC[:, 3, :, :], -1.0, ALU.mult))
        do(nc.vector.memset(CDG[:], 0.0))
        sync()
        for e in range(2):
            do(nc.vector.tensor_copy(CDG[64 * e:64 * e + 64, :, :, e, :], BC[64 * e:64 * e + 64, 2:4, :, :]))
        sync()
        s4 = [P, NP, SUB, 16]
        tmp = KT[:, NP:NG, :, :].rearrange("p a b c -> p (a b c)").rearrange("p (a b c) -> p a b c", a=NP, b=SUB)
        v4 = lambda a: a.rearrange("p a (b c) -> p a b c", b=SUB)
        pw = lambda a: bc(a.unsqueeze(3), s4)
        xw = lambda a: bc(a.unsqueeze(2), s4)
        pdr, pdi = pw(PWD[:, 0, :, :]), pw(PWD[:, 1, :, :])
        par, pai = pw(PWA[:, 0, :, 1:9]), pw(PWA[:, 1, :, 1:9])
        b_re, b_im, c_re, nc_im = (xw(BC[:, i, :, :]) for i in range(4))

        def combine(dst, a, x, b, y, op):
            do(tt(v4(dst[:]), a, x))
            do(tt(tmp, b, y))
            sync()
            do(tt(v4(dst[:]), v4(dst[:]), tmp, op))
            sync()

        combine(W_re, pdr, b_re, pdi, b_im, ALU.subtract)
        combine(W_im, pdr, b_im, pdi, b_re, ALU.add)
        dve.sem_inc(w_ok, 1)

        dve.wait_ge(s_bst, 48)
        do(nc.vector.memset(HST[:], 0.0))
        nc.vector.memset(U[:, :, CH:UC], 0.0).then_inc(u_zero, 1)
        def sq(o_re, o_im, re, im):
            cmul(o_re, o_im, re, im, re, im, t4)
            unit(o_re, o_im)

        sq(SF("q_re"), SF("q_im"), SF("cos"), SF("sin"))
        sq(SF("q2_re"), SF("q2_im"), SF("q_re"), SF("q_im"))
        sq(SF("up_re0"), SF("up_im0"), SF("q2_re"), SF("q2_im"))
        for lv in range(6):
            sq(SF(f"up_re{lv + 1}"), SF(f"up_im{lv + 1}"), SF(f"up_re{lv}"), SF(f"up_im{lv}"))
        for a, b in (("mag2", "mag"), ("mag4", "mag2"), ("mag8", "mag4")):
            do(tt(SF(a), SF(b), SF(b)))
            sync()

        combine(OFF_re, c_re, par, nc_im, pai, ALU.add)
        combine(OFF_im, nc_im, par, c_re, pai, ALU.subtract)
        dve.sem_inc(off_ok, 1)

        s3 = [P, NP, NSEQ]
        t3 = [TS4[:, i, :, :] for i in range(4)]
        a4 = [bc(PWA[:, i, :, 4:5], s3) for i in range(2)]
        cmul(FINS[:, 0, :, :], FINS[:, 1, :, :], S0[:, 0, :, :], S0[:, 1, :, :], a4[0], a4[1], t3)
        dve.wait_ge(tap_mm, 1)
        dve.wait_ge(stt_mm, 8)
        nc.vector.memset(KTS[:], 0.0).then_inc(kt_zero, 1)
        dve.wait_ge(s_kt, 7 * 16)
        nc.vector.tensor_copy(KT[:].rearrange("p g t h -> p t g h"), KTS[:]).then_inc(kt_ok, 1)
        dve.wait_ge(kt_ok, 1)
        fins_done = [False]
        rot = [ROT[:, i, :, :] for i in range(2)]

        def rotations(b):
            pr0, k = 4 * b, 1
            for lv in range(7):
                cmul(rot[0][:, :, k:2 * k], rot[1][:, :, k:2 * k], rot[0][:, :, 0:k], rot[1][:, :, 0:k],
                     bc(SF(f"up_re{lv}")[:, pr0:pr0 + 4].unsqueeze(2), [P, 4, k]),
                     bc(SF(f"up_im{lv}")[:, pr0:pr0 + 4].unsqueeze(2), [P, 4, k]),
                     [RT[:, i, :, 0:k] for i in range(4)])
                k *= 2

        do(nc.vector.memset(ROT[:, 0, :, 0:1], 1.0))
        do(nc.vector.memset(ROT[:, 1, :, 0:1], 0.0))
        sync()
        rotations(0)
        for b in range(4):
            pr0 = 4 * b
            if not fins_done[0]:
                dve.wait_ge(sb_mm, 1)
                sums = bank[7].rearrange("p (a e b) -> p a e b", e=2, b=NSEQ)
                fins = FINS[:].rearrange("p i a b -> p (i a) b")
                do(tt(fins[0:64], fins[0:64], sums[0:64, :, 0, :], ALU.add))
                tt(fins[64:P], fins[64:P], sums[64:P, :, 1, :], ALU.add).then_inc(fin_ok, 1)
                sync()
                fins_done[0] = True
            dve.wait_ge(st_mm, b + 1)
            s_re = bank[3].rearrange("p (a c) -> p a c", a=4)
            s_im = bank[4].rearrange("p (a c) -> p a c", a=4)
            do(tt(RT[:, 0], s_re, rot[0]))
            do(tt(RT[:, 1], s_im, rot[1]))
            do(tt(RT[:, 2], s_im, rot[0]))
            do(tt(RT[:, 3], s_re, rot[1]))
            sync()
            do(tt(KI[:, 0], RT[:, 0], RT[:, 1], ALU.add))
            tt(KI[:, 1], RT[:, 2], RT[:, 3], ALU.subtract).then_inc(ki_ok, 1)
            dve.wait_ge(ki_ok, b + 1)
            sync()
            for j in range(4):
                for i in range(2):
                    do(nc.vector.tensor_tensor_scan(KSC[:, i, j, :], bc(SF("mag8")[:, pr0 + j:pr0 + j + 1], [P, CH]),
                                                    KI[:, i, j, :], 0.0, ALU.mult, ALU.add))
            sync()
            do(tt(RT[:, 0], KSC[:, 0], rot[0]))
            do(tt(RT[:, 1], KSC[:, 1], rot[1]))
            do(tt(RT[:, 2], KSC[:, 0], rot[1]))
            do(tt(RT[:, 3], KSC[:, 1], rot[0]))
            if b >= 1:
                dve.wait_ge(y_mm, 4 * b)
            sync()
            do(tt(HST[:, 0, :, 1:CH], RT[:, 0, :, 0:CH - 1], RT[:, 1, :, 0:CH - 1], ALU.subtract))
            do(tt(HST[:, 1, :, 1:CH], RT[:, 2, :, 0:CH - 1], RT[:, 3, :, 0:CH - 1], ALU.add))
            do(nc.vector.tensor_copy(HST[:, :, :, CH + 1:YC], S0[:, :, pr0:pr0 + 4, :]))
            do(tt(FIN[:, 0, pr0:pr0 + 4], RT[:, 0, :, CH - 1], RT[:, 1, :, CH - 1], ALU.subtract))
            tt(FIN[:, 1, pr0:pr0 + 4], RT[:, 2, :, CH - 1], RT[:, 3, :, CH - 1], ALU.add).then_inc(fin_ok, 1)
            dve.wait_ge(fin_ok, b + 2)
            sync()
            dve.sem_inc(hst_ok, 1)
            if b < 3:
                rotations(b + 1)
            for j in range(4):
                pr = pr0 + j
                dve.wait_ge(y_mm, pr + 1)
                for e in range(2):
                    g = 2 * pr + e
                    last = stt(U[:, g, 0:YC], U[:, g, 0:YC], prm("s5_d", g, 1), bank[5 + pr % 2][:, 256 * e:256 * e + YC],
                               ALU.mult, ALU.add)
                last.then_inc(y_ev, 1)

        for j in range(4):
            dve.wait_ge(gg_hi, j + 1)
            tt(as_blocks(GGL[:, j, :], NBLK), as_steps(GF[:, j, :], 0, NBLK),
               as_blocks(GGH[:, j, :].bitcast(F32), NBLK), ALU.subtract)
            tt(GGL[:, j, SEQ:T], GF[:, j, SEQ:T], GGH[:, j, SEQ:T].bitcast(F32), ALU.subtract).then_inc(gg_lo, 1)
        for i in range(4):
            no = TILE0["glu"] + 2 * i
            for n, (c0, w) in enumerate(CHUNKS):
                dve.wait_ge(acc_done[n], no + 2)
                dve.wait_ge(acc_free[n], no + 1)
                tt(PU[:, i, c0:c0 + w], GLT[:, n, 0:w], acc[n][:, 0:w]).then_inc(acc_free[n], 1)

        do(ts(CW[:], PRM[:, PCOL["conv_w"][0]:PCOL["conv_w"][0] + 30], 0.5, ALU.mult))
        sync()
        dve.wait_ge(s_scv, 16)
        for i in range(6):
            for n in range(3):
                dve.wait_ge(acc_free[n], TILE0["proj"] + i + 1)
            if i >= 2:
                dve.wait_ge(xbc_ok, i - 1)
            cv = CV[:, i % 2, :]
            x = PX[:, i, :]
            do(nc.vector.tensor_copy(CST[:, i, :], blk(x, NBLK - 1).rearrange("p (s c) -> p s c", s=SUB)[:, SUB - 3:SUB, CB - 1]))
            do(nc.vector.tensor_copy(CSS[:, i, :], x[:, SEQ + NSEQ:T]))
            do(ts(cv, x, CW[:, 4 * i + 3:4 * i + 4], ALU.mult, CW[:, 24 + i:25 + i], ALU.add))
            sync()
            cvp, xp = as_blocks(cv, NBLK), as_blocks(x, NBLK)
            scv = SCV[:, i, :, :].rearrange("p k b -> p (k b)")
            for d in range(1, 4):
                w = CW[:, 4 * i + 3 - d:4 * i + 4 - d]
                do(stt(cvp[:, :, d:, :], xp[:, :, 0:SUB - d, :], w, cvp[:, :, d:, :], ALU.mult, ALU.add))
                for s in range(d):
                    do(stt(cvp[:, :, s, 1:], xp[:, :, SUB - d + s, 0:CB - 1], w, cvp[:, :, s, 1:], ALU.mult, ALU.add))
                do(stt(cvp[:, 1:, 0:d, 0], xp[:, 0:NBLK - 1, SUB - d:, CB - 1], w, cvp[:, 1:, 0:d, 0], ALU.mult, ALU.add))
                o = SEQ + d * NSEQ
                do(stt(cv[:, o:T], x[:, SEQ:T - d * NSEQ], w, cv[:, o:T], ALU.mult, ALU.add))
                last = stt(cv[:, SEQ:o], scv[:, (3 - d) * NSEQ:3 * NSEQ], w, cv[:, SEQ:o], ALU.mult, ALU.add)
                if d < 3:
                    do(last)
                    sync()
                else:
                    last.then_inc(conv_last, 1)
            dve.wait_ge(conv_last, i + 1)
            sync()
            dve.sem_inc(conv_ok, 1)
            if i == 5:
                dve.sem_inc(cst_ok, 1)
            if i == 1:
                softplus_and_cumsum(dve, do, sync, tt, ts, stt)
            if i >= 1:
                conv_finish(dve, stt, i - 1)
        conv_finish(dve, stt, 5)
        dve.wait_ge(xbc_ok, 6)

        dve.wait_ge(nac_mm, 1)
        do(nc.vector.tensor_copy(DTT[:, 7, 0:8, :], bank[4][:, 0:64].rearrange("p (a b) -> p a b", b=8)))
        nc.vector.tensor_copy(DTT[0:SMP, 7, 8, :], bank[4][0:SMP, 64:72]).then_inc(nac_ok, 1)
        dve.wait_ge(s_out, 16 * 6)
        nc.vector.memset(HS[:, 0, :, :], 0.0).then_inc(h_ok, 1)
        dve.wait_ge(s_h0, 16)
        for n in range(NBLK + 1):
            smp = n == NBLK
            rows = SMP if smp else P
            if n >= 1:
                dve.wait_ge(yd_mm, n)
                if n >= 2:
                    dve.wait_ge(ss_mm, n - 1)
            dve.wait_ge(tr_mm, n + 1)
            tt(XS[0:rows].rearrange("p (h d) -> p h d", d=HD), bank[3][0:rows].rearrange("p (h d) -> p h d", d=HD),
               bc(DTT[0:rows, 5, n, :].unsqueeze(2), [rows, 8, HD])).then_inc(xs_ok, 1)
            dve.wait_ge(et_ok, n + 1)
            c = PX[:, 5, SEQ:T] if smp else blk(PX[:, 5, :], n)
            etf, cdf = ET[:].rearrange("p a b -> p (a b)"), CD[:].rearrange("p a b -> p (a b)")
            if smp:
                tt(cdf[:, 0:4 * SMP].rearrange("p (k q) -> p k q", k=4), etf[:, 0:4 * SMP].rearrange("p (k q) -> p k q", k=4),
                   bc(c.unsqueeze(1), [P, 4, SMP])).then_inc(cd_ok, 1)
            else:
                tt(CD[:], ET[:], bc(c.unsqueeze(1), [P, 4, P])).then_inc(cd_ok, 1)
            dve.wait_ge(l_ok, n + 1)
            if smp:
                do(nc.vector.tensor_reduce(DE[0:SMP, :], LS[:, 0, :, SMP - NSEQ:SMP], AX.X, ALU.add))
            else:
                do(nc.vector.tensor_copy(DE[:], L[:, :, P - 1]))
            sync()
            dve.wait_ge(xs_ok, n + 1)
            dve.wait_ge(cb_mm, n + 1)
            if n >= 1:
                dve.wait_ge(ss_mm, n)
            tt(XD[0:rows].rearrange("p (h d) -> p h d", d=HD), XS[0:rows].rearrange("p (h d) -> p h d", d=HD),
               bc(DE[0:rows, :].unsqueeze(2), [rows, 8, HD])).then_inc(xd_ok, 1)
            for g in range(2):
                cbt = bank[4][0:rows, P + 128 * g:P + 128 * g + rows]
                if smp:
                    last = tt(LS[:, 1, 4 * g:4 * g + 4, :], LS[:, 0, 4 * g:4 * g + 4, :],
                              bc(cbt.unsqueeze(1), [rows, 4, rows]))
                else:
                    last = tt(L[:, 4 * g:4 * g + 4, :], L[:, 4 * g:4 * g + 4, :], bc(cbt.unsqueeze(1), [P, 4, P]))
                do(last)
            sync()
            dve.sem_inc(mm_ok, 1)
            if not smp:
                hp, hn = HS[:, n % 2, :, :], HS[:, (n + 1) % 2, :, :]
                do(tt(hn, hp, bc(ET[:, :, P - 1:P], [P, 4, HD])))
                sync()
                dve.wait_ge(ss_mm, n + 1)
                tt(hn, hn, bank[3][:, 0:256].rearrange("p (k d) -> p k d", d=HD), ALU.add).then_inc(h_ok, 1)
            dve.wait_ge(yd_mm, n + 1)
            for i in range(4):
                xi = PX[:, i, SEQ:T] if smp else blk(PX[:, i, :], n)
                yi = bank[7][:, i * P:i * P + rows]
                last = stt(xi, xi, prm("ssd_d", i, 1), yi, ALU.mult, ALU.add)
            last.then_inc(ye_ok, 1)
            dve.wait_ge(zt_ok, n + 1)
            c0, c1 = (SEQ, T) if smp else (P * n, P * n + P)
            for half in range(2):
                zb = ZB[half][:, :, 0:rows]
                do(stt(zb, zb, 1.0, PX[:, 8 + 2 * half:10 + 2 * half, c0:c1], ALU.add, ALU.mult))
            sync()
            dve.wait_ge(ye_ok, n + 1)
            for half in range(2):
                y = PX[:, 2 * half:2 * half + 2, c0:c1]
                last = stt(y, y, 0.5, ZB[half][:, :, 0:rows], ALU.mult, ALU.mult)
            last.then_inc(ya_ok, 1)
        for half in range(2):
            if half == 1:
                dve.wait_ge(ss_mm, NBLK + 4)
            else:
                dve.wait_ge(bt_ok, NBLK + 1)
            tt(BTM, bc(BT[0:SMP, :].unsqueeze(1), [SMP, 4, P]),
               bc(prm("seqmask", 4 * half, 4)[0:SMP, :].unsqueeze(2), [SMP, 4, P])).then_inc(btm_ok, 1)
            for b in range(4 * half, 4 * half + 4):
                etf = ET[:].rearrange("p a b -> p (a b)")[:, 0:4 * SMP].rearrange("p (k q) -> p k q", k=4)
                do(tt(H0[:, b, :, :], H0[:, b, :, :], bc(etf[:, :, SMP - NSEQ + b:SMP - NSEQ + b + 1], [P, 4, HD])))
                sync()
                dve.wait_ge(ss_mm, NBLK + b + 1)
                tt(H0[:, b, :, :], H0[:, b, :, :], bank[(3, 4)[b % 2]][:, 0:256].rearrange("p (k d) -> p k d", d=HD),
                   ALU.add).then_inc(h_ok, 1)
        norm_sum_dve(1)
        dve.wait_ge(rs_ok, 6)
        for k in range(4):
            stt(PX[:, k, :], PX[:, k, :], prm("ssd_norm", k, 1), ZR[:], ALU.mult, ALU.mult).then_inc(yn_ok, 1)

        dve.wait_ge(s_bias[1], 8 * 16)

        def maxima(p):
            a = ATTN_STEPS[p]
            smp, first = a is None, a is not None and a < 2
            z = SB[:, p % 2, :, :]
            w = P + DSEQ if smp else 2 * P
            if p >= 2:
                dve.wait_ge(tp_mm, p - 1)
            if first:
                do(nc.vector.memset(z, NEG))
                sync()
            if p == 2:
                dve.wait_ge(s_bias[0], 8 * 16)
            dve.wait_ge(at_s, p + 1)
            kv = 0 if smp else a % 2
            for j in range(2):
                ps = bank[3 + j].rearrange("p (i w) -> p i w", i=2)
                if smp:
                    last = stt(z[:, 2 * j:2 * j + 2, 0:w], ps[:, :, 0:w], HD ** -0.5, BIASS[:], ALU.mult, ALU.add)
                elif first:
                    v = lambda x: x[:, :, P:]
                    last = stt(v(z[:, 2 * j:2 * j + 2, :]), v(ps), HD ** -0.5, v(BIAS[:, 4 * kv + 2 * j:4 * kv + 2 * j + 2, :]),
                               ALU.mult, ALU.add)
                else:
                    last = stt(z[:, 2 * j:2 * j + 2, :], ps, HD ** -0.5, BIAS[:, 4 * kv + 2 * j:4 * kv + 2 * j + 2, :],
                               ALU.mult, ALU.add)
                do(last)
            sync()
            dve.sem_inc(sb_rd, 1)
            sink = prm("sinks_s") if smp else prm("sinks", 4 * kv, 4)
            m = SM[:, p % 2, :, :]
            do(nc.vector.tensor_reduce(m[:, 0, :], z[:, :, 0:w], AX.X, ALU.max))
            sync()
            do(tt(m[:, 0, :], m[:, 0, :], sink, ALU.max))
            sync()
            do(ts(m[:, 1, :], m[:, 0, :], -1.0, ALU.mult))
            do(tt(m[:, 2, :], sink, m[:, 0, :], ALU.subtract))
            sync()
            dve.sem_inc(sm_ok, 1)

        def probs(p):
            m = SM[:, p % 2, :, :]
            w = P + DSEQ if ATTN_STEPS[p] is None else 2 * P
            dve.wait_ge(ex_ok, p + 1)
            do(tt(m[:, 5, :], m[:, 3, :], m[:, 4, :], ALU.add))
            sync()
            do(nc.vector.reciprocal(m[:, 5, :], m[:, 5, :]))
            sync()
            z = SB[:, p % 2, :, 0:w]
            tt(z, z, bc(m[:, 5, :].unsqueeze(2), [P, 4, w])).then_inc(p_ok, 1)

        def y_low(q):
            for j in range(4):
                src = [PU[:, j, :], PX[:, j, :], PU[:, 4 + j, :]][q]
                k = (4, 0, 4)[q] + j
                dve.wait_ge(yh_hi, 4 * q + j + 1)
                tt(HL[:, k, :], src, HH[:, k, :].bitcast(F32), ALU.subtract).then_inc(yh_lo, 1)

        mt = [0]

        def mix(t):
            q, j = divmod(t, 8)
            no = TILE0["branch"] + t
            dve.wait_ge(s_gt[t % 2], 16 * (t // 2 + 1))
            for n, (c0, w) in enumerate(CHUNKS):
                dve.wait_ge(acc_done[n], no + 1)
                if mt[0] >= 2:
                    dve.wait_ge(mix_ok, mt[0] - 1)
                half = MT[:, mt[0] % 2, 0:w]
                stt(half, GTB[:, t % 2, c0:c0 + w], 1.0, acc[n][:, 0:w], ALU.add, ALU.mult).then_inc(acc_free[n], 1)
                dve.wait_ge(acc_free[n], no + 1)
                dst = y_dst(j)[:, c0:c0 + w]
                if q == 0:
                    ts(dst, half, 0.5, ALU.mult).then_inc(mix_ok, 1)
                else:
                    dve.wait_ge(mix_ok, mt[0])
                    stt(dst, half, 0.5, dst, ALU.mult, ALU.add).then_inc(mix_ok, 1)
                mt[0] += 1

        def sample_keys():
            dve.wait_ge(s_biass, 8 * 16)
            dve.wait_ge(s_ks, 16)
            nc.vector.tensor_copy(KS[:, :, P:P + DSEQ],
                                  PX[:, 6, SEQ:T].rearrange("p (t b) -> p b t", b=NSEQ)).then_inc(ks_ok, 1)
            for d in range(2):
                for i in range(4):
                    last = nc.vector.tensor_copy(QS[:, :, 16 * d + 4 * i:16 * d + 4 * i + 4],
                                                 PU[:, 4 + i, SEQ:T].rearrange("p (t b) -> p b t", b=NSEQ))
            last.then_inc(ks_ok, 1)

        maxima(0)
        probs(0)
        maxima(1)
        y_low(0)
        for p in range(NSTEP):
            if p >= 1:
                probs(p)
            if p == 3:
                sample_keys()
            if 1 <= p < NSTEP - 1:
                maxima(p + 1)
            if p == 1:
                y_low(1)
                dve.wait_ge(yh_lo, 8)
            if branch_at(p) is not None and p < NSTEP - 1:
                mix(branch_at(p))
        y_low(2)
        mix(NSTEP - 2)
        for t in range(16, 24):
            mix(t)
        i = 0
        for n, (c0, w) in enumerate(CHUNKS):
            for k in range(KD):
                i += 1
                dve.wait_ge(mx_hi, i)
                tt(HL[:, k, c0:c0 + w], y_dst(k)[:, c0:c0 + w], HH[:, k, c0:c0 + w].bitcast(F32),
                   ALU.subtract).then_inc(mx_lo, 1)

        def add_to_x1(stage, norm=None):
            for k in range(KD):
                no = TILE0[stage] + k
                if stage == "out":
                    dve.wait_ge(s_x[k], 32)
                for n, (c0, w) in enumerate(CHUNKS):
                    dve.wait_ge(acc_done[n], no + 1)
                    tt(X1[:, k, c0:c0 + w], X1[:, k, c0:c0 + w], acc[n][:, 0:w], ALU.add).then_inc(acc_free[n], 1)
                if norm is not None and k >= 1:
                    norm_add_dve(norm, k - 1)

        add_to_x1("out", norm=2)
        norm_sum_dve(2, first=KD - 1)
        norm_split_dve(2)
        low_wait(dve, 2, 3 * KD - 1)

        ff = 0
        for p, nf in enumerate(FFN_PASSES):
            t0 = TILE0[f"up{p}"]
            for f in range(nf):
                no = t0 + 2 * f
                for n, (c0, w) in enumerate(CHUNKS):
                    dve.wait_ge(acc_done[n], no + 2)
                    dve.wait_ge(acc_free[n], no + 1)
                    if ff > 0:
                        dve.wait_ge(f_lo, 3 * ff - 2 + n)
                    tt(FM[:, n, 0:w], FS[:, n, 0:w], acc_of(no + 1, n)[:, 0:w]).then_inc(acc_free[n], 1)
                for n, (c0, w) in enumerate(CHUNKS):
                    dve.wait_ge(f_hi, 3 * ff + n + 1)
                    tt(FL[:, f, c0:c0 + w], FM[:, n, 0:w], FH[:, f, c0:c0 + w].bitcast(F32), ALU.subtract).then_inc(f_lo, 1)
                ff += 1
            add_to_x1(f"down{p}", norm=3 if p == len(FFN_PASSES) - 1 else None)
        norm_sum_dve(3, first=KD - 1)
        dve.wait_ge(rs_ok, 12)
        for k in range(KD - 2):
            stt(X1[:, k, :], X1[:, k, :], prm("normf", k, 1), RS5[:], ALU.mult, ALU.mult).then_inc(y_ok, 1)

    top.close()


def kernel(**inputs):
    import numpy as _np
    import concourse.bacc as _bacc
    from concourse.bass_utils import run_bass_kernel_spmd as _run

    a = {k: _np.asarray(v) for k, v in inputs.items()}
    f32 = _np.float32

    def cols(x):
        p = x["p"].reshape(NBLK, CB, SUB, -1).transpose(0, 2, 1, 3).reshape(SEQ, -1)
        s = x["s"].reshape(NSEQ, DSEQ, -1).transpose(1, 0, 2).reshape(SMP, -1)
        return _np.concatenate([p, s], 0).T

    x = cols({"p": a["x_prompt"][0], "s": a["x_sample"]}).reshape(KD, P, T)

    w_in = a["w_in"][0]
    z0, xbc0, dt0, u0, q0, k0, v0, g0 = 0, 512, 1280, 1288, 1800, 2312, 2440, 2568

    def tiles(w, c0, n):
        k = w.shape[0] // P
        return w[:, c0:c0 + n * P].reshape(k, P, n, P).transpose(2, 1, 0, 3)

    def flat(t):
        return t.reshape(t.shape[0], P, -1)

    wdt = _np.zeros((D, P), f32)
    wdt[:, 0:8] = w_in[:, dt0:dt0 + 8]
    wq = w_in[:, q0:q0 + 512].reshape(D, 2, 4, 64).transpose(0, 2, 1, 3).reshape(D, 512)
    gates = flat(tiles(w_in, g0, 24))
    glu = tiles(a["s5_w_glu"][0], 0, 8)
    glu = _np.stack([_np.concatenate([glu[j + 4], glu[j]], 1) for j in range(4)])
    wc = a["w_br_c"][0].reshape(2, 4, 64, D).transpose(1, 0, 2, 3).reshape(512, D)
    branch = []
    for w in (a["w_br_b"][0], a["w_br_a"][0], wc):
        t = tiles(w, 0, 8)
        branch += [_np.concatenate([t[2 * i], t[2 * i + 1]], 1) for i in range(4)]
    up = tiles(a["w_ffn_up"][0], 0, 2 * KF)
    down = tiles(a["w_ffn_down"][0], 0, KD)
    units = [flat(tiles(w_in, u0, 4)), gates[0:12], flat(glu),
             flat(tiles(w_in, xbc0, 6)), flat(tiles(wdt, 0, 1)), flat(tiles(w_in, k0, 1)), flat(tiles(w_in, v0, 1)),
             flat(tiles(w_in, z0, 4)), flat(tiles(wq, 0, 4)), gates[12:24], flat(_np.stack(branch)),
             flat(tiles(a["w_out"][0], 0, 8))]
    f = 0
    for n in FFN_PASSES:
        for j in range(f, f + n):
            units += [flat(up[j:j + 1]), flat(up[KF + j:KF + j + 1])]
        d = _np.zeros((KD, P, 1024), f32)
        d[:, :, 0:n * P] = flat(down[:, :, f:f + n])
        units.append(d)
        f += n
    w = _np.concatenate(units, 0)
    assert w.shape == (UNITS, P, 1024), w.shape

    consts, hot = shape_constants()
    par = _np.zeros((P, NPAR), f32)

    def put(name, v):
        at, n = PCOL[name]
        v = _np.asarray(v)
        par[0:v.shape[0], at:at + n] = v

    def rows(v):
        return _np.broadcast_to(v, (P, v.shape[-1]))

    for name, v in consts.items():
        put(name, v)
    for name, key in (("norm1", "norm1_w"), ("norm2", "norm2_w"), ("normf", "final_norm_w"), ("ssd_norm", "ssd_norm_w")):
        put(name, a[key].reshape(-1, P).T)
    put("conv_w", a["conv_w"][0].reshape(4, 6, P).transpose(2, 1, 0).reshape(P, 24))
    put("conv_b", a["conv_b"][0].reshape(6, P).T)
    put("ssd_d", _np.repeat(a["ssd_d"][0], HD).reshape(4, P).T)
    put("a_log", rows(a["ssd_a_log"][0]))
    put("dt_bias", rows(a["ssd_dt_bias"][0]))
    put("sinks", rows(a["attn_sinks"][0]))
    sk = a["attn_sinks"][0].reshape(2, 4)
    sk = _np.broadcast_to(sk.T[None, None, :, None, None, :], (4, 2, 4, DSEQ, 2, 2)).reshape(P, 4)
    put("sinks_s", sk)
    put("s5_d", _np.tile(a["s5_d"][0].T, (SUB, 1)))

    def pairs(v):
        return v.reshape(16, 2, 64, *v.shape[2:]).transpose(1, 2, 0, *range(3, v.ndim + 1)).reshape(P, 16, *v.shape[2:])

    put("lam_re", pairs(a["s5_lam_re"][0]))
    put("lam_im", pairs(a["s5_lam_im"][0]))
    put("log_dt", pairs(_np.broadcast_to(a["s5_log_dt"][0][:, None], (32, 64))))
    bcm = _np.stack([pairs(a["s5_b_re"][0]), pairs(a["s5_b_im"][0]),
                     pairs(a["s5_c_re"][0].transpose(0, 2, 1)), pairs(a["s5_c_im"][0].transpose(0, 2, 1))], 1)
    s0 = _np.stack([pairs(a[k][0].transpose(1, 2, 0)) for k in ("state_s5_re", "state_s5_im")], 1)
    hotp = _np.zeros((P, BHALF), f32)
    hotp[0:33] = hot[:, 0:BHALF]
    hotp[64:97] = hot[:, BHALF:]
    rtab = _np.zeros((P, 8), f32)
    for r in (0, 64):
        rtab[r:r + 32] = a["rel_bias"]
        rtab[r + 32] = 1.0
    h0 = a["state_ssd"][0].reshape(NSEQ, 2, 4, 64, 64).transpose(1, 4, 0, 2, 3).reshape(P, NSEQ, 4, 64)
    scv = a["state_conv"][0].reshape(NSEQ, 3, 6, P).transpose(3, 2, 1, 0)
    ks = a["cache_k"][0].reshape(NSEQ, P, P).transpose(2, 0, 1)
    vc = a["cache_v"][0].reshape(NSEQ, P, P).transpose(1, 0, 2)

    ins = {"params": par, "x": x, "w": w, "hot": hotp, "rtab": rtab, "bc": bcm, "s0": s0, "h0": h0, "scv": scv,
           "ks": ks, "vc": vc}
    outs = {"y": (KD, P, T), "ssd_p": (P, 4, HD), "conv_p": (P, 6, 3), "conv_s": (P, 6, 24), "s5p": (P, 2, 16),
            "s5s": (P, 2, 16, NSEQ), "kp": (P, P), "vp": (P, P), "ssd_s": (P, NSEQ, 4, HD),
            "kns": (P, NSEQ, P), "vns": (P, NSEQ, P)}
    nc = _bacc.Bacc("TRN2", target_bir_lowering=False, num_devices=1)
    io, arrays = {}, {}
    for name, v in ins.items():
        arrays["in_" + name] = _np.ascontiguousarray(v, dtype=f32)
        io[name] = nc.dram_tensor("in_" + name, v.shape, F32, kind="ExternalInput").ap()
    for name, shape in outs.items():
        io[name] = nc.dram_tensor("out_" + name, shape, F32, kind="ExternalOutput").ap()
    build(nc, io)
    res = _run(nc, [arrays], core_ids=[0]).results[0]
    o = {name: _np.asarray(res["out_" + name]) for name in outs}

    y = o["y"].reshape(D, T)
    y_p = y[:, 0:SEQ].reshape(D, NBLK, SUB, CB).transpose(1, 3, 2, 0).reshape(1, SEQ, D)
    y_s = y[:, SEQ:].reshape(D, DSEQ, NSEQ).transpose(2, 1, 0)
    ssd_p = o["ssd_p"].reshape(2, 64, 4, 64).transpose(0, 2, 3, 1).reshape(1, 1, 8, 64, 64)
    conv_p = o["conv_p"].transpose(2, 1, 0).reshape(1, 1, 3, 768)
    s5 = o["s5p"].reshape(2, 64, 2, 16).transpose(2, 3, 0, 1).reshape(2, 1, 1, 32, 64)

    def last_block(t):
        return t.reshape(2, 64, SUB, CB).transpose(3, 2, 0, 1).reshape(1, 1, P, 2, 64)

    ssd_s = o["ssd_s"].reshape(2, 64, NSEQ, 4, 64).transpose(2, 0, 3, 4, 1).reshape(1, NSEQ, 8, 64, 64)
    conv_s = o["conv_s"].reshape(P, 6, 3, NSEQ).transpose(3, 2, 1, 0).reshape(1, NSEQ, 3, 768)
    s5s = o["s5s"].reshape(2, 64, 2, 16, NSEQ).transpose(2, 4, 3, 0, 1).reshape(2, 1, NSEQ, 32, 64)
    k_s = o["kns"].reshape(2, 64, NSEQ, P).transpose(2, 3, 0, 1).reshape(1, NSEQ, P, 2, 64)
    v_s = o["vns"].reshape(P, NSEQ, 2, 64).transpose(1, 0, 2, 3).reshape(1, NSEQ, P, 2, 64)
    c = _np.ascontiguousarray
    return tuple(c(t) for t in (y_p, y_s, ssd_p, conv_p, s5[0], s5[1], last_block(o["kp"]), last_block(o["vp"]),
                                ssd_s, conv_s, s5s[0], s5s[1], k_s, v_s))
```
